# Optimizing a Trainium2 kernel written in Bass

```python
import math
import jax
import jax.numpy as jnp
from jax import lax
import numpy as np

D_MODEL = 1024
BATCH = 1
SEQ = 256
DEPTH = 2

GRID_W = 64
CTX_LEN = 256
RMS_EPS = 1e-6
N_MOD = 9
FFN_HIDDEN = 2816

GM_GROUPS = 4
GM_WIDTH = 512
GM_CHUNK = 128

DN_HEADS = 4
DN_HEAD_DIM = 128
DN_WIDTH = DN_HEADS * DN_HEAD_DIM
DN_CONV = 5
DN_CHUNK = 64

MLA_HEADS = 8
MLA_NOPE = 64
MLA_ROPE = 32
MLA_QK = MLA_NOPE + MLA_ROPE
MLA_V = 64
MLA_WIDTH = MLA_HEADS * MLA_V
MLA_Q_LORA = 384
MLA_KV_LORA = 256
Q_BLOCK = 128
ROPE_BASE = 10000.0

N_BRANCH = 3
IN_SPLITS = (2 * GM_WIDTH, 3 * DN_WIDTH, DN_WIDTH, 4 * DN_HEADS, MLA_Q_LORA, MLA_KV_LORA + MLA_ROPE, N_BRANCH * D_MODEL)
IN_WIDTH = sum(IN_SPLITS)

kernel_name = 'hybrid_gmlp_deltanet_mla_prefix_dit'

def rms_norm(x, w):
    x32 = x.astype(jnp.float32)
    y = x32 * lax.rsqrt(jnp.mean(x32 * x32, axis=-1, keepdims=True) + RMS_EPS)
    return y.astype(x.dtype) * w

def layer_norm(x, w):
    x32 = x.astype(jnp.float32)
    mu = jnp.mean(x32, axis=-1, keepdims=True)
    xc = x32 - mu
    y = xc * lax.rsqrt(jnp.mean(xc * xc, axis=-1, keepdims=True) + RMS_EPS)
    return y.astype(x.dtype) * w

def l2_normalize(x):
    return x * lax.rsqrt(jnp.sum(x * x, axis=-1, keepdims=True) + RMS_EPS)

def modulate(x, shift, scale):
    return x * (1.0 + scale) + shift

def swiglu(h, w_gu, w_down):
    g, u = jnp.split(h @ w_gu, 2, axis=-1)
    return (jax.nn.silu(g) * u) @ w_down

def ada_ffn_half(h, shift, scale, gate, norm_w, w_gu, w_down):
    return h + 0.5 * gate * swiglu(modulate(rms_norm(h, norm_w), shift, scale), w_gu, w_down)

def split_in(p):
    offsets = np.cumsum(IN_SPLITS)[:-1].tolist()
    return jnp.split(p, offsets, axis=-1)

def axial_rope_tables(n_tokens, dtype):
    rows = n_tokens // GRID_W
    row = jnp.repeat(jnp.arange(rows), GRID_W).astype(jnp.float32)
    col = jnp.tile(jnp.arange(GRID_W), rows).astype(jnp.float32)
    half = MLA_ROPE // 2
    inv_freq = 1.0 / (ROPE_BASE ** (jnp.arange(0, half, 2, dtype=jnp.float32) / half))
    ang_r = row[:, None] * inv_freq
    ang_c = col[:, None] * inv_freq
    ang = jnp.concatenate([ang_r, ang_r, ang_c, ang_c], axis=-1)
    return jnp.cos(ang).astype(dtype), jnp.sin(ang).astype(dtype)

def rotate_half(y):
    y1, y2 = jnp.split(y, 2, axis=-1)
    return jnp.concatenate([-y2, y1], axis=-1)

def apply_axial_rope(t, cos, sin):
    tr, tc = jnp.split(t, 2, axis=-1)
    rot = jnp.concatenate([rotate_half(tr), rotate_half(tc)], axis=-1)
    return t * cos[None, :, None, :] + rot * sin[None, :, None, :]

def rope_tail(t, rope):
    if rope is None:
        return t
    cos, sin = rope
    return jnp.concatenate([t[..., :MLA_NOPE], apply_axial_rope(t[..., MLA_NOPE:], cos, sin)], axis=-1)

def chunk_gmlp_branch(z, ln_w, w_s, b_s):
    z = jax.nn.gelu(z)
    u, v = jnp.split(z, 2, axis=-1)
    v = layer_norm(v, ln_w)
    b, n, _ = v.shape
    v = v.reshape(b, n // GM_CHUNK, GM_CHUNK, GM_GROUPS, GM_WIDTH // GM_GROUPS)
    s = jnp.einsum('gpq,bnqgc->bnpgc', w_s, v) + b_s.T[None, None, :, :, None]
    return u * s.reshape(b, n, GM_WIDTH)

def centred_depthwise_conv(x, w):
    ch = x.shape[-1]
    return lax.conv_general_dilated(
        x, w[:, None, :].astype(x.dtype), window_strides=(1,),
        padding=[(DN_CONV // 2, DN_CONV // 2)],
        dimension_numbers=('NWC', 'WIO', 'NWC'), feature_group_count=ch)

def delta_prepare(qkv, ab, conv_w, a_log, dt_bias):
    b, n, _ = qkv.shape
    qkv = jax.nn.silu(centred_depthwise_conv(qkv, conv_w)).astype(jnp.float32)
    q, k, v = jnp.split(qkv, 3, axis=-1)

    def heads(y):
        return y.reshape(b, n, DN_HEADS, DN_HEAD_DIM).transpose(0, 2, 1, 3)

    q = l2_normalize(heads(q))
    k = l2_normalize(heads(k))
    v = heads(v)
    ab = ab.astype(jnp.float32).reshape(b, n, 2, 2, DN_HEADS)
    a, bpre = ab[:, :, 0], ab[:, :, 1]
    g = -jnp.exp(a_log.astype(jnp.float32)) * jax.nn.softplus(a + dt_bias.astype(jnp.float32))
    beta = jax.nn.sigmoid(bpre)
    return q, k, v, g.transpose(2, 0, 3, 1), beta.transpose(2, 0, 3, 1)

def gated_delta_chunked(q, k, v, g, beta, s0):
    b, h, n, dk = q.shape
    dv = v.shape[-1]
    nc = n // DN_CHUNK
    q = (q * dk ** -0.5).reshape(b, h, nc, DN_CHUNK, dk)
    k = k.reshape(b, h, nc, DN_CHUNK, dk)
    v = v.reshape(b, h, nc, DN_CHUNK, dv)
    beta = beta.reshape(b, h, nc, DN_CHUNK)
    gam = jnp.cumsum(g.reshape(b, h, nc, DN_CHUNK), axis=-1)
    incl = jnp.tril(jnp.ones((DN_CHUNK, DN_CHUNK), dtype=bool))
    strict = jnp.tril(jnp.ones((DN_CHUNK, DN_CHUNK), dtype=bool), k=-1)
    diff = gam[..., :, None] - gam[..., None, :]
    decay = jnp.where(incl, jnp.exp(jnp.where(incl, diff, 0.0)), 0.0)
    kb = k * beta[..., None]
    m = jnp.where(strict, jnp.einsum('bhncd,bhnsd->bhncs', kb, k) * decay, 0.0)
    eye = jnp.eye(DN_CHUNK, dtype=jnp.float32)
    t_inv = lax.linalg.triangular_solve(eye + m, jnp.broadcast_to(eye, m.shape), left_side=True, lower=True)
    u = jnp.einsum('bhncs,bhnse->bhnce', t_inv, v * beta[..., None])
    w = jnp.einsum('bhncs,bhnsd->bhncd', t_inv, kb * jnp.exp(gam)[..., None])
    qk = jnp.einsum('bhncd,bhnsd->bhncs', q, k) * decay

    def step(s, xs):
        q_c, k_c, u_c, w_c, qk_c, gam_c = xs
        v_new = u_c - jnp.einsum('bhcd,bhde->bhce', w_c, s)
        o = (jnp.einsum('bhcd,bhde->bhce', q_c * jnp.exp(gam_c)[..., None], s)
             + jnp.einsum('bhcs,bhse->bhce', qk_c, v_new))
        g_last = gam_c[..., -1]
        s = (s * jnp.exp(g_last)[..., None, None]
             + jnp.einsum('bhcd,bhce->bhde', k_c * jnp.exp(g_last[..., None] - gam_c)[..., None], v_new))
        return s, o

    xs = tuple(jnp.moveaxis(a, 2, 0) for a in (q, k, u, w, qk, gam))
    s_final, o = lax.scan(step, s0, xs)
    o = jnp.moveaxis(o, 0, 2).reshape(b, h, n, dv)
    return o, s_final

def _orient(t, reverse):
    return jnp.flip(t, axis=2) if reverse else t

def bidirectional_delta(qkv_c, ab_c, qkv_x, ab_x, conv_w, a_log, dt_bias):
    qc, kc, vc, gc, bc = delta_prepare(qkv_c, ab_c, conv_w, a_log, dt_bias)
    qx, kx, vx, gx, bx = delta_prepare(qkv_x, ab_x, conv_w, a_log, dt_bias)
    s_zero = jnp.zeros((qx.shape[0], DN_HEADS, DN_HEAD_DIM, DN_HEAD_DIM), jnp.float32)
    outs_c, outs_x = [], []
    for d in range(2):
        rev = d == 1
        oc, s_ctx = gated_delta_chunked(_orient(qc, rev), _orient(kc, rev), _orient(vc, rev),
                                        _orient(gc[d], rev), _orient(bc[d], rev), s_zero)
        ox, _ = gated_delta_chunked(_orient(qx, rev), _orient(kx, rev), _orient(vx, rev),
                                    _orient(gx[d], rev), _orient(bx[d], rev), s_ctx)
        outs_c.append(_orient(oc, rev))
        outs_x.append(_orient(ox, rev))
    return outs_c[0] + outs_c[1], outs_x[0] + outs_x[1]

def delta_output(o, z, norm_w):
    b, _, n, _ = o.shape
    o = rms_norm(o.transpose(0, 2, 1, 3), norm_w).astype(z.dtype)
    return (o * jax.nn.silu(z.reshape(b, n, DN_HEADS, DN_HEAD_DIM))).reshape(b, n, DN_WIDTH)

def mla_q(cq, q_norm, w_uq, qk_norm_q, rope):
    b, n, _ = cq.shape
    q = (rms_norm(cq, q_norm) @ w_uq).reshape(b, n, MLA_HEADS, MLA_QK)
    return rope_tail(rms_norm(q, qk_norm_q), rope)

def mla_kv(ckv_in, kv_norm, w_ukv, qk_norm_k, rope):
    b, n, _ = ckv_in.shape
    ckv, k_rope = jnp.split(ckv_in, [MLA_KV_LORA], axis=-1)
    kv = (rms_norm(ckv, kv_norm) @ w_ukv).reshape(b, n, MLA_HEADS, MLA_NOPE + MLA_V)
    k_nope, v = jnp.split(kv, [MLA_NOPE], axis=-1)
    k = jnp.concatenate([k_nope, jnp.broadcast_to(k_rope[:, :, None, :], (b, n, MLA_HEADS, MLA_ROPE))], axis=-1)
    return rope_tail(rms_norm(k, qk_norm_k), rope), v

def attend(q, k, v):
    s = jnp.einsum('bqhd,bkhd->bhqk', q, k, preferred_element_type=jnp.float32) * MLA_QK ** -0.5
    p = jax.nn.softmax(s, axis=-1).astype(v.dtype)
    return jnp.einsum('bhqk,bkhd->bqhd', p, v)

def latent_attention(q, k, v, k_ctx, v_ctx):
    b, n, h, d = q.shape
    k_all = jnp.concatenate([k, k_ctx], axis=1)
    v_all = jnp.concatenate([v, v_ctx], axis=1)
    qb = q.reshape(b, n // Q_BLOCK, Q_BLOCK, h, d).transpose(1, 0, 2, 3, 4)
    o = lax.map(lambda qq: attend(qq, k_all, v_all), qb)
    return o.transpose(1, 0, 2, 3, 4).reshape(b, n, MLA_WIDTH)

def merge_branches(ya, yb, yc, gates, w_a, w_b, w_c, w_o):
    ga, gb, gc = jnp.split(gates, N_BRANCH, axis=-1)
    m = (jax.nn.sigmoid(ga) * (ya @ w_a) + jax.nn.sigmoid(gb) * (yb @ w_b)
         + jax.nn.sigmoid(gc) * (yc @ w_c))
    return m @ w_o

def token_mixing(uc, ux, rope, w_in, gm_ln, gm_ws, gm_bs, dn_conv, dn_a_log, dn_dt_bias, dn_out_norm,
                 mla_q_norm, mla_w_uq, mla_kv_norm, mla_w_ukv, mla_qk_norm_q, mla_qk_norm_k,
                 w_branch_gm, w_branch_dn, w_branch_mla, w_out, need_ctx):
    gm_c, qkv_c, z_c, ab_c, cq_c, ckv_c, gate_c = split_in(uc @ w_in)
    gm_x, qkv_x, z_x, ab_x, cq_x, ckv_x, gate_x = split_in(ux @ w_in)
    ya_x = chunk_gmlp_branch(gm_x, gm_ln, gm_ws, gm_bs)
    o_c, o_x = bidirectional_delta(qkv_c, ab_c, qkv_x, ab_x, dn_conv, dn_a_log, dn_dt_bias)
    yb_x = delta_output(o_x, z_x, dn_out_norm)
    k_c, v_c = mla_kv(ckv_c, mla_kv_norm, mla_w_ukv, mla_qk_norm_k, None)
    k_x, v_x = mla_kv(ckv_x, mla_kv_norm, mla_w_ukv, mla_qk_norm_k, rope)
    q_x = mla_q(cq_x, mla_q_norm, mla_w_uq, mla_qk_norm_q, rope)
    yc_x = latent_attention(q_x, k_x, v_x, k_c, v_c)
    y_x = merge_branches(ya_x, yb_x, yc_x, gate_x, w_branch_gm, w_branch_dn, w_branch_mla, w_out)
    if not need_ctx:
        return None, y_x
    ya_c = chunk_gmlp_branch(gm_c, gm_ln, gm_ws, gm_bs)
    yb_c = delta_output(o_c, z_c, dn_out_norm)
    q_c = mla_q(cq_c, mla_q_norm, mla_w_uq, mla_qk_norm_q, None)
    yc_c = attend(q_c, k_c, v_c).reshape(q_c.shape[0], q_c.shape[1], MLA_WIDTH)
    y_c = merge_branches(ya_c, yb_c, yc_c, gate_c, w_branch_gm, w_branch_dn, w_branch_mla, w_out)
    return y_c, y_x

def setup_inputs(seed: int = 0) -> dict:
    key = jax.random.key(seed)
    keys = iter(jax.random.split(key, 48))
    f32 = jnp.float32
    L, D = DEPTH, D_MODEL

    def nrm(shape, scale):
        return jax.random.normal(next(keys), shape, f32) * scale

    def gain(shape):
        return 1.0 + 0.05 * jax.random.normal(next(keys), shape, f32)

    dt = jnp.exp(jax.random.uniform(next(keys), (L, 2, DN_HEADS), f32, math.log(1e-3), math.log(1e-1)))
    a_log = jnp.log(jax.random.uniform(next(keys), (L, 2, DN_HEADS), f32, 1.0, 16.0))
    return {
        'x': nrm((BATCH, SEQ, D), 1.0),
        'c': nrm((BATCH, D), 1.0),
        'ctx': nrm((BATCH, CTX_LEN, D), 1.0),
        'c_ctx': nrm((D,), 1.0),
        'ada_w': nrm((L, D, N_MOD * D), D ** -0.5),
        'ada_b': nrm((L, N_MOD * D), 0.02),
        'ffn1_norm': gain((L, D)),
        'ffn1_w_gu': nrm((L, D, 2 * FFN_HIDDEN), D ** -0.5),
        'ffn1_w_down': nrm((L, FFN_HIDDEN, D), FFN_HIDDEN ** -0.5),
        'mix_norm': gain((L, D)),
        'w_in': nrm((L, D, IN_WIDTH), D ** -0.5),
        'gm_ln': gain((L, GM_WIDTH)),
        'gm_ws': nrm((L, GM_GROUPS, GM_CHUNK, GM_CHUNK), GM_CHUNK ** -0.5),
        'gm_bs': 1.0 + nrm((L, GM_GROUPS, GM_CHUNK), 0.1),
        'dn_conv': nrm((L, DN_CONV, 3 * DN_WIDTH), DN_CONV ** -0.5),
        'dn_a_log': a_log,
        'dn_dt_bias': jnp.log(jnp.expm1(dt)),
        'dn_out_norm': gain((L, DN_HEAD_DIM)),
        'mla_q_norm': gain((L, MLA_Q_LORA)),
        'mla_w_uq': nrm((L, MLA_Q_LORA, MLA_HEADS * MLA_QK), MLA_Q_LORA ** -0.5),
        'mla_kv_norm': gain((L, MLA_KV_LORA)),
        'mla_w_ukv': nrm((L, MLA_KV_LORA, MLA_HEADS * (MLA_NOPE + MLA_V)), MLA_KV_LORA ** -0.5),
        'mla_qk_norm_q': gain((L, MLA_QK)),
        'mla_qk_norm_k': gain((L, MLA_QK)),
        'w_branch_gm': nrm((L, GM_WIDTH, D), GM_WIDTH ** -0.5),
        'w_branch_dn': nrm((L, DN_WIDTH, D), DN_WIDTH ** -0.5),
        'w_branch_mla': nrm((L, MLA_WIDTH, D), MLA_WIDTH ** -0.5),
        'w_out': nrm((L, D, D), D ** -0.5),
        'ffn2_norm': gain((L, D)),
        'ffn2_w_gu': nrm((L, D, 2 * FFN_HIDDEN), D ** -0.5),
        'ffn2_w_down': nrm((L, FFN_HIDDEN, D), FFN_HIDDEN ** -0.5),
    }

def reference(x, c, ctx, c_ctx, ada_w, ada_b, ffn1_norm, ffn1_w_gu, ffn1_w_down, mix_norm, w_in,
              gm_ln, gm_ws, gm_bs, dn_conv, dn_a_log, dn_dt_bias, dn_out_norm,
              mla_q_norm, mla_w_uq, mla_kv_norm, mla_w_ukv, mla_qk_norm_q, mla_qk_norm_k,
              w_branch_gm, w_branch_dn, w_branch_mla, w_out, ffn2_norm, ffn2_w_gu, ffn2_w_down):
    rope = axial_rope_tables(x.shape[1], x.dtype)
    hx, hc = x, ctx
    for l in range(DEPTH):
        need_ctx = l < DEPTH - 1
        mx = jnp.split((jax.nn.silu(c) @ ada_w[l] + ada_b[l])[:, None, :], N_MOD, axis=-1)
        mc = jnp.split(jax.nn.silu(c_ctx) @ ada_w[l] + ada_b[l], N_MOD, axis=-1)
        hc = ada_ffn_half(hc, mc[0], mc[1], mc[2], ffn1_norm[l], ffn1_w_gu[l], ffn1_w_down[l])
        hx = ada_ffn_half(hx, mx[0], mx[1], mx[2], ffn1_norm[l], ffn1_w_gu[l], ffn1_w_down[l])
        uc = modulate(rms_norm(hc, mix_norm[l]), mc[3], mc[4])
        ux = modulate(rms_norm(hx, mix_norm[l]), mx[3], mx[4])
        yc, yx = token_mixing(uc, ux, rope, w_in[l], gm_ln[l], gm_ws[l], gm_bs[l], dn_conv[l],
                              dn_a_log[l], dn_dt_bias[l], dn_out_norm[l], mla_q_norm[l], mla_w_uq[l],
                              mla_kv_norm[l], mla_w_ukv[l], mla_qk_norm_q[l], mla_qk_norm_k[l],
                              w_branch_gm[l], w_branch_dn[l], w_branch_mla[l], w_out[l], need_ctx)
        hx = hx + mx[5] * yx
        hx = ada_ffn_half(hx, mx[6], mx[7], mx[8], ffn2_norm[l], ffn2_w_gu[l], ffn2_w_down[l])
        if need_ctx:
            hc = hc + mc[5] * yc
            hc = ada_ffn_half(hc, mc[6], mc[7], mc[8], ffn2_norm[l], ffn2_w_gu[l], ffn2_w_down[l])
    return hx


_drawn_inputs = setup_inputs


def setup_inputs(seed=0):
    import zlib

    import numpy as np

    out = dict(_drawn_inputs(seed))
    spreads = {}
    factors = {'gm_ln': 3.185,
     'dn_out_norm': 3.54,
     'mla_q_norm': 8.0,
     'mla_kv_norm': 7.604,
     'mla_qk_norm_q': 8.0,
     'mla_qk_norm_k': 8.0}
    for name, (base, spread) in spreads.items():
        noise = np.random.default_rng([zlib.crc32(name.encode()), seed]).standard_normal(out[name].shape)
        drawn = base * np.exp(spread * noise) if base else spread * noise
        out[name] = jnp.asarray(drawn.astype(out[name].dtype))
    for name, factor in factors.items():
        out[name] = (out[name] * factor).astype(out[name].dtype)
    return out
```

```python
from contextlib import ExitStack

import numpy as np

import concourse.bass as bass
from concourse import mybir

F32 = mybir.dt.float32
ACT = mybir.ActivationFunctionType
ALU = mybir.AluOpType
AX = mybir.AxisListType

P = 128
D = 1024
DC = D // P
SEQ = 256
CTX = 256
T = SEQ + CTX
DEPTH = 2
FFN = 2816
FC = FFN // P
EPS = 1e-6
GMW = 512
GMC = GMW // P
HEADS = 4
MH = 8
NOPE = 64
ROPE = 32
QK = NOPE + ROPE
LQ = 384
LKV = 256
GRID_W = 64
LEVELS = 7
UNIT = 256
PANEL = 8 * UNIT
RING = 6
ADA_FIRST = 13
ADA_PANELS = 36

PAR = {}
_at = 0
for _name, _n in (("gm_ln", 4), ("conv", 60),
                  ("dn_out", 1), ("q_norm", 3), ("kv_norm", 2), ("qk_q", 1), ("qk_k", 1),
                  ("dt_bias", 8), ("a_log", 8), ("gm_bs", 512), ("gm_ws", 512)):
    PAR[_name] = (_at, _n)
    _at += _n
NPAR = _at
CST = {}
_at = 0
for _name, _n in (("ident", 128), ("upto", 128), ("from", 128), ("ones", 128), ("level", LEVELS * 128),
                  ("cos", 256), ("sin", 256), ("rot", 32)):
    CST[_name] = (_at, _n)
    _at += _n
NCST = _at


def constants():
    c = np.zeros((P, NCST), np.float32)

    def put(name, a, rows=slice(0, P)):
        at, n = CST[name]
        c[rows, at:at + n] = a.reshape(a.shape[0], n)

    i = np.arange(P)
    put("ident", np.eye(P, dtype=np.float32))
    put("upto", (i[:, None] <= i[None, :]).astype(np.float32))
    put("from", (i[:, None] >= i[None, :]).astype(np.float32))
    put("ones", np.ones((P, P), np.float32))
    lev = np.zeros((P, LEVELS, P), np.float32)
    for n in range(LEVELS):
        b = 1 << n
        lev[:, n, :] = (i[:, None] // (2 * b) == i[None, :] // (2 * b)) & (i[:, None] // b != i[None, :] // b)
    put("level", lev)
    pos = np.arange(SEQ)
    half = ROPE // 2
    freq = (1.0 / (np.float32(10000.0) ** (np.arange(0, half, 2, dtype=np.float32) / np.float32(half)))).astype(np.float32)
    row = (pos // GRID_W).astype(np.float32)[:, None] * freq
    col = (pos % GRID_W).astype(np.float32)[:, None] * freq
    ang = np.concatenate([row, row, col, col], axis=-1)
    tail = slice(NOPE, QK)
    put("cos", np.cos(ang).astype(np.float32).T, tail)
    put("sin", np.sin(ang).astype(np.float32).T, tail)
    rot = np.zeros((ROPE, ROPE), np.float32)
    q = half // 2
    for base in (0, half):
        for m in range(q):
            rot[base + q + m, base + m] = -1.0
            rot[base + m, base + q + m] = 1.0
    put("rot", rot, tail)
    return c


def stream(inp):
    out = []

    def rows(w, cols):
        w = w[:, cols] if not isinstance(cols, slice) else w[:, cols]
        return w.reshape(w.shape[0] // P, P, w.shape[1]).transpose(1, 0, 2)

    def put(*parts):
        panel = np.zeros((P, PANEL), np.float32)
        at = 0
        for part in parts:
            flat = part.reshape(P, -1)
            panel[:, at:at + flat.shape[1]] = flat
            at += flat.shape[1]
        out.append(panel)

    def std(w, c0):
        put(rows(w, slice(c0, c0 + UNIT)))

    def ada(l, p):
        std(inp["ada_w"][l], p * UNIT)

    def ffn(l, f, carry):
        gu, down = inp[f"ffn{f + 1}_w_gu"][l], inp[f"ffn{f + 1}_w_down"][l]
        a = ADA_FIRST
        for i in range(FC // 2):
            std(gu, i * UNIT)
            std(gu, FFN + i * UNIT)
            if carry is not None:
                ada(carry, a)
                a += 1
        for g in range(4):
            w = rows(down, slice(g * UNIT, (g + 1) * UNIT))
            for s in range(3):
                put(w[:, 8 * s:8 * s + 8])
            if carry is not None:
                for _ in range(3):
                    ada(carry, a)
                    a += 1
        assert carry is None or a == ADA_PANELS

    for p in range(ADA_FIRST):
        ada(0, p)
    for l in range(DEPTH):
        ffn(l, 0, 0 if l == 0 else None)
        w = inp["w_in"][l]
        for i in range(4):
            std(w, i * UNIT)
        o = 2 * GMW + 4 * 512 + 16
        ab, cq, ckv = 2 * GMW + 4 * 512, o, o + LQ
        gates = ckv + LKV + ROPE
        put(rows(w, slice(cq, cq + 256)))
        put(rows(w, np.r_[cq + 256:cq + 384, ckv:ckv + 128]))
        put(rows(w, np.r_[ckv + 128:ckv + 256 + ROPE, ab:ab + 16]))
        uq, ukv = inp["mla_w_uq"][l], inp["mla_w_ukv"][l]
        h = np.arange(MH)[:, None] * 128
        put(rows(ukv, np.concatenate([(h + np.arange(64)).ravel(), (h + 64 + np.arange(64)).ravel()])))
        put(rows(uq, slice(0, 4 * QK)))
        put(rows(uq, slice(4 * QK, 8 * QK)))
        for i in range(6):
            std(w, 2 * GMW + i * UNIT)
        for i in range(2):
            std(w, 2 * GMW + 1536 + i * UNIT)
        for g in range(4):
            cols = slice(g * UNIT, (g + 1) * UNIT)
            for b in range(3):
                std(w, gates + b * D + g * UNIT)
            put(rows(inp["w_branch_gm"][l], cols), rows(inp["w_branch_dn"][l], cols))
            put(rows(inp["w_branch_mla"][l], cols))
            if l + 1 < DEPTH:
                for p in range(3 * g, 3 * g + 3 + (g == 3)):
                    ada(l + 1, p)
        for g in range(4):
            std(inp["w_out"][l], g * UNIT)
        ffn(l, 1, l + 1 if l + 1 < DEPTH else None)
    return np.stack(out)


def params(inp):
    out = np.zeros((P, DEPTH, NPAR), np.float32)

    def feat(v):
        return v.reshape(-1, P).T

    for l in range(DEPTH):
        def put(name, a, rows=slice(0, P)):
            at, n = PAR[name]
            out[rows, l, at:at + n] = a.reshape(a.shape[0], n)

        put("gm_ln", feat(inp["gm_ln"][l]))
        put("conv", inp["dn_conv"][l].reshape(5, 12, P).transpose(2, 1, 0))
        put("dn_out", feat(inp["dn_out_norm"][l]))
        put("q_norm", feat(inp["mla_q_norm"][l]))
        put("kv_norm", feat(inp["mla_kv_norm"][l]))
        put("qk_q", inp["mla_qk_norm_q"][l][:, None], slice(0, QK))
        put("qk_k", inp["mla_qk_norm_k"][l][:, None], slice(0, QK))
        put("dt_bias", np.broadcast_to(inp["dn_dt_bias"][l].reshape(1, 8), (P, 8)))
        put("a_log", np.broadcast_to(inp["dn_a_log"][l].reshape(1, 8), (P, 8)))
        put("gm_bs", np.broadcast_to(inp["gm_bs"][l].reshape(1, 512), (P, 512)))
        put("gm_ws", inp["gm_ws"][l].transpose(2, 0, 1))
    return out.reshape(P, DEPTH * NPAR)


def modulation_params(inp):
    both = [np.concatenate([inp["ada_b"][l], inp["ffn1_norm"][l], inp["mix_norm"][l], inp["ffn2_norm"][l]])
            for l in range(DEPTH)]
    return np.stack(both).reshape(DEPTH, 96, P).transpose(2, 0, 1)


N_PANELS = ADA_FIRST + (22 + 12) * 4 + 23 * 2 + DEPTH * (4 + 3 + 1 + 2 + 8 + 20 + 4) + ADA_FIRST


def product_owners():
    number, owner = {}, []

    def add(key, who):
        number[key] = len(owner)
        owner.append(who)

    for l in range(DEPTH):
        nt = 4 if l + 1 < DEPTH else 2
        for f in range(2):
            if f == 1:
                for c in range(GMC):
                    add((l, "gmu", c), "a")
                for p in range(2):
                    for t in range(nt):
                        add((l, "gmv", p, t), "a")
                for c in range(3):
                    add((l, "cq", c), "a")
                for c in range(2):
                    add((l, "ckv", c), "a")
                add((l, "krope"), "a")
                add((l, "ab"), "v")
                for c in range(GMC):
                    add((l, "spatial", c), "v")
                for c in range(4):
                    add((l, "nope", c), "a")
                for t in range(4):
                    add((l, "mv", t), "a")
                for h in range(MH):
                    add((l, "uq", h), "a")
                for c in range(12):
                    add((l, "qkv", c), "a")
                for c in range(4):
                    add((l, "z", c), "a")
                for pair in range(DC // 2):
                    for kind, who in (("gate", "a"), ("branch", "v")):
                        for b in range(3):
                            for j in (2 * pair, 2 * pair + 1):
                                add((l, kind, j, b), who)
                for j in range(DC):
                    add((l, "out", j), "v")
            for i in range(FC // 2):
                for c in (2 * i, 2 * i + 1):
                    add((l, "g", f, c), "a")
                for c in (2 * i, 2 * i + 1):
                    add((l, "u", f, c), "v")
            for j in range(DC):
                add((l, "down", f, j), "v")
    counts = {"a": [0], "v": [0]}
    for who in owner:
        for k in "av":
            counts[k].append(counts[k][-1] + (who == k))
    return number, owner, counts


def backbone(nc, wts, par_d, cst_d, mod_d, x_d, c_d, out_d, dbg=None):
    number, owner, counts = product_owners()
    with ExitStack() as ctx:
        def sb(name, shape):
            return ctx.enter_context(nc.sbuf_tensor(name, shape, F32))

        def sem(name):
            return ctx.enter_context(nc.semaphore(name))

        ring = sb("ring", [P, RING * PANEL])
        h = sb("h", [P, DC, T])
        uT = sb("uT", [P, DC, T])
        ya = sb("ya", [P, 4, T])
        yb = sb("yb", [P, 4, T])
        yc = sb("yc", [P, 4, T])
        sq = sb("sq", [P, 4, T])
        rt = sb("rt", [P, 2, T])
        par = sb("par", [P, NPAR])
        cst = sb("cst", [P, NCST])
        cond = sb("cond", [P, DC, 2])
        mod_par = sb("mod_par", [P, DEPTH, 96])
        mods = sb("mods", [P, DEPTH, 72, 2])
        scales = sb("scales", [P, DEPTH, 3, DC, 2])
        small = sb("small", [P, 256])
        WORK = 36 * T
        work = sb("work", [P, WORK])

        def view(at, n, w=T):
            return work[:, at * T:at * T + n * w].rearrange("p (n w) -> p n w", w=w)

        hidden = view(0, FC)
        sg = view(FC, 4)
        gv = view(29, 4)
        gtmp = view(33, 2)
        cq = view(0, 3)
        ckv = view(3, 2)
        kr = view(5, 1)
        krw = view(6, 1)
        rsin = view(7, 2)
        kk = view(9, MH)
        qq = view(9 + MH, MH)
        vm = view(25, 4)
        pr = view(29, 2)
        prT = view(31, 2)
        qT = view(0, 4)
        kT = view(4, 4)
        ktok = view(8, 4)
        vtok = view(12, 4)
        S = view(16, 2)
        E = view(18, 2)
        EG = view(20, 2)
        att = view(22, 2)
        mt = view(24, 2)
        ml = view(26, 2)
        X = view(28, 2)
        XT = view(30, 2)
        Y = view(32, 2)
        gB = view(34, 2)
        vnew, nwT, kd, kg = mt, X, Y, gB
        vT = view(32, 2)
        acc = view(30, 2)
        CONV = 16 * T
        convin = work[:, CONV:CONV + 3 * 520].rearrange("p (n s w) -> p n s w", n=3, s=2)
        mT = view(0, DC)
        sig = view(8, 6)
        mtmp = view(18, 2)
        zs = view(14, 4)
        assert CONV + 3 * 520 <= WORK

        gab = small[:, 0:64].rearrange("p (t c) -> p t c", c=16)
        g = small[:, 64:96].rearrange("p (t c) -> p t c", c=8)
        beta = small[:, 96:128].rearrange("p (t c) -> p t c", c=8)
        t1 = small[:, 128:160].rearrange("p (t c) -> p t c", c=8)
        expa = small[:, 160:168]
        gamc = small[:, 168:176].rearrange("p (d c) -> p d c", c=4)
        egam = small[:, 176:184].rearrange("p (d c) -> p d c", c=4)
        kds = small[:, 184:192].rearrange("p (d c) -> p d c", c=4)
        mx = small[:, 192:194]
        nb = small[:, 194:196]
        eL = small[:, 220:228].rearrange("p (d c) -> p d c", c=4)
        rs = small[:, 196:198]
        ri = small[:, 198:200]
        stats = small[:, 200:206]
        mv = small[:, 208:216].rearrange("p (t c) -> p t c", c=2)
        lnr = small[:, 216:220]
        eps = small[:, 228:229]

        bank = [ctx.enter_context(nc.psum_tensor(f"bank{i}", [P, 512], F32)) for i in range(8)]

        def C(name, rows=slice(0, P)):
            at, n = CST[name]
            return cst[rows, at:at + n]

        def par_of(name, a=0, b=None, rows=slice(0, P)):
            at, n = PAR[name]
            return par[rows, at + a:at + (n if b is None else b)]

        ident, ones = C("ident"), C("ones")
        tail = slice(NOPE, QK)

        def heads(ap):
            return ap.rearrange("p (h c) -> p h c", h=HEADS)

        inputs_in = sem("inputs_in")
        par_in = sem("par_in")
        par_free = sem("par_free")
        panel_in = [sem(f"panel_in{i}") for i in range(RING)]
        panel_used = sem("panel_used")
        cond_ready = sem("cond_ready")
        ada_done = sem("ada_done")
        mods_ready = sem("mods_ready")
        prod = sem("prod")
        drained = {"a": sem("drained_by_act"), "v": sem("drained_by_dve")}
        squares = sem("squares")
        summed = sem("summed")
        roots = sem("roots")
        scaled = sem("scaled")
        normed = sem("normed")
        mod_done = sem("mod_done")
        gmv_norm = sem("gmv_norm")
        gmv_var = sem("gmv_var")
        gmv_root = sem("gmv_root")
        ya_ready = sem("ya_ready")
        pads = sem("pads")
        kr_ready = sem("kr_ready")
        kr_rot = sem("kr_rot")
        krw_ready = sem("krw_ready")
        q_rot = sem("q_rot")
        q_ready = sem("q_ready")
        k_ready = sem("k_ready")
        att_s = sem("att_s")
        att_max = sem("att_max")
        att_exp = sem("att_exp")
        att_p = sem("att_p")
        att_t = sem("att_t")
        att_pt = sem("att_pt")
        att_o = sem("att_o")
        att_y = sem("att_y")
        conv_done = sem("conv_done")
        conv_silu = sem("conv_silu")
        tok_t = sem("tok_t")
        tok_c = sem("tok_c")
        dt_ready = sem("dt_ready")
        dt_ln = sem("dt_ln")
        g_ready = sem("g_ready")
        dpe = [sem(f"delta_product{d}") for d in range(2)]
        dact = [sem(f"delta_act{d}") for d in range(2)]
        ddve = [sem(f"delta_dve{d}") for d in range(2)]
        dpool = [sem(f"delta_pool{d}") for d in range(2)]
        m_ready = sem("m_ready")
        yb_ready = sem("yb_ready")
        eps_ready = sem("eps_ready")
        act_step = sem("act_step")
        dve_step = sem("dve_step")
        pool_step = sem("pool_step")
        out_done = sem("out_done")
        ATT = [0, 4 * MH]

        class Steps:

            def __init__(self, eng, s):
                self.eng, self.s, self.n = eng, s, 0

            def __call__(self, ins):
                ins.then_inc(self.s, 1)
                self.n += 1
                return self.n

            def wait(self, n=None):
                self.eng.wait_ge(self.s, self.n if n is None else n)

        def unit_plan():
            plan, n, m = {}, 0, 0

            def add(key, k):
                nonlocal n, m
                plan[key] = (n, m, k)
                n += 1
                m += k

            for l in range(DEPTH):
                add((l, "norm", 0), DC)
                add((l, "norm", 1), DC)
                add((l, "cq"), 3)
                add((l, "ckv"), 2)
                for hd in range(MH):
                    add((l, "k", hd), 1)
                for hd in range(MH):
                    add((l, "q", hd), 1)
                for c in range(8):
                    add((l, "qk", c), 1)
                for c in range(4):
                    add((l, "o", c), 1)
                add((l, "norm", 2), DC)
            return plan

        units = unit_plan()

        def width(l):
            return T if l + 1 < DEPTH else SEQ

        def halves(nt):
            return [(0, slice(0, SEQ)), (1, slice(SEQ, T))][:nt // SEQ]

        def count_after(q, who):
            return counts[who][q + 1]

        def wait_drained(eng, key):
            q = number[key] if isinstance(key, tuple) else key
            eng.wait_ge(drained[owner[q]], count_after(q, owner[q]))

        def wait_product(eng, key):
            eng.wait_ge(prod, number[key] + 1)

        def bank_of(key):
            return bank[number[key] % 4]

        ORDER = [[2, 3, 0, 1], [3, 2, 1, 0]]
        D_PE, D_ACT, D_DVE, D_POOL = 18, 11, 16, 8
        block = ctx.enter_context(nc.Block())

        @block.sync
        def _(sp):
            sp.dma_start(cond[:, :, :], c_d).then_inc(inputs_in, 16)
            for i in range(RING):
                sp.dma_start(ring[:, i * PANEL:(i + 1) * PANEL], wts[i]).then_inc(panel_in[i], 16)
            for k in range(DC):
                sp.dma_start(h[:, k, :], x_d[k * P:(k + 1) * P, :]).then_inc(inputs_in, 16)
            sp.dma_start(mod_par[:, :, :], mod_d).then_inc(inputs_in, 16)
            sp.dma_start(cst[:, :], cst_d).then_inc(inputs_in, 16)
            sp.dma_start(par[:, :], par_d[:, 0:NPAR]).then_inc(par_in, 16)
            rounds = N_PANELS // RING

            with sp.Fori(1, rounds) as r:
                for i in range(RING):
                    sp.wait_ge(panel_used, r * RING + (i - RING + 1))
                    sp.dma_start(ring[:, i * PANEL:(i + 1) * PANEL],
                                 wts[bass.ds(r * RING + i, 1)].rearrange("o p n -> p (o n)")).then_inc(panel_in[i], 16)
            for n in range(rounds * RING, N_PANELS):
                sp.wait_ge(panel_used, n - RING + 1)
                i = n % RING
                sp.dma_start(ring[:, i * PANEL:(i + 1) * PANEL], wts[n]).then_inc(panel_in[i], 16)
            last = DEPTH - 1
            for j in range(DC):
                wait_drained(sp, (last, "down", 1, j))
                sp.dma_start(out_d[j * P:(j + 1) * P, :], h[:, j, 0:SEQ]).then_inc(out_done, 16)
            sp.wait_ge(out_done, 16 * DC)

        @block.gpsimd
        def _(pool):
            pool.memset(eps, EPS).then_inc(eps_ready, 1)
            pool.wait_ge(inputs_in, 16 * (DC + 3))
            for l in range(DEPTH):
                pool.wait_ge(att_y, ATT[l] + width(l) // P * MH)
                for a in (0, 258):
                    last = pool.memset(convin[:, :, :, a:a + 2], 0.0)
                last.then_inc(pads, 1)
                for j in range(4):
                    it = l * 4 + j
                    for d in range(2):
                        pool.wait_ge(dact[d], it * D_ACT + 1)
                        mask = C("upto" if d == 0 else "from").unsqueeze(1).to_broadcast([P, HEADS, P])
                        pool.tensor_tensor(heads(E[:, d, :]), heads(E[:, d, :]), mask, ALU.mult).then_inc(dpool[d], 1)
                    for n in range(LEVELS):
                        for d in range(2):
                            if n == 0:
                                pool.wait_ge(ddve[d], it * D_DVE + 5)
                            elif n == 2:
                                pool.wait_ge(ddve[d], it * D_DVE + 6)
                            elif n >= 3:
                                pool.wait_ge(dpe[d], it * D_PE + 2 + 2 * (n - 2))
                            dst = (ml if n % 2 == 0 else E)[:, d, :]
                            mask = C("level")[:, n * P:(n + 1) * P].unsqueeze(1).to_broadcast([P, HEADS, P])
                            pool.tensor_tensor(heads(dst), heads(mt[:, d, :]), mask, ALU.mult).then_inc(dpool[d], 1)

        @block.scalar
        def _(act):
            step = Steps(act, act_step)

            def square(key, k, src, rows=slice(0, P), w=T, stop=slice(0, P)):
                n, m, _ = units[key]
                m += k
                if m >= 4:
                    act.wait_ge(summed, m - 3)
                act.activation(sq[rows, m % 4, 0:w], src, ACT.Square).then_inc(squares, 1)

            def root(key, size, w=T, rows=slice(0, P)):
                n, m, k = units[key]
                act.wait_ge(summed, m + k)
                if n >= 2:
                    act.wait_ge(scaled, n - 1)
                act.activation(rt[rows, n % 2, 0:w], bank[4 + n % 2][rows, 0:w], ACT.Sqrt, bias=eps[rows, :],
                               scale=1.0 / size).then_inc(roots, 1)

            def norm(l, i, w, h_key):
                n, m, _ = units[(l, "norm", i)]
                for k in range(DC):
                    if h_key is not None:
                        wait_drained(act, h_key + (k,))
                    square((l, "norm", i), k, h[:, k, 0:w], w=w)
                root((l, "norm", i), D, w)
                act.wait_ge(mods_ready, 2 * l + (1 if i == 0 else 2))
                for k in range(DC):
                    if k < DC - 1:
                        act.wait_ge(normed, (3 * l + i) * (DC - 1) + k + 1)
                    else:
                        act.wait_ge(scaled, n + 1)
                    for s, cols in halves(w):
                        last = act.activation(uT[:, k, cols], uT[:, k, cols], ACT.Identity,
                                              scale=scales[:, l, i, k, s:s + 1],
                                              bias=mods[:, l, 3 * i * DC + k, s:s + 1])
                    last.then_inc(mod_done, 1)

            def silus(l, f, w):
                q0 = number[(l, "g", f, 0)]

                def pair(i, i0, per):
                    for c in range(2):
                        act.wait_ge(prod, q0 + 1 + 4 * i0 + c + 4 * per)
                        if i >= 2:
                            act.wait_ge(drained["v"], counts["v"][q0] + 2 * (i0 - 2) + c + 1 + 2 * per)
                        act.activation(sg[:, 2 * (i % 2) + c, 0:w], bank[(q0 + c) % 4][:, 0:w],
                                       ACT.Silu).then_inc(drained["a"], 1)

                pair(0, 0, 0)
                pair(1, 1, 0)
                with act.Fori(0, 4) as r:
                    pair(2, 2, r * 2)
                    pair(3, 3, r * 2)
                pair(10, 10, 0)

            act.wait_ge(inputs_in, 16 * (DC + 3))
            act.activation(cond[:, :, :], cond[:, :, :], ACT.Silu).then_inc(cond_ready, 1)
            act.wait_ge(eps_ready, 1)
            for l in range(DEPTH):
                w = width(l)
                nt = w // P
                if l:
                    wait_drained(act, (l - 1, "out", DC - 1))
                    act.dma_start(par[:, :], par_d[:, l * NPAR:(l + 1) * NPAR]).then_inc(par_in, 16)
                norm(l, 0, T, (l - 1, "down", 1) if l else None)
                silus(l, 0, T)
                norm(l, 1, T, (l, "down", 0))

                for c in range(GMC):
                    wait_product(act, (l, "gmu", c))
                    act.activation(ya[:, c, 0:w], bank_of((l, "gmu", c))[:, 0:w],
                                   ACT.Gelu_apprx_tanh).then_inc(drained["a"], 1)
                for p in range(2):
                    for t in range(nt):
                        wait_product(act, (l, "gmv", p, t))
                        act.activation(gv[:, t, p * UNIT:(p + 1) * UNIT], bank_of((l, "gmv", p, t))[:, 0:UNIT],
                                       ACT.Gelu_apprx_tanh).then_inc(drained["a"], 1)
                act.wait_ge(gmv_var, l + 1)
                act.activation(lnr[:, 0:nt], mv[:, 0:nt, 1], ACT.Sqrt, bias=eps[:, :]).then_inc(gmv_root, 1)

                for i in range(3):
                    key = (l, "cq", i)
                    wait_product(act, key)
                    square((l, "cq"), i, bank_of(key)[:, 0:w], w=w)
                    act.activation(cq[:, i, 0:w], bank_of(key)[:, 0:w], ACT.Copy).then_inc(drained["a"], 1)
                for i in range(2):
                    key = (l, "ckv", i)
                    wait_product(act, key)
                    square((l, "ckv"), i, bank_of(key)[:, :])
                    act.activation(ckv[:, i, :], bank_of(key)[:, :], ACT.Copy).then_inc(drained["a"], 1)
                key = (l, "krope")
                wait_product(act, key)
                act.activation(kr[tail, 0, :], bank_of(key)[tail, :], ACT.Copy).then_inc(drained["a"], 1)
                root((l, "cq"), LQ, w)
                root((l, "ckv"), LKV)
                act.wait_ge(drained["a"], count_after(number[key], "a"))
                act.wait_ge(summed, units[(l, "ckv")][1] + 2)
                for i in range(4):
                    act.activation(sq[tail, i, :], kr[tail, 0, :], ACT.Square)
                for hd in range(MH):
                    key = (l, "nope", hd // 2)
                    rows = slice(NOPE * (hd % 2), NOPE * (hd % 2) + NOPE)
                    if hd % 2 == 0:
                        wait_product(act, key)
                    square((l, "k", hd), 0, bank_of(key)[rows, :], slice(0, NOPE))
                    last = act.activation(kk[0:NOPE, hd, :], bank_of(key)[rows, :], ACT.Copy)
                    if hd % 2:
                        last.then_inc(drained["a"], 1)
                    if hd:
                        root((l, "k", hd - 1), QK, rows=slice(0, QK))
                root((l, "k", MH - 1), QK, rows=slice(0, QK))
                for t in range(4):
                    wait_product(act, (l, "mv", t))
                    act.activation(vm[:, t, :], bank_of((l, "mv", t))[:, :], ACT.Copy).then_inc(drained["a"], 1)
                for hd in range(MH):
                    key = (l, "uq", hd)
                    wait_product(act, key)
                    square((l, "q", hd), 0, bank_of(key)[0:QK, 0:w], slice(0, QK), w)
                    act.activation(qq[0:QK, hd, 0:w], bank_of(key)[0:QK, 0:w], ACT.Copy).then_inc(drained["a"], 1)
                    if hd:
                        root((l, "q", hd - 1), QK, w, slice(0, QK))
                root((l, "q", MH - 1), QK, w, slice(0, QK))
                a0 = ATT[l]
                for i in range(nt * MH + 1):
                    a = a0 + i
                    if i < nt * MH:
                        act.wait_ge(att_max, a + 1)
                        keys = slice(0, T) if i // MH < 2 else slice(0, CTX)
                        if a >= 2:
                            act.wait_ge(att_t, a - 1)
                        act.activation(pr[:, a % 2, keys], bank[a % 2][:, keys], ACT.Exp,
                                       scale=QK ** -0.5, bias=nb[:, a % 2:a % 2 + 1],
                                       accum_out=rs[:, a % 2:a % 2 + 1]).then_inc(att_exp, 1)
                    if i > 0:
                        b = a - 1
                        nk = 4 if (i - 1) // MH < 2 else 2
                        act.wait_ge(att_t, b + 1)
                        if b >= 2:
                            act.wait_ge(att_o, b - 1)
                        act.activation(prT[:, b % 2, 0:nk * P], bank[2 + b % 2][:, 0:nk * P],
                                       ACT.Copy).then_inc(att_pt, 1)

                act.wait_ge(dt_ready, l + 1)
                act.wait_ge(par_in, 16 * (l + 1))
                act.activation(t1, t1, ACT.Exp, scale=-1.0)
                act.activation(beta, gab[:, :, 8:16], ACT.Exp, scale=-1.0)
                step(act.activation(expa, par_of("a_log"), ACT.Exp))
                step.wait()
                act.activation(t1, t1, ACT.Ln, bias=ones[:, 0:1]).then_inc(dt_ln, 1)

                def conv_in(c):
                    key = (l, "qkv", c)
                    wait_product(act, key)
                    if 12 * l + c >= 3:
                        act.wait_ge(conv_done, 12 * l + c - 2)
                    act.activation(convin[:, c % 3, :, 2:258],
                                   bank_of(key)[:, :].rearrange("p (s w) -> p s w", s=2),
                                   ACT.Copy).then_inc(drained["a"], 1)

                def conv_out(c):
                    act.wait_ge(conv_done, 12 * l + c + 1)
                    dst = qT[:, c, :] if c < 4 else kT[:, c - 4, :] if c < 8 else vT[:, c % 2, :]
                    if c >= 10:
                        act.wait_ge(tok_t, 8 * l + c - 9)
                    act.activation(dst, acc[:, c % 2, :], ACT.Silu).then_inc(conv_silu, 1)

                def tok_copy(i):
                    act.wait_ge(tok_t, 8 * l + i + 1)
                    dst = (vtok if i < 4 else ktok)[:, :, (i % 4) * P:(i % 4 + 1) * P]
                    act.activation(dst, bank[6][:, :].rearrange("p (t c) -> p t c", t=4),
                                   ACT.Copy).then_inc(tok_c, 1)

                conv_in(0)
                conv_in(1)
                for c in range(12):
                    if c + 2 < 12:
                        conv_in(c + 2)
                    conv_out(c)
                    if c >= 9:
                        tok_copy(c - 9)
                tok_copy(3)
                act.wait_ge(conv_silu, 12 * l + 12)
                for i in range(9):
                    if i < 8:
                        square((l, "qk", i), 0, (kT if i < 4 else qT)[:, i % 4, :])
                    if i > 0:
                        root((l, "qk", i - 1), 1.0)
                    if 2 <= i <= 5:
                        tok_copy(2 + i)

                for j in range(4):
                    it = l * 4 + j
                    for d in range(2):
                        A = bank[3 * d]
                        act.wait_ge(ddve[d], it * D_DVE + 2)
                        act.activation(E[:, d, :], E[:, d, :], ACT.Exp).then_inc(dact[d], 1)
                        act.activation(EG[:, d, :], A[:, :], ACT.Exp).then_inc(dact[d], 1)
                        act.wait_ge(ddve[d], it * D_DVE + 3)
                        act.activation(egam[:, d, :], gamc[:, d, :], ACT.Exp)
                        act.activation(kds[:, d, :], kds[:, d, :], ACT.Exp).then_inc(dact[d], 1)
                    for n in range(LEVELS):
                        for d in range(2):
                            act.wait_ge(dpe[d], it * D_PE + (3 if n == 0 else 2 + 2 * n))
                            act.activation((X if n == 0 else Y)[:, d, :], bank[3 * d][:, :],
                                           ACT.Copy).then_inc(dact[d], 1)
                    for d in range(2):
                        act.wait_ge(dpe[d], it * D_PE + 16)
                        act.activation(nwT[:, d, :], bank[3 * d][:, :], ACT.Copy, scale=-1.0).then_inc(dact[d], 1)

                for d in range(2):
                    act.wait_ge(ddve[d], (l * 4 + 4) * D_DVE)
                for i in range(5):
                    if i < 4:
                        square((l, "o", i), 0, yb[:, i, 0:w], w=w)
                    if i > 0:
                        root((l, "o", i - 1), P, w)
                for c in range(4):
                    key = (l, "z", c)
                    wait_product(act, key)
                    act.activation(zs[:, c, 0:w], bank_of(key)[:, 0:w], ACT.Silu).then_inc(drained["a"], 1)

                for pair in range(DC // 2):
                    for b in range(3):
                        for c in range(2):
                            key = (l, "gate", 2 * pair + c, b)
                            wait_product(act, key)
                            if pair:
                                wait_drained(act, (l, "branch", 2 * pair + c - 2, b))
                            act.activation(sig[:, 2 * b + c, 0:w], bank_of(key)[:, 0:w],
                                           ACT.Sigmoid).then_inc(drained["a"], 1)
                norm(l, 2, w, (l, "out"))
                silus(l, 1, w)

        @block.tensor
        def _(pe):
            class Panels:

                def __init__(self):
                    self.n, self.first, self.extra = 0, False, 0

                def take(self):
                    slot = self.n % RING
                    pe.wait_ge(panel_in[slot], 16 * (self.n // RING + 1) + self.extra)
                    self.first = self.n > 0
                    self.n += 1
                    return ring[:, slot * PANEL:(slot + 1) * PANEL]

                def used(self, ins):
                    if self.first:
                        ins.then_inc(panel_used, 1)
                        self.first = False
                    return ins

            panels = Panels()

            def free_bank(key):
                q = number[key]
                if q >= 4:
                    wait_drained(pe, q - 4)

            def product(out, parts, signal):
                for n, (lhsT, rhs) in enumerate(parts):
                    last = pe.matmul(out, lhsT, rhs, start=n == 0, stop=n == len(parts) - 1)
                    if n == 0:
                        panels.used(last)
                if signal is not None:
                    last.then_inc(signal, 1)

            def units_of(panel, width=UNIT):
                return panel.rearrange("p (k n) -> p k n", n=width)

            def ada(l, p):
                panel = units_of(panels.take())
                for c in range(2):
                    at = (p * 2 + c) * 2
                    out = bank[7][:, bass.ds(at, 2)] if not isinstance(at, int) else bank[7][:, at:at + 2]
                    product(out, [(panel[:, k, c * P:(c + 1) * P], cond[:, k, :]) for k in range(DC)],
                            ada_done if c else None)

            def sums(key, w=T, rows=slice(0, P)):
                n, m, count = units[key]
                if n >= 2:
                    pe.wait_ge(roots, n - 1)
                for k in range(count):
                    pe.wait_ge(squares, m + k + 1)
                    pe.matmul(bank[4 + n % 2][:, 0:w], ones[rows, :], sq[rows, (m + k) % 4, 0:w],
                              start=k == 0, stop=k == count - 1).then_inc(summed, 1)

            def std(keys, w, src, ready, base):
                panel = units_of(panels.take())
                for c, key in enumerate(keys):
                    free_bank(key)
                    parts = []
                    out = bank_of(key)[:, 0:w]
                    for k in range(DC):
                        if ready is not None:
                            pe.wait_ge(ready, base + k + 1)
                        last = pe.matmul(out, panel[:, k, c * P:(c + 1) * P], src[:, k, 0:w],
                                         start=k == 0, stop=k == DC - 1)
                        if k == 0:
                            panels.used(last)
                    ready = None
                    last.then_inc(prod, 1)

            def ffn(l, f, w, carry, ready_base):
                q0 = number[(l, "g", f, 0)]
                v0 = counts["v"][q0]
                a0 = counts["a"][q0]
                d0 = number[(l, "down", f, 0)]

                def pair(i, per, first):
                    for part in range(2):
                        panel = units_of(panels.take())
                        for c in range(2):
                            b = 2 * part + c
                            if first:
                                free_bank((l, "gu"[part], f, c))
                            elif part == 0:
                                pe.wait_ge(drained["a"], a0 + 2 * (i - 1) + c + 1 + 2 * per)
                            else:
                                pe.wait_ge(drained["v"], v0 + 2 * (i - 1) + c + 1 + 2 * per)
                            for k in range(DC):
                                if first and b == 0:
                                    pe.wait_ge(mod_done, ready_base + k + 1)
                                last = pe.matmul(bank[(q0 + b) % 4][:, 0:w], panel[:, k, c * P:(c + 1) * P],
                                                 uT[:, k, 0:w], start=k == 0, stop=k == DC - 1)
                                if k == 0:
                                    panels.used(last)
                            last.then_inc(prod, 1)
                    if carry is not None:
                        ada(carry, ADA_FIRST + i + per)

                if carry is not None:
                    pe.wait_ge(mods_ready, 2 * carry + 1)
                peel, per_body = (1, 2) if carry is not None else (2, 3)
                for i in range(peel):
                    pair(i, 0, i == 0)
                rounds = (FC // 2 - peel) // per_body
                n0 = panels.n
                with pe.Fori(0, rounds) as r:
                    taken = per_body * (3 if carry is not None else 2)
                    panels.extra = r * (16 * taken // RING)
                    for i in range(per_body):
                        pair(peel + i, r * per_body, False)
                panels.extra = 0
                panels.n = n0 + rounds * taken

                pe.wait_ge(drained["a"], a0 + FC)
                vd = counts["v"][d0]
                n0 = panels.n
                per_group = 6 if carry is not None else 3
                with pe.Fori(0, 2) as r:
                    panels.extra = r * (16 * 2 * per_group // RING)
                    for g in range(2):
                        for s in range(3):
                            panel = units_of(panels.take())
                            if g == 0:
                                pe.wait_ge(drained["v"], v0 + min(8 * s + 8, FC))
                            for k in range(8 * s, min(8 * s + 8, FC)):
                                for c in range(2):
                                    m = 2 * g + c
                                    if k == 0:
                                        pe.wait_ge(drained["v"], r * 4 + (vd + m - 3))
                                    last = pe.matmul(bank[(d0 + m) % 4][:, 0:w], panel[:, k - 8 * s, c * P:(c + 1) * P],
                                                     hidden[:, k, 0:w], start=k == 0, stop=k == FC - 1)
                                    if k == 8 * s and c == 0:
                                        panels.used(last)
                                    if k == FC - 1:
                                        last.then_inc(prod, 1)
                        if carry is not None:
                            for s in range(3):
                                ada(carry, r * 6 + (ADA_FIRST + FC // 2 + 3 * g + s))
                panels.extra = 0
                panels.n = n0 + 4 * per_group

            pe.wait_ge(inputs_in, 16 * (DC + 3))
            pe.wait_ge(cond_ready, 1)
            for p in range(ADA_FIRST):
                ada(0, p)
            for l in range(DEPTH):
                w = width(l)
                nt = w // P
                sums((l, "norm", 0))
                ffn(l, 0, T, 0 if l == 0 else None, (3 * l) * DC)
                sums((l, "norm", 1))

                for p in range(2):
                    std([(l, "gmu", 2 * p), (l, "gmu", 2 * p + 1)], w, uT, mod_done if p == 0 else None,
                        (3 * l + 1) * DC)
                for p in range(2):
                    panel = units_of(panels.take())
                    for t in range(nt):
                        key = (l, "gmv", p, t)
                        free_bank(key)
                        product(bank_of(key)[:, 0:UNIT],
                                [(uT[:, k, t * P:(t + 1) * P], panel[:, k, :]) for k in range(DC)], prod)

                def rows_product(key, out, panel, at, m):
                    free_bank(key)
                    product(out, [(panel[:, k, at:at + m], uT[:, k, 0:out.shape[-1]]) for k in range(DC)], prod)

                p0 = units_of(panels.take())
                for i in range(2):
                    rows_product((l, "cq", i), bank_of((l, "cq", i))[:, 0:w], p0, i * P, P)
                p1 = units_of(panels.take())
                rows_product((l, "cq", 2), bank_of((l, "cq", 2))[:, 0:w], p1, 0, P)
                rows_product((l, "ckv", 0), bank_of((l, "ckv", 0))[:, :], p1, P, P)
                p2 = panels.take()[:, 0:8 * 176].rearrange("p (k n) -> p k n", n=176)
                rows_product((l, "ckv", 1), bank_of((l, "ckv", 1))[:, :], p2, 0, P)
                rows_product((l, "krope"), bank_of((l, "krope"))[tail, :], p2, P, ROPE)
                key = (l, "ab")
                free_bank(key)
                for t in range(4):
                    for k in range(DC):
                        last = pe.matmul(bank_of(key)[:, 16 * t:16 * t + 16], uT[:, k, t * P:(t + 1) * P],
                                         p2[:, k, 160:176], start=k == 0, stop=k == DC - 1)
                last.then_inc(prod, 1)
                sums((l, "cq"), w)
                pe.wait_ge(gmv_norm, l + 1)
                pe.wait_ge(par_in, 16 * (l + 1))
                for c in range(GMC):
                    key = (l, "spatial", c)
                    free_bank(key)
                    for t in range(nt):
                        last = pe.matmul(bank_of(key)[:, t * P:(t + 1) * P], gv[:, t, c * P:(c + 1) * P],
                                         par_of("gm_ws", c * P, (c + 1) * P), start=True, stop=True)
                    last.then_inc(prod, 1)
                sums((l, "ckv"))
                pe.wait_ge(kr_ready, l + 1)
                pe.matmul(bank[6][tail, 0:SEQ], C("rot", tail), krw[tail, 0, 0:SEQ], start=True,
                          stop=True).then_inc(kr_rot, 1)
                ukv = panels.take().rearrange("p (k n) -> p k n", n=1024)
                pe.wait_ge(scaled, units[(l, "ckv")][0] + 1)
                for hp in range(4):
                    key = (l, "nope", hp)
                    free_bank(key)
                    product(bank_of(key)[:, :], [(ukv[:, k, hp * P:(hp + 1) * P], ckv[:, k, :]) for k in range(2)], prod)
                    for hd in (2 * hp, 2 * hp + 1):
                        sums((l, "k", hd), rows=slice(0, QK))
                for t in range(4):
                    key = (l, "mv", t)
                    free_bank(key)
                    product(bank_of(key)[:, :], [(ckv[:, k, t * P:(t + 1) * P], ukv[:, k, 512:1024]) for k in range(2)],
                            prod)

                def rotate_q(hd):
                    pe.wait_ge(scaled, units[(l, "q", hd)][0] + 1)
                    if hd or l:
                        pe.wait_ge(q_ready, MH * l + hd)
                    pe.matmul(bank[6][tail, 0:SEQ], C("rot", tail), qq[tail, hd, 0:SEQ], start=True,
                              stop=True).then_inc(q_rot, 1)

                pe.wait_ge(krw_ready, l + 1)
                for hd in range(MH):
                    if hd % 4 == 0:
                        uq = panels.take()[:, 0:3 * 4 * QK].rearrange("p (k n) -> p k n", n=4 * QK)
                    key = (l, "uq", hd)
                    free_bank(key)
                    at = (hd % 4) * QK
                    product(bank_of(key)[0:QK, 0:w], [(uq[:, k, at:at + QK], cq[:, k, 0:w]) for k in range(3)], prod)
                    sums((l, "q", hd), w, slice(0, QK))
                    if hd:
                        rotate_q(hd - 1)
                rotate_q(MH - 1)

                a0 = ATT[l]
                pe.wait_ge(drained["a"], count_after(number[(l, "uq", MH - 1)], "a"))
                pe.wait_ge(roots, units[(l, "q", MH - 1)][0] + 1)
                pe.wait_ge(q_ready, MH * (l + 1))
                pe.wait_ge(k_ready, MH * (l + 1))
                na = nt * MH
                for i in range(na + 2):
                    if i < na:
                        a = a0 + i
                        t, hd = divmod(i, MH)
                        keys = slice(0, T) if t < 2 else slice(CTX, T)
                        if a >= 2:
                            pe.wait_ge(att_exp, a - 1)
                        pe.matmul(bank[a % 2][:, 0:keys.stop - keys.start], qq[0:QK, hd, t * P:(t + 1) * P],
                                  kk[0:QK, hd, keys], start=True, stop=True).then_inc(att_s, 1)
                    if 0 < i <= na:
                        a = a0 + i - 1
                        nk = 4 if (i - 1) // MH < 2 else 2
                        pe.wait_ge(att_p, a + 1)
                        if a >= 2:
                            pe.wait_ge(att_pt, a - 1)
                        for n in range(nk):
                            last = pe.transpose(bank[2 + a % 2][:, n * P:(n + 1) * P], pr[:, a % 2, n * P:(n + 1) * P],
                                                ident)
                        last.then_inc(att_t, 1)
                    if i > 1:
                        a = a0 + i - 2
                        t, hd = divmod(i - 2, MH)
                        nk, k0 = (4, 0) if t < 2 else (2, 2)
                        pe.wait_ge(att_pt, a + 1)
                        if a >= 2:
                            pe.wait_ge(att_y, a - 1)
                        rows = slice(NOPE * (hd % 2), NOPE * (hd % 2) + NOPE)
                        for n in range(nk):
                            last = pe.matmul(bank[4 + a % 2][rows, 0:P], vm[:, k0 + n, hd * 64:hd * 64 + 64],
                                             prT[:, a % 2, n * P:(n + 1) * P], start=n == 0, stop=n == nk - 1)
                        last.then_inc(att_o, 1)

                pe.wait_ge(att_pt, a0 + na)
                pe.wait_ge(att_y, a0 + na)

                def turn(i, src):
                    if 8 * l + i:
                        pe.wait_ge(tok_c, 8 * l + i)
                    for t in range(4):
                        last = pe.transpose(bank[6][:, t * P:(t + 1) * P], src[:, t * P:(t + 1) * P], ident)
                    last.then_inc(tok_t, 1)

                for p in range(6):
                    std([(l, "qkv", 2 * p), (l, "qkv", 2 * p + 1)], T, uT, None, 0)
                for i in range(4):
                    pe.wait_ge(conv_silu, 12 * l + 9 + i)
                    turn(i, vT[:, i % 2, :])
                for i in range(8):
                    sums((l, "qk", i))
                    if 1 <= i <= 4:
                        pe.wait_ge(scaled, units[(l, "qk", i - 1)][0] + 1)
                        turn(3 + i, kT[:, i - 1, :])

                pe.wait_ge(scaled, units[(l, "qk", 7)][0] + 1)
                pe.wait_ge(tok_c, 8 * (l + 1))
                pe.wait_ge(g_ready, l + 1)
                for j in range(4):
                    it = l * 4 + j
                    tiles = [ORDER[d][j] for d in range(2)]

                    def each(what, d):
                        for hd in range(HEADS):
                            last = what(hd, slice(hd * P, (hd + 1) * P), slice(tiles[d] * P, (tiles[d] + 1) * P))
                        last.then_inc(dpe[d], 1)

                    def mm(out, lhsT, rhs, start=True, stop=True):
                        return pe.matmul(out, lhsT, rhs, start=start, stop=stop)

                    for d in range(2):
                        pe.wait_ge(ddve[d], it * D_DVE + 1)
                        mm(bank[6][:, 4 * d:4 * d + 4], C("upto" if d == 0 else "from"),
                           g[:, tiles[d], 4 * d:4 * d + 4])
                    for d in range(2):
                        A, upto = bank[3 * d], C("upto" if d == 0 else "from")
                        each(lambda hd, c, t: mm(A[:, c], gB[:, d, c], upto), d)
                    for d in range(2):
                        B, K = bank[3 * d + 1], bank[3 * d + 2]

                        def both(hd, c, t):
                            mm(B[:, c], kT[:, hd, t], kT[:, hd, t])
                            return mm(K[:, c], kT[:, hd, t], qT[:, hd, t])
                        each(both, d)
                    for d in range(2):
                        pe.wait_ge(ddve[d], it * D_DVE + 6)
                        pe.wait_ge(dact[d], it * D_ACT + 2)
                        each(lambda hd, c, t: pe.transpose(bank[3 * d][:, c], XT[:, d, c], ident), d)
                    for n in range(1, LEVELS):
                        level = E if n % 2 else ml
                        for d in range(2):
                            pe.wait_ge(dpool[d], it * D_POOL + 2 + n)
                            if n == 1:
                                pe.wait_ge(dact[d], it * D_ACT + 4)
                            else:
                                pe.wait_ge(ddve[d], it * D_DVE + 7 + n)
                            each(lambda hd, c, t: mm(bank[3 * d][:, c], level[:, d, c], X[:, d, c]), d)
                        for d in range(2):
                            pe.wait_ge(dact[d], it * D_ACT + 4 + n)

                            def step_z(hd, c, t):
                                if n < LEVELS - 1:
                                    mm(bank[3 * d + 1][:, c], XT[:, d, c], Y[:, d, c])
                                return mm(bank[3 * d + 2][:, c], Y[:, d, c], XT[:, d, c])
                            each(step_z, d)
                    for d in range(2):
                        pe.wait_ge(ddve[d], it * D_DVE + 14)
                        each(lambda hd, c, t: mm(bank[3 * d][:, c], kg[:, d, c], XT[:, d, c]), d)
                    for d in range(2):
                        pe.wait_ge(dact[d], it * D_ACT + 11)

                        def fresh(hd, c, t):
                            last = mm(bank[3 * d + 1][:, c], XT[:, d, c], vtok[:, tiles[d], c], stop=j == 0)
                            if j:
                                last = mm(bank[3 * d + 1][:, c], nwT[:, d, c], S[:, d, c], start=False)
                            return last
                        each(fresh, d)
                    for d in range(2):
                        pe.wait_ge(ddve[d], it * D_DVE + 15)

                        def outs(hd, c, t):
                            last = None
                            if tiles[d] < nt:
                                if j:
                                    mm(bank[3 * d][:, c], S[:, d, c], EG[:, d, c], stop=False)
                                last = mm(bank[3 * d][:, c], vnew[:, d, c], att[:, d, c], start=j == 0)
                            if j < 3:
                                last = mm(bank[3 * d + 2][:, c], kd[:, d, c], vnew[:, d, c])
                            return last
                        each(outs, d)

                for d in range(2):
                    pe.wait_ge(ddve[d], (l * 4 + 4) * D_DVE)
                for c in range(4):
                    sums((l, "o", c), w)
                for p in range(2):
                    std([(l, "z", 2 * p), (l, "z", 2 * p + 1)], w, uT, None, 0)

                if l + 1 < DEPTH:
                    pe.wait_ge(mods_ready, 2 * l + 2)
                pe.wait_ge(ya_ready, l + 1)
                pe.wait_ge(yb_ready, l + 1)
                for gq in range(4):
                    for b in range(3):
                        std([(l, "gate", 2 * gq + c, b) for c in range(2)], w, uT, None, 0)
                    for b, src in enumerate((ya, yb, yc)):
                        if b != 1:
                            panel = units_of(panels.take())
                        for c in range(2):
                            key = (l, "branch", 2 * gq + c, b)
                            free_bank(key)
                            product(bank_of(key)[:, 0:w],
                                    [(panel[:, k + 4 * (b == 1), c * P:(c + 1) * P], src[:, k, 0:w]) for k in range(4)],
                                    prod)
                    if l + 1 < DEPTH:
                        for p in range(3 * gq, 3 * gq + 3 + (gq == 3)):
                            ada(l + 1, p)
                for p in range(4):
                    std([(l, "out", 2 * p), (l, "out", 2 * p + 1)], w, mT, m_ready if p == 0 else None, DC * l)
                sums((l, "norm", 2), w)
                ffn(l, 1, w, l + 1 if l + 1 < DEPTH else None, (3 * l + 2) * DC)

        @block.vector
        def _(dve):
            step = Steps(dve, dve_step)
            tt, ts, stt = dve.tensor_tensor, dve.tensor_scalar, dve.scalar_tensor_tensor

            def reciprocal_root(key, w=T, rows=slice(0, P)):
                n = units[key][0]
                r = rt[rows, n % 2, 0:w]
                dve.wait_ge(roots, n + 1)
                step(dve.reciprocal(r, r))
                step.wait()
                return r

            def norm(l, i, w):
                n = units[(l, "norm", i)][0]
                r = reciprocal_root((l, "norm", i), w)
                for k in range(DC):
                    last = tt(uT[:, k, 0:w], h[:, k, 0:w], r, ALU.mult)
                    last.then_inc(normed if k < DC - 1 else scaled, 1)

            def modulations(l, part):
                a, b = (0, 24) if part == 0 else (24, 72)
                dve.wait_ge(ada_done, ADA_PANELS * l + (ADA_FIRST if part == 0 else ADA_PANELS))
                step(tt(mods[:, l, a:b, :], bank[7][:, 2 * a:2 * b].rearrange("p (c s) -> p c s", s=2),
                        mod_par[:, l, a:b].unsqueeze(2).to_broadcast([P, b - a, 2]), ALU.add))
                step.wait()
                for i in ((0,) if part == 0 else (1, 2)):
                    c = (3 * i + 1) * DC
                    step(stt(scales[:, l, i, :, :], mods[:, l, c:c + DC, :], 1.0,
                             mod_par[:, l, 72 + i * DC:72 + (i + 1) * DC].unsqueeze(2).to_broadcast([P, DC, 2]),
                             ALU.add, ALU.mult))
                c = (2 if part == 0 else 8) * DC
                step(ts(mods[:, l, c:c + DC, :], mods[:, l, c:c + DC, :], 0.5, None, ALU.mult))
                step.wait()
                dve.sem_inc(mods_ready, 1)

            def residual(key, l, i, j, w):
                wait_product(dve, key)
                for s, cols in halves(w):
                    last = stt(h[:, j, cols], bank_of(key)[:, cols], mods[:, l, (3 * i + 2) * DC + j, s:s + 1],
                               h[:, j, cols], ALU.mult, ALU.add)
                last.then_inc(drained["v"], 1)

            def ffn(l, f, w):
                q0 = number[(l, "g", f, 0)]
                a0 = counts["a"][q0]

                def pair(i, per):
                    for c in range(2):
                        dve.wait_ge(prod, q0 + 4 * i + 3 + c + 4 * per)
                        dve.wait_ge(drained["a"], a0 + 2 * i + c + 1 + 2 * per)
                        if isinstance(per, int):
                            dst = hidden[:, 2 * i + c, 0:w]
                        else:
                            at = per * (2 * T) + (2 * i + c) * T
                            dst = work[:, bass.ds(at, w)]
                        tt(dst, sg[:, 2 * (i % 2) + c, 0:w], bank[(q0 + 2 + c) % 4][:, 0:w],
                           ALU.mult).then_inc(drained["v"], 1)

                pair(0, 0)
                pair(1, 0)
                with dve.Fori(0, 4) as r:
                    pair(2, r * 2)
                    pair(3, r * 2)
                pair(10, 0)
                for j in range(DC):
                    residual((l, "down", f, j), l, 0 if f == 0 else 2, j, w)

            def rope(dst, source, at, out_sem):
                tmp = rsin[tail, at, 0:SEQ]
                step(tt(tmp, source, C("sin", tail), ALU.mult))
                step(tt(dst, dst, C("cos", tail), ALU.mult))
                step.wait()
                return tt(dst, dst, tmp, ALU.add).then_inc(out_sem, 1)

            dve.wait_ge(inputs_in, 16 * (DC + 3))
            modulations(0, 0)
            for l in range(DEPTH):
                w = width(l)
                nt = w // P
                norm(l, 0, T)
                ffn(l, 0, T)
                modulations(l, 1)
                norm(l, 1, T)

                dve.wait_ge(par_in, 16 * (l + 1))
                for t in range(nt):
                    wait_drained(dve, (l, "gmv", 1, t))
                    step(dve.bn_stats(stats, gv[:, t, :]))
                    step.wait()
                    step(dve.bn_aggr(mv[:, t, :], stats))
                    step.wait()
                dve.sem_inc(gmv_var, 1)
                dve.wait_ge(gmv_root, l + 1)
                step(dve.reciprocal(lnr[:, 0:nt], lnr[:, 0:nt]))
                step.wait()
                for t in range(nt):
                    last = ts(gv[:, t, :], gv[:, t, :], mv[:, t, 0:1], lnr[:, t:t + 1], ALU.subtract, ALU.mult)
                last.then_inc(gmv_norm, 1)

                wait_drained(dve, (l, "krope"))
                stt_w = par_of("qk_k", rows=tail)
                ts(krw[tail, 0, :], kr[tail, 0, :], stt_w, None, ALU.mult).then_inc(kr_ready, 1)
                wait_product(dve, (l, "ab"))
                step(dve.tensor_copy(gab, bank_of((l, "ab"))[:, 0:64].rearrange("p (t c) -> p t c", c=16)))
                step.wait()
                dve.sem_inc(drained["v"], 1)
                step(tt(gab[:, :, 0:8], gab[:, :, 0:8], par_of("dt_bias").unsqueeze(1).to_broadcast([P, 4, 8]), ALU.add))
                step.wait()
                step(ts(t1, gab[:, :, 0:8], -1.0, None, ALU.mult))
                step.wait()
                tt(t1, t1, gab[:, :, 0:8], ALU.max).then_inc(dt_ready, 1)

                r = reciprocal_root((l, "cq"), w)
                for i in range(3):
                    last = stt(cq[:, i, 0:w], cq[:, i, 0:w], par_of("q_norm", i, i + 1), r, ALU.mult, ALU.mult)
                last.then_inc(scaled, 1)
                for c in range(GMC):
                    key = (l, "spatial", c)
                    wait_product(dve, key)
                    bias = par_of("gm_bs", c * P, (c + 1) * P).unsqueeze(1).to_broadcast([P, nt, P])
                    stt(gtmp[:, c % 2, 0:w].rearrange("p (t c) -> p t c", c=P),
                        bank_of(key)[:, 0:w].rearrange("p (t c) -> p t c", c=P),
                        par_of("gm_ln", c, c + 1), bias, ALU.mult, ALU.add).then_inc(drained["v"], 1)
                    wait_drained(dve, key)
                    step(tt(ya[:, c, 0:w], gtmp[:, c % 2, 0:w], ya[:, c, 0:w], ALU.mult))
                    step.wait()
                dve.sem_inc(ya_ready, 1)
                r = reciprocal_root((l, "ckv"))
                for i in range(2):
                    last = stt(ckv[:, i, :], ckv[:, i, :], par_of("kv_norm", i, i + 1), r, ALU.mult, ALU.mult)
                last.then_inc(scaled, 1)
                dve.wait_ge(kr_rot, l + 1)
                dve.wait_ge(kr_ready, l + 1)
                rope(krw[tail, 0, 0:SEQ], bank[6][tail, 0:SEQ], 0, krw_ready)
                dve.wait_ge(krw_ready, l + 1)
                for hd in range(MH):
                    r = reciprocal_root((l, "k", hd), rows=slice(0, QK))
                    stt(kk[0:NOPE, hd, :], kk[0:NOPE, hd, :], par_of("qk_k", rows=slice(0, NOPE)), r[0:NOPE, :],
                        ALU.mult, ALU.mult).then_inc(k_ready, 1)
                    tt(kk[tail, hd, :], krw[tail, 0, :], r[tail, :], ALU.mult).then_inc(scaled, 1)
                for hd in range(MH):
                    r = reciprocal_root((l, "q", hd), w, slice(0, QK))
                    stt(qq[0:QK, hd, 0:w], qq[0:QK, hd, 0:w], par_of("qk_q", rows=slice(0, QK)), r,
                        ALU.mult, ALU.mult).then_inc(scaled, 1)
                    dve.wait_ge(scaled, units[(l, "q", hd)][0] + 1)
                    dve.wait_ge(q_rot, MH * l + hd + 1)
                    rope(qq[tail, hd, 0:SEQ], bank[6][tail, 0:SEQ], hd % 2, q_ready)

                a0 = ATT[l]
                for i in range(nt * MH + 2):
                    if i < nt * MH:
                        a = a0 + i
                        s = a % 2
                        keys = slice(0, T) if i // MH < 2 else slice(0, CTX)
                        dve.wait_ge(att_s, a + 1)
                        if a >= 2:
                            dve.wait_ge(att_exp, a - 1)
                        step(dve.reduce_max(mx[:, s:s + 1], bank[s][:, keys], AX.X))
                        step.wait()
                        ts(nb[:, s:s + 1], mx[:, s:s + 1], -QK ** -0.5, None, ALU.mult).then_inc(att_max, 1)
                    if 0 < i <= nt * MH:
                        a = a0 + i - 1
                        s = a % 2
                        keys = slice(0, T) if (i - 1) // MH < 2 else slice(0, CTX)
                        dve.wait_ge(att_exp, a + 1)
                        step(dve.reciprocal(ri[:, s:s + 1], rs[:, s:s + 1]))
                        step.wait()
                        ts(pr[:, s, keys], pr[:, s, keys], ri[:, s:s + 1], None, ALU.mult).then_inc(att_p, 1)
                    if i > 1:
                        a = a0 + i - 2
                        t, hd = divmod(i - 2, MH)
                        rows = slice(NOPE * (hd % 2), NOPE * (hd % 2) + NOPE)
                        dve.wait_ge(att_o, a + 1)
                        dve.tensor_copy(yc[rows, hd // 2, t * P:(t + 1) * P], bank[4 + a % 2][rows, 0:P]).then_inc(att_y, 1)

                dve.wait_ge(dt_ln, l + 1)
                step(stt(g, gab[:, :, 0:8], 0.0, t1, ALU.max, ALU.add))
                step(ts(beta, beta, 1.0, None, ALU.add))
                step.wait()
                step(stt(g, g, -1.0, expa.unsqueeze(1).to_broadcast([P, 4, 8]), ALU.mult, ALU.mult))
                step(dve.reciprocal(beta, beta))
                step.wait()
                dve.sem_inc(g_ready, 1)

                dve.wait_ge(pads, l + 1)
                for c in range(12):
                    wait_drained(dve, (l, "qkv", c))
                    if 12 * l + c >= 2:
                        dve.wait_ge(conv_silu, 12 * l + c - 1)
                    a = acc[:, c % 2, :].rearrange("p (s w) -> p s w", s=2)
                    for tap in range(5):
                        src = convin[:, c % 3, :, tap:tap + SEQ]
                        wt = par_of("conv", 5 * c + tap, 5 * c + tap + 1)
                        if tap == 0:
                            step(ts(a, src, wt, None, ALU.mult))
                        elif tap < 4:
                            step(stt(a, src, wt, a, ALU.mult, ALU.add))
                        else:
                            stt(a, src, wt, a, ALU.mult, ALU.add).then_inc(conv_done, 1)
                        if tap < 4:
                            step.wait()
                for i in range(8):
                    r = reciprocal_root((l, "qk", i))
                    if i < 4:
                        tt(kT[:, i, :], kT[:, i, :], r, ALU.mult).then_inc(scaled, 1)
                    else:
                        stt(qT[:, i - 4, :], qT[:, i - 4, :], float(P) ** -0.5, r, ALU.mult, ALU.mult).then_inc(scaled, 1)
                dve.wait_ge(scaled, units[(l, "qk", 7)][0] + 1)
                dve.wait_ge(tok_c, 8 * (l + 1))

                def per_head(x):
                    return x.unsqueeze(2).to_broadcast([P, HEADS, P])

                for j in range(4):
                    it = l * 4 + j
                    tiles = [ORDER[d][j] for d in range(2)]
                    for d in range(2):
                        dve.wait_ge(ddve[d], it * D_DVE) if it else None
                        dve.tensor_copy(heads(gB[:, d, :]), per_head(g[:, tiles[d], 4 * d:4 * d + 4])).then_inc(ddve[d], 1)
                    for d in range(2):
                        A = heads(bank[3 * d][:, :])
                        end = P - 1 if d == 0 else 0
                        dve.wait_ge(dpe[d], it * D_PE + 1)
                        step(dve.tensor_copy(gamc[:, d, :], bank[6][:, 4 * d:4 * d + 4]))
                        step.wait()
                        step(tt(heads(E[:, d, :]), A, per_head(gamc[:, d, :]), ALU.subtract))
                        step(tt(kds[:, d, :], A[:, :, end], gamc[:, d, :], ALU.subtract))
                        step.wait()
                        ts(E[:, d, :], E[:, d, :], 0.0, None, ALU.min).then_inc(ddve[d], 1)
                        dve.wait_ge(ddve[d], it * D_DVE + 2)
                        dve.sem_inc(ddve[d], 1)
                    for d in range(2):
                        dve.wait_ge(dpe[d], it * D_PE + 2)
                        dve.wait_ge(dpool[d], it * D_POOL + 1)
                        tt(att[:, d, :], bank[3 * d + 2][:, :], E[:, d, :], ALU.mult).then_inc(ddve[d], 1)
                        step(tt(mt[:, d, :], bank[3 * d + 1][:, :], E[:, d, :], ALU.mult))
                        step.wait()
                        tt(heads(mt[:, d, :]), heads(mt[:, d, :]), per_head(beta[:, tiles[d], 4 * d:4 * d + 4]),
                           ALU.mult).then_inc(ddve[d], 1)
                    for d in range(2):
                        dve.wait_ge(dpool[d], it * D_POOL + 2)
                        tt(heads(XT[:, d, :]), ident.unsqueeze(1).to_broadcast([P, HEADS, P]), heads(ml[:, d, :]),
                           ALU.subtract).then_inc(ddve[d], 1)
                    for d in range(2):
                        end = P - 1 if d == 0 else 0
                        qs = qT[:, :, tiles[d] * P:(tiles[d] + 1) * P]
                        dve.wait_ge(dact[d], it * D_ACT + 3)
                        step(dve.tensor_copy(eL[:, d, :], heads(EG[:, d, :])[:, :, end]))
                        step.wait()
                        tt(heads(EG[:, d, :]), heads(EG[:, d, :]), qs, ALU.mult).then_inc(ddve[d], 1)
                        tt(heads(kg[:, d, :]), heads(ktok[:, tiles[d], :]), per_head(egam[:, d, :]),
                           ALU.mult).then_inc(ddve[d], 1)
                    for n in range(1, LEVELS):
                        for d in range(2):
                            dve.wait_ge(dpe[d], it * D_PE + 3 + 2 * n)
                            if n < LEVELS - 1:
                                step(tt(X[:, d, :], X[:, d, :], bank[3 * d + 1][:, :], ALU.subtract))
                            tt(XT[:, d, :], XT[:, d, :], bank[3 * d + 2][:, :], ALU.subtract).then_inc(ddve[d], 1)
                    for d in range(2):
                        step(tt(heads(kd[:, d, :]), heads(ktok[:, tiles[d], :]), per_head(kds[:, d, :]), ALU.mult))
                        dve.wait_ge(dpe[d], it * D_PE + 17)
                        tt(heads(vnew[:, d, :]), heads(bank[3 * d + 1][:, :]),
                           per_head(beta[:, tiles[d], 4 * d:4 * d + 4]), ALU.mult).then_inc(ddve[d], 1)
                    for d in range(2):
                        dve.wait_ge(dpe[d], it * D_PE + 18)
                        t = tiles[d]
                        last = None
                        if t < nt:
                            out = yb[:, :, t * P:(t + 1) * P]
                            o = heads(bank[3 * d][:, :])
                            if j % 2 == 0:
                                last = dve.tensor_copy(out, o)
                            else:
                                last = tt(out, out, o, ALU.add)
                        if j < 3:
                            if last is not None:
                                step(last)
                            if j:
                                step(tt(heads(S[:, d, :]), heads(S[:, d, :]), per_head(eL[:, d, :]), ALU.mult))
                                step.wait()
                                last = tt(S[:, d, :], S[:, d, :], bank[3 * d + 2][:, :], ALU.add)
                            else:
                                last = dve.tensor_copy(S[:, d, :], bank[3 * d + 2][:, :])
                        last.then_inc(ddve[d], 1)
                    for d in range(2):
                        dve.wait_ge(ddve[d], (it + 1) * D_DVE)

                for i in range(4):
                    r = reciprocal_root((l, "o", i), w)
                    stt(yb[:, i, 0:w], yb[:, i, 0:w], par_of("dn_out"), r, ALU.mult, ALU.mult).then_inc(scaled, 1)
                dve.wait_ge(scaled, units[(l, "o", 3)][0] + 1)
                wait_drained(dve, (l, "z", 3))
                tt(yb[:, :, 0:w], yb[:, :, 0:w], zs[:, :, 0:w], ALU.mult).then_inc(yb_ready, 1)

                for pair in range(DC // 2):
                    for b in range(3):
                        for c in range(2):
                            j = 2 * pair + c
                            key = (l, "branch", j, b)
                            wait_product(dve, key)
                            wait_drained(dve, (l, "gate", j, b))
                            m = mT[:, j, 0:w]
                            dst = m if b == 0 else mtmp[:, c, 0:w]
                            tt(dst, sig[:, 2 * b + c, 0:w], bank_of(key)[:, 0:w], ALU.mult).then_inc(drained["v"], 1)
                            if b:
                                wait_drained(dve, key)
                                last = tt(m, m, mtmp[:, c, 0:w], ALU.add)
                                if b == 1:
                                    step(last)
                                    step.wait()
                                else:
                                    last.then_inc(m_ready, 1)
                if l + 1 < DEPTH:
                    modulations(l + 1, 0)
                for j in range(DC):
                    residual((l, "out", j), l, 1, j, w)
                norm(l, 2, w)
                ffn(l, 1, w)


_NAMES = ("wts", "par", "cst", "mod", "x", "c")


def kernel(**inputs):
    import concourse.bacc as bacc
    from concourse.bass_utils import run_bass_kernel_spmd

    inp = {k: np.asarray(v) for k, v in inputs.items()}
    arrays = {
        "wts": stream(inp),
        "par": params(inp),
        "cst": constants(),
        "mod": np.ascontiguousarray(modulation_params(inp)),
        "x": np.ascontiguousarray(np.concatenate([inp["x"][0].T, inp["ctx"][0].T], axis=1)),
        "c": np.ascontiguousarray(np.stack([inp["c"][0], inp["c_ctx"]], axis=-1).reshape(DC, P, 2).transpose(1, 0, 2)),
    }
    nc = bacc.Bacc("TRN2", target_bir_lowering=False, num_devices=1)
    args = [nc.dram_tensor("in_" + n, arrays[n].shape, F32, kind="ExternalInput").ap() for n in _NAMES]
    args.append(nc.dram_tensor("out", (D, SEQ), F32, kind="ExternalOutput").ap())
    backbone(nc, *args)
    r = run_bass_kernel_spmd(nc, [{"in_" + n: arrays[n] for n in _NAMES}], core_ids=[0])
    return np.asarray(r.results[0]["out"]).T.reshape(1, SEQ, D)
```

```python
from contextlib import ExitStack

import numpy as np

import concourse.bass as bass
from concourse import mybir

F32 = mybir.dt.float32
F32R = mybir.dt.float32r
ACT = mybir.ActivationFunctionType
ALU = mybir.AluOpType
AX = mybir.AxisListType

P = 128
D = 1024
DC = D // P
SEQ = 256
CTX = 256
T = SEQ + CTX
DEPTH = 2
FFN = 2816
FC = FFN // P
EPS = 1e-6
GMW = 512
GMC = GMW // P
HEADS = 4
MH = 8
NOPE = 64
ROPE = 32
QK = NOPE + ROPE
LQ = 384
LKV = 256
GRID_W = 64
LEVELS = 7
UNIT = 256
PANEL = 8 * UNIT
RING = 3
HALF = PANEL // 2
HALVES = 3
ADA_FIRST = 13
ADA_PANELS = 36

PAR = {}
_at = 0
for _name, _n in (("gm_ln", 4), ("conv", 60),
                  ("dn_out", 1), ("q_norm", 3), ("kv_norm", 2), ("qk_q", 1), ("qk_k", 1),
                  ("dt_bias", 8), ("a_log", 8), ("gm_bs", 512), ("gm_ws", 512)):
    PAR[_name] = (_at, _n)
    _at += _n
NPAR = _at
CST = {}
_at = 0
for _name, _n in (("ident", 128), ("upto", 128), ("from", 128), ("ones", 128), ("level", LEVELS * 128),
                  ("cos", 256), ("sin", 256), ("rot", 32), ("fold", 2), ("pick", 63)):
    CST[_name] = (_at, _n)
    _at += _n
NCST = _at


def constants():
    c = np.zeros((P, NCST), np.float32)

    def put(name, a, rows=slice(0, P)):
        at, n = CST[name]
        c[rows, at:at + n] = a.reshape(a.shape[0], n)

    i = np.arange(P)
    put("ident", np.eye(P, dtype=np.float32))
    put("upto", (i[:, None] <= i[None, :]).astype(np.float32))
    put("from", (i[:, None] >= i[None, :]).astype(np.float32))
    put("ones", np.ones((P, P), np.float32))
    lev = np.zeros((P, LEVELS, P), np.float32)
    for n in range(LEVELS):
        b = 1 << n
        lev[:, n, :] = (i[:, None] // (2 * b) == i[None, :] // (2 * b)) & (i[:, None] // b != i[None, :] // b)
    put("level", lev)
    pos = np.arange(SEQ)
    half = ROPE // 2
    freq = (1.0 / (np.float32(10000.0) ** (np.arange(0, half, 2, dtype=np.float32) / np.float32(half)))).astype(np.float32)
    row = (pos // GRID_W).astype(np.float32)[:, None] * freq
    col = (pos % GRID_W).astype(np.float32)[:, None] * freq
    ang = np.concatenate([row, row, col, col], axis=-1)
    tail = slice(NOPE, QK)
    put("cos", np.cos(ang).astype(np.float32).T, tail)
    put("sin", np.sin(ang).astype(np.float32).T, tail)
    rot = np.zeros((ROPE, ROPE), np.float32)
    q = half // 2
    for base in (0, half):
        for m in range(q):
            rot[base + q + m, base + m] = -1.0
            rot[base + m, base + q + m] = 1.0
    put("rot", rot, tail)
    pick = np.zeros((P, 63), np.float32)
    pick[:, 31] = 1.0
    put("pick", pick)
    put("fold", np.concatenate([np.eye(2), np.eye(2)]).astype(np.float32), slice(0, 4))
    return c


def stream(inp):
    out = []

    def rows(w, cols):
        w = w[:, cols] if not isinstance(cols, slice) else w[:, cols]
        return w.reshape(w.shape[0] // P, P, w.shape[1]).transpose(1, 0, 2)

    def put(*parts):
        panel = np.zeros((P, PANEL), np.float32)
        at = 0
        for part in parts:
            flat = part.reshape(P, -1)
            panel[:, at:at + flat.shape[1]] = flat
            at += flat.shape[1]
        out.append(panel)

    def std(w, c0):
        put(rows(w, slice(c0, c0 + UNIT)))

    def ada(l, p):
        std(inp["ada_w"][l], p * UNIT)

    def ffn(l, f, carry):
        gu, down = inp[f"ffn{f + 1}_w_gu"][l], inp[f"ffn{f + 1}_w_down"][l]
        a = ADA_FIRST
        for i in range(FC // 2):
            std(gu, i * UNIT)
            std(gu, FFN + i * UNIT)
            if carry is not None:
                ada(carry, a)
                a += 1
        for g in range(4):
            w = rows(down, slice(g * UNIT, (g + 1) * UNIT))
            for s in range(3):
                put(w[:, 8 * s:8 * s + 8])
                if carry is not None:
                    ada(carry, a)
                    a += 1
        assert carry is None or a == ADA_PANELS

    for p in range(ADA_FIRST):
        ada(0, p)
    for l in range(DEPTH):
        ffn(l, 0, 0 if l == 0 else None)
        w = inp["w_in"][l]
        for i in range(4):
            std(w, i * UNIT)
        o = 2 * GMW + 4 * 512 + 16
        ab, cq, ckv = 2 * GMW + 4 * 512, o, o + LQ
        gates = ckv + LKV + ROPE
        put(rows(w, slice(cq, cq + 256)))
        put(rows(w, np.r_[cq + 256:cq + 384, ckv:ckv + 128]))
        last = np.zeros((D, UNIT), np.float32)
        last[:, 0:128] = w[:, ckv + 128:ckv + 256]
        last[:, 128:128 + ROPE] = w[:, ckv + 256:ckv + 256 + ROPE]
        last[:, 128 + ROPE:128 + ROPE + 16] = w[:, ab:ab + 16]
        put(rows(last, slice(0, UNIT)))
        uq, ukv = inp["mla_w_uq"][l], inp["mla_w_ukv"][l]
        h = np.arange(MH)[:, None] * 128
        put(rows(ukv, np.concatenate([(h + np.arange(64)).ravel(), (h + 64 + np.arange(64)).ravel()])))
        put(rows(uq, slice(0, 4 * QK)))
        put(rows(uq, slice(4 * QK, 8 * QK)))
        for i in range(6):
            std(w, 2 * GMW + i * UNIT)
        for i in range(2):
            std(w, 2 * GMW + 1536 + i * UNIT)
        for g in range(4):
            cols = slice(g * UNIT, (g + 1) * UNIT)
            for b in range(3):
                std(w, gates + b * D + g * UNIT)
                if l + 1 < DEPTH:
                    ada(l + 1, 3 * g + b)
            put(rows(inp["w_branch_gm"][l], cols), rows(inp["w_branch_dn"][l], cols))
            put(rows(inp["w_branch_mla"][l], cols))
            if g == 3 and l + 1 < DEPTH:
                ada(l + 1, 12)
        for g in range(4):
            std(inp["w_out"][l], g * UNIT)
        ffn(l, 1, l + 1 if l + 1 < DEPTH else None)
    return np.stack(out)


def params(inp):
    out = np.zeros((P, DEPTH, NPAR), np.float32)

    def feat(v):
        return v.reshape(-1, P).T

    for l in range(DEPTH):
        def put(name, a, rows=slice(0, P)):
            at, n = PAR[name]
            out[rows, l, at:at + n] = a.reshape(a.shape[0], n)

        put("gm_ln", feat(inp["gm_ln"][l]))
        put("conv", inp["dn_conv"][l].reshape(5, 12, P).transpose(2, 1, 0))
        put("dn_out", feat(inp["dn_out_norm"][l]))
        put("q_norm", feat(inp["mla_q_norm"][l]))
        put("kv_norm", feat(inp["mla_kv_norm"][l]))
        put("qk_q", inp["mla_qk_norm_q"][l][:, None], slice(0, QK))
        put("qk_k", inp["mla_qk_norm_k"][l][:, None], slice(0, QK))
        put("dt_bias", np.broadcast_to(inp["dn_dt_bias"][l].reshape(1, 8), (P, 8)))
        put("a_log", np.broadcast_to(inp["dn_a_log"][l].reshape(1, 8), (P, 8)))
        put("gm_bs", np.broadcast_to(inp["gm_bs"][l].reshape(1, 512), (P, 512)))
        put("gm_ws", inp["gm_ws"][l].transpose(2, 0, 1))
    return out.reshape(P, DEPTH * NPAR)


def modulation_params(inp):
    both = [np.concatenate([inp["ada_b"][l], inp["ffn1_norm"][l], inp["mix_norm"][l], inp["ffn2_norm"][l]])
            for l in range(DEPTH)]
    return np.stack(both).reshape(DEPTH, 96, P).transpose(2, 0, 1)


def panel_kinds():
    out, start = ["k"] * ADA_FIRST, {}

    def ffn(l, f, carry):
        start[l, "gu", f] = len(out)
        for _ in range(FC // 2):
            out.extend(["c", "c"] + ["k"] * carry)
        start[l, "down", f] = len(out)
        for _ in range(4):
            out.extend((["c"] + ["k"] * carry) * 3)

    for l in range(DEPTH):
        more = l + 1 < DEPTH
        ffn(l, 0, l == 0)
        for stage, kinds in (("gmu", "cc"), ("gmv", "kk"), ("low", "ccc"), ("ukv", "r"), ("uq", "rr"),
                             ("qkv", "cccccc"), ("z", "cc")):
            start[l, stage] = len(out)
            out.extend({"r": "raw"}.get(k, k) for k in kinds)
        for g in range(4):
            start[l, "merge", g] = len(out)
            out.extend((["c"] + ["k"] * more) * 3 + ["raw"] * 2 + ["k"] * ((g == 3) * more))
        start[l, "out"] = len(out)
        out.extend(["c"] * 4)
        ffn(l, 1, more)
    return out, start


KINDS, START = panel_kinds()
N_PANELS = ADA_FIRST + (22 + 12) * 4 + 23 * 2 + DEPTH * (4 + 3 + 1 + 2 + 8 + 20 + 4) + ADA_FIRST


def product_owners():
    number, owner = {}, []

    def add(key, who):
        number[key] = len(owner)
        owner.append(who)

    for l in range(DEPTH):
        nt = 4 if l + 1 < DEPTH else 2
        for f in range(2):
            if f == 1:
                for c in range(GMC):
                    add((l, "gmu", c), "a")
                for p in range(2):
                    for t in range(nt):
                        add((l, "gmv", p, t), "a")
                for c in range(3):
                    add((l, "cq", c), "a")
                for c in range(2):
                    add((l, "ckv", c), "a")
                add((l, "krope"), "a")
                for c in range(GMC):
                    add((l, "spatial", c), "v")
                for c in range(4):
                    add((l, "nope", c), "a")
                for t in range(4):
                    add((l, "mv", t), "a")
                for h in range(MH):
                    add((l, "uq", h), "a")
                for kind in ("k_spread", "q_spread"):
                    for h in range(MH):
                        add((l, kind, h), "v")
                for c in range(12):
                    add((l, "qkv", c), "a")
                for c in range(4):
                    add((l, "z", c), "a")
                for pair in range(DC // 2):
                    for kind, who in (("gate", "a"), ("branch", "v")):
                        for b in range(3):
                            for j in (2 * pair, 2 * pair + 1):
                                add((l, kind, j, b), who)
                for j in range(DC):
                    add((l, "out", j), "v")
            for i in range(FC // 2):
                for c in (2 * i, 2 * i + 1):
                    add((l, "g", f, c), "a")
                for c in (2 * i, 2 * i + 1):
                    add((l, "u", f, c), "v")
            for j in range(DC):
                add((l, "down", f, j), "v")
    counts = {"a": [0], "v": [0]}
    for who in owner:
        for k in "av":
            counts[k].append(counts[k][-1] + (who == k))
    return number, owner, counts


def backbone(nc, wts, par_d, cst_d, mod_d, x_d, c_d, out_d, dbg=None):
    number, owner, counts = product_owners()
    assert len(KINDS) == N_PANELS
    split_before = np.cumsum([0] + [k != "raw" for k in KINDS]).tolist()
    with ExitStack() as ctx:
        def sb(name, shape, dt=F32):
            return ctx.enter_context(nc.sbuf_tensor(name, shape, dt))

        def sem(name):
            return ctx.enter_context(nc.semaphore(name))

        ring = sb("ring", [P, RING * PANEL])
        w_hi = sb("w_hi", [P, HALVES, HALF], F32R)
        w_lo = sb("w_lo", [P, HALVES, HALF], F32R)
        h = sb("h", [P, DC, T])
        u_hi = sb("u_hi", [P, DC, T], F32R)
        u_lo = sb("u_lo", [P, DC, T], F32R)
        sq = sb("sq", [P, 4, T])
        rt = sb("rt", [P, 2, T])
        par = sb("par", [P, NPAR])
        cst = sb("cst", [P, NCST])
        cond = sb("cond", [P, DC, 2])
        c4 = sb("c4", [P, DC, 4], F32R)
        ada_rows = sb("ada_rows", [4, 2, UNIT])
        mod_par = sb("mod_par", [P, DEPTH, 96])
        mods = sb("mods", [P, DEPTH, 72, 2])
        scales = sb("scales", [P, DEPTH, 3, DC, 2])
        small = sb("small", [P, 256])

        SLOT = T * 4
        ARENA = 48 * SLOT
        base = -(-nc.sbuf_base // 32) * 32
        sb("arena", [P, 48 * T])

        def at(name, slot, n, dt=F32):
            return nc.alloc_sbuf_tensor_at(name, [P, n, T], dt, offset=base + slot * SLOT)

        h_hi = at("hidden_hi", 0, FC, F32R)
        h_lo = at("hidden_lo", FC, FC, F32R)
        sg = at("sg", 2 * FC, 2)
        work = nc.alloc_sbuf_tensor_at("work", [P, 36 * T], F32, offset=base)
        ya, yb, yc = at("ya", 36, 4), at("yb", 40, 4), at("yc", 44, 4)
        m_hi = at("m_hi", 0, DC, F32R)
        m_lo = at("m_lo", DC, DC, F32R)

        def view(at, n, w=T):
            return work[:, at * T:at * T + n * w].rearrange("p (n w) -> p n w", w=w)

        gv = view(29, 4)
        gtmp = view(33, 2)
        cq = view(0, 3)
        ckv = view(3, 2)
        kr = view(5, 1)
        krw = view(6, 1)
        rsin = view(7, 2)
        kk = view(9, MH)
        qq = view(9 + MH, MH)
        vm = view(25, 4)
        pr = view(29, 4)
        prT = view(33, 2)
        qT = view(0, 4)
        kT = view(4, 4)
        ktok = view(8, 4)
        vtok = view(12, 4)
        S = view(16, 2)
        E = view(18, 2)
        EG = view(20, 2)
        att = view(22, 2)
        mt = view(24, 2)
        ml = view(26, 2)
        X = view(28, 2)
        XT = view(30, 2)
        Y = view(32, 2)
        gB = view(34, 2)
        vnew, nwT, kd, kg = mt, X, Y, gB
        vT = view(32, 2)
        acc = view(30, 2)
        CONV = 16 * T
        convin = work[:, CONV:CONV + 3 * 520].rearrange("p (n s w) -> p n s w", n=3, s=2)
        sig = view(16, 6)
        macc = view(22, 2)
        mtmp = view(24, 2)
        zs = view(26, 4)

        gab = small[:, 0:64].rearrange("p (t c) -> p t c", c=16)
        g = small[:, 64:96].rearrange("p (t c) -> p t c", c=8)
        beta = small[:, 96:128].rearrange("p (t c) -> p t c", c=8)
        t1 = small[:, 128:160].rearrange("p (t c) -> p t c", c=8)
        expa = small[:, 160:168]
        gamc = small[:, 168:176].rearrange("p (d c) -> p d c", c=4)
        egam = small[:, 176:184].rearrange("p (d c) -> p d c", c=4)
        kds = small[:, 184:192].rearrange("p (d c) -> p d c", c=4)
        mx = small[:, 192:196]
        nb = small[:, 196:200]
        eL = small[:, 220:228].rearrange("p (d c) -> p d c", c=4)
        rs = small[:, 232:236]
        ri = small[:, 236:240]
        stats = small[:, 200:206]
        mv = small[:, 208:216].rearrange("p (t c) -> p t c", c=2)
        lnr = small[:, 216:220]
        eps = small[:, 228:229]

        bank = [ctx.enter_context(nc.psum_tensor(f"bank{i}", [P, 512], F32)) for i in range(8)]

        def C(name, rows=slice(0, P)):
            at, n = CST[name]
            return cst[rows, at:at + n]

        def par_of(name, a=0, b=None, rows=slice(0, P)):
            at, n = PAR[name]
            return par[rows, at + a:at + (n if b is None else b)]

        ident, ones = C("ident"), C("ones")
        tail = slice(NOPE, QK)

        def heads(ap):
            return ap.rearrange("p (h c) -> p h c", h=HEADS)

        inputs_in = sem("inputs_in")
        par_in = sem("par_in")
        par_free = sem("par_free")
        panel_in = [sem(f"panel_in{i}") for i in range(RING)]
        panel_left = [sem(f"panel_left{i}") for i in range(RING)]
        half_used = sem("half_used")
        hi_ready = sem("hi_ready")
        lo_first = sem("lo_first")
        c_ready = sem("c_ready")
        ada_product = sem("ada_product")
        ada_copied = sem("ada_copied")
        u_rounded = sem("u_rounded")
        hidden_rounded = sem("hidden_rounded")
        hidden_ready = sem("hidden_ready")
        up_scaled = sem("up_scaled")
        ab_turned = sem("ab_turned")
        ab_read = sem("ab_read")
        m_added = sem("m_added")
        m_rounded = sem("m_rounded")
        cond_ready = sem("cond_ready")
        ada_done = sem("ada_done")
        mods_ready = sem("mods_ready")
        prod = sem("prod")
        drained = {"a": sem("drained_by_act"), "v": sem("drained_by_dve")}
        squares = sem("squares")
        summed = sem("summed")
        roots = sem("roots")
        scaled = sem("scaled")
        normed = sem("normed")
        mod_done = sem("mod_done")
        gmv_norm = sem("gmv_norm")
        gmv_var = sem("gmv_var")
        gmv_root = sem("gmv_root")
        ya_ready = sem("ya_ready")
        pads = sem("pads")
        kr_ready = sem("kr_ready")
        kr_rot = sem("kr_rot")
        krw_ready = sem("krw_ready")
        q_rot = sem("q_rot")
        q_ready = sem("q_ready")
        inverted = sem("inverted")
        att_s = sem("att_s")
        att_max = sem("att_max")
        att_exp = sem("att_exp")
        att_p = sem("att_p")
        att_t = sem("att_t")
        att_pt = sem("att_pt")
        att_o = sem("att_o")
        att_y = sem("att_y")
        conv_done = sem("conv_done")
        conv_silu = sem("conv_silu")
        tok_t = sem("tok_t")
        tok_c = sem("tok_c")
        dt_ready = sem("dt_ready")
        dt_ln = sem("dt_ln")
        g_ready = sem("g_ready")
        dpe = [sem(f"delta_product{d}") for d in range(2)]
        dact = [sem(f"delta_act{d}") for d in range(2)]
        ddve = [sem(f"delta_dve{d}") for d in range(2)]
        dpool = [sem(f"delta_pool{d}") for d in range(2)]
        m_ready = sem("m_ready")
        yb_ready = sem("yb_ready")
        eps_ready = sem("eps_ready")
        act_step = sem("act_step")
        dve_step = sem("dve_step")
        pool_step = sem("pool_step")
        out_done = sem("out_done")
        ATT = [0, 4 * MH]
        S_BANKS = (0, 1, 4, 5)

        class Steps:

            def __init__(self, eng, s):
                self.eng, self.s, self.n = eng, s, 0

            def __call__(self, ins):
                ins.then_inc(self.s, 1)
                self.n += 1
                return self.n

            def wait(self, n=None):
                self.eng.wait_ge(self.s, self.n if n is None else n)

        def unit_plan():
            plan, n, m = {}, 0, 0

            def add(key, k):
                nonlocal n, m
                plan[key] = (n, m, k)
                n += 1
                m += k

            for l in range(DEPTH):
                add((l, "norm", 0), DC)
                add((l, "norm", 1), DC)
                add((l, "cq"), 3)
                add((l, "ckv"), 2)
                add((l, "k"), MH)
                add((l, "q"), MH)
                for c in range(8):
                    add((l, "qk", c), 1)
                for c in range(4):
                    add((l, "o", c), 1)
                add((l, "norm", 2), DC)
            return plan

        units = unit_plan()

        def width(l):
            return T if l + 1 < DEPTH else SEQ

        def halves(nt):
            return [(0, slice(0, SEQ)), (1, slice(SEQ, T))][:nt // SEQ]

        def count_after(q, who):
            return counts[who][q + 1]

        def wait_drained(eng, key):
            q = number[key] if isinstance(key, tuple) else key
            eng.wait_ge(drained[owner[q]], count_after(q, owner[q]))

        def wait_product(eng, key):
            eng.wait_ge(prod, number[key] + 1)

        def bank_of(key):
            return bank[number[key] % 4]

        ORDER = [[2, 3, 0, 1], [3, 2, 1, 0]]
        D_PE, D_ACT, D_DVE, D_POOL = 18, 11, 16, 8
        block = ctx.enter_context(nc.Block())

        def half_source(slot, kind, part):
            panel = ring[:, slot * PANEL:(slot + 1) * PANEL]
            if kind == "k":
                return panel[:, part * HALF:(part + 1) * HALF]
            return panel.rearrange("p (k n) -> p k n", n=UNIT)[:, :, part * P:(part + 1) * P]

        def half_dest(buf, b, kind):
            dst = buf[:, b % HALVES, :]
            return dst if kind == "k" else dst.rearrange("p (k n) -> p k n", n=P)

        class Splits:

            def __init__(self, one):
                self.one, self.n, self.r, self.per = one, 0, 0, 0

            def next(self, count=1):
                for _ in range(count):
                    while self.n < N_PANELS and KINDS[self.n] == "raw":
                        self.n += 1
                    if self.n >= N_PANELS:
                        return
                    self.one(self.n, split_before[self.n], KINDS[self.n], self.r, self.per)
                    self.n += 1

            def upto(self, n):
                while self.n < min(n, N_PANELS):
                    if KINDS[self.n] == "raw":
                        self.n += 1
                    else:
                        self.next()

        @block.sync
        def _(sp):
            sp.dma_start(cond[:, :, :], c_d).then_inc(inputs_in, 16)
            for k in range(DC):
                sp.dma_start(h[:, k, :], x_d[k * P:(k + 1) * P, :]).then_inc(inputs_in, 16)
            sp.dma_start(cst[:, :], cst_d).then_inc(inputs_in, 16)
            sp.dma_start(mod_par[:, :, :], mod_d).then_inc(inputs_in, 16)
            sp.dma_start(par[:, :], par_d[:, 0:NPAR]).then_inc(par_in, 16)
            rounds = N_PANELS // RING
            for i in range(RING):
                sp.dma_start(ring[:, i * PANEL:(i + 1) * PANEL], wts[i]).then_inc(panel_in[i], 16)
            with sp.Fori(1, rounds) as r:
                for i in range(RING):
                    sp.wait_ge(panel_left[i], r)
                    sp.dma_start(ring[:, i * PANEL:(i + 1) * PANEL],
                                 wts[bass.ds(r * RING + i, 1)].rearrange("o p n -> p (o n)")).then_inc(panel_in[i], 16)
            for n in range(rounds * RING, N_PANELS):
                i = n % RING
                sp.wait_ge(panel_left[i], n // RING)
                sp.dma_start(ring[:, i * PANEL:(i + 1) * PANEL], wts[n]).then_inc(panel_in[i], 16)
            last = DEPTH - 1
            for j in range(DC):
                wait_drained(sp, (last, "down", 1, j))
                sp.dma_start(out_d[j * P:(j + 1) * P, :], h[:, j, 0:SEQ]).then_inc(out_done, 16)
            sp.wait_ge(out_done, 16 * DC)

        @block.gpsimd
        def _(pool):
            pool.memset(eps, EPS).then_inc(eps_ready, 1)
            pool.wait_ge(inputs_in, 16 * (DC + 3))
            for l in range(DEPTH):
                pool.wait_ge(att_y, ATT[l] + width(l) // P * MH)
                for a in (0, 258):
                    last = pool.memset(convin[:, :, :, a:a + 2], 0.0)
                last.then_inc(pads, 1)
                for j in range(4):
                    it = l * 4 + j
                    for d in range(2):
                        pool.wait_ge(dact[d], it * D_ACT + 1)
                        mask = C("upto" if d == 0 else "from").unsqueeze(1).to_broadcast([P, HEADS, P])
                        pool.tensor_tensor(heads(E[:, d, :]), heads(E[:, d, :]), mask, ALU.mult).then_inc(dpool[d], 1)
                    for n in range(LEVELS):
                        for d in range(2):
                            if n == 0:
                                pool.wait_ge(ddve[d], it * D_DVE + 5)
                            elif n == 2:
                                pool.wait_ge(ddve[d], it * D_DVE + 6)
                            elif n >= 3:
                                pool.wait_ge(dpe[d], it * D_PE + 2 + 2 * (n - 2))
                            dst = (ml if n % 2 == 0 else E)[:, d, :]
                            mask = C("level")[:, n * P:(n + 1) * P].unsqueeze(1).to_broadcast([P, HEADS, P])
                            pool.tensor_tensor(heads(dst), heads(mt[:, d, :]), mask, ALU.mult).then_inc(dpool[d], 1)

        @block.scalar
        def _(act):
            step = Steps(act, act_step)

            def round_panel(n, sb, kind, r, per):
                for part in range(2):
                    b = 2 * sb + part
                    if part == 0:
                        act.wait_ge(panel_in[n % RING], 16 * (n // RING + 1) + r * (16 * per // RING))
                    if b >= HALVES:
                        act.wait_ge(half_used, b - HALVES + 1 + r * (2 * per))
                    act.activation(half_dest(w_hi, b, kind), half_source(n % RING, kind, part),
                                   ACT.Copy).then_inc(hi_ready, 1)

            splits = Splits(round_panel)

            def ada_copy(l, p, r=0, per=0):
                g = ADA_PANELS * l + p
                act.wait_ge(ada_product, g + 1 + r * per)
                if g >= 2:
                    act.wait_ge(ada_done, g - 1 + r * per)
                act.activation(ada_rows[:, p % 2, :], bank[5 + p % 2][0:4, 0:UNIT], ACT.Copy).then_inc(ada_copied, 1)

            def square(key, k, src, rows=slice(0, P), w=T, stop=slice(0, P)):
                n, m, _ = units[key]
                m += k
                if m >= 4:
                    act.wait_ge(summed, m - 3)
                act.activation(sq[rows, m % 4, 0:w], src, ACT.Square).then_inc(squares, 1)

            def root(key, size, w=T, rows=slice(0, P)):
                n, m, k = units[key]
                act.wait_ge(summed, m + k)
                if n >= 2:
                    act.wait_ge(scaled, n - 1)
                act.activation(rt[rows, n % 2, 0:w], bank[4 + n % 2][rows, 0:w], ACT.Sqrt, bias=eps[rows, :],
                               scale=1.0 / size).then_inc(roots, 1)

            def norm(l, i, w, h_key):
                n, m, _ = units[(l, "norm", i)]
                for k in range(DC):
                    if h_key is not None:
                        wait_drained(act, h_key + (k,))
                    square((l, "norm", i), k, h[:, k, 0:w], w=w)
                root((l, "norm", i), D, w)
                act.wait_ge(mods_ready, 2 * l + (1 if i == 0 else 2))

                def rounded(k, done):
                    step.wait(done)
                    act.activation(u_hi[:, k, 0:w], sq[:, k % 4, 0:w], ACT.Copy).then_inc(u_rounded, 1)

                before = None
                for k in range(DC):
                    if k < DC - 1:
                        act.wait_ge(normed, (3 * l + i) * (DC - 1) + k + 1)
                    else:
                        act.wait_ge(scaled, n + 1)
                    for s, cols in halves(w):
                        last = act.activation(sq[:, k % 4, cols], sq[:, k % 4, cols], ACT.Identity,
                                              scale=scales[:, l, i, k, s:s + 1],
                                              bias=mods[:, l, 3 * i * DC + k, s:s + 1])
                    done = step(last)
                    if before is not None:
                        rounded(k - 1, before)
                    before = done
                rounded(DC - 1, before)

            def ffn(l, f, w, carry):
                q0 = number[(l, "g", f, 0)]
                v0 = counts["v"][q0]
                h0 = FC * (2 * l + f)
                flat = h_hi[:, :, :].rearrange("p n w -> p (n w)")
                peel, body = (1, 2) if carry is not None else (2, 3)

                def pair(i, loop=None):
                    r = 0 if loop is None else loop
                    more = r * body
                    splits.next()
                    for c in range(2):
                        act.wait_ge(prod, q0 + 1 + 4 * i + c + 4 * more)
                        if i:
                            act.wait_ge(hidden_ready, h0 + 2 * i + c - 1 + 2 * more)
                        act.activation(sg[:, c, 0:w], bank[(q0 + c) % 4][:, 0:w], ACT.Silu).then_inc(drained["a"], 1)
                    splits.next(2 if carry is not None else 1)
                    for c in range(2):
                        act.wait_ge(drained["v"], v0 + 2 * i + c + 1 + 2 * more)
                        dst = flat[:, bass.ds(more * (2 * T) + (2 * i + c) * T, w)] if loop is not None else h_hi[:, 2 * i + c, 0:w]
                        act.activation(dst, sg[:, c, 0:w], ACT.Copy).then_inc(hidden_rounded, 1)
                    if carry is not None:
                        ada_copy(carry, ADA_FIRST + i, r, body)

                splits.upto(START[l, "gu", f] + 1)
                for i in range(peel):
                    pair(i)
                n0, rounds = splits.n, (FC // 2 - peel) // body
                splits.per = body * (3 if carry is not None else 2)
                with act.Fori(0, rounds) as r:
                    splits.r = r
                    for i in range(body):
                        pair(peel + i, r)
                splits.r, splits.n = 0, n0 + rounds * splits.per
                splits.per = 0
                n = START[l, "down", f]
                p = ADA_FIRST + FC // 2
                for s in range(12):
                    splits.upto(n + 2)
                    n += 1
                    if carry is not None:
                        splits.upto(n + 2)
                        ada_copy(carry, p)
                        n += 1
                        p += 1

            act.wait_ge(inputs_in, 16 * (DC + 3))
            step(act.activation(cond[:, :, :], cond[:, :, :], ACT.Silu))
            step.wait()
            act.activation(c4[:, :, 0:2], cond[:, :, :], ACT.Copy).then_inc(cond_ready, 1)
            act.wait_ge(eps_ready, 1)
            for p in range(ADA_FIRST):
                splits.upto(p + 2)
                ada_copy(0, p)
            for l in range(DEPTH):
                w = width(l)
                nt = w // P
                if l:
                    wait_drained(act, (l - 1, "out", DC - 1))
                    act.dma_start(par[:, :], par_d[:, l * NPAR:(l + 1) * NPAR]).then_inc(par_in, 16)
                norm(l, 0, T, (l - 1, "down", 1) if l else None)
                ffn(l, 0, T, 0 if l == 0 else None)
                norm(l, 1, T, (l, "down", 0))

                for c in range(GMC):
                    if c % 2 == 0:
                        splits.upto(START[l, "gmu"] + c // 2 + 2)
                    wait_product(act, (l, "gmu", c))
                    act.activation(ya[:, c, 0:w], bank_of((l, "gmu", c))[:, 0:w],
                                   ACT.Gelu_apprx_tanh).then_inc(drained["a"], 1)
                for p in range(2):
                    splits.upto(START[l, "gmv"] + p + 2)
                    for t in range(nt):
                        wait_product(act, (l, "gmv", p, t))
                        act.activation(gv[:, t, p * UNIT:(p + 1) * UNIT], bank_of((l, "gmv", p, t))[:, 0:UNIT],
                                       ACT.Gelu_apprx_tanh).then_inc(drained["a"], 1)
                act.wait_ge(gmv_var, l + 1)
                act.activation(lnr[:, 0:nt], mv[:, 0:nt, 1], ACT.Sqrt, bias=eps[:, :]).then_inc(gmv_root, 1)

                for i in range(3):
                    key = (l, "cq", i)
                    if i != 1:
                        splits.upto(START[l, "low"] + i // 2 + 2)
                    wait_product(act, key)
                    square((l, "cq"), i, bank_of(key)[:, 0:w], w=w)
                    act.activation(cq[:, i, 0:w], bank_of(key)[:, 0:w], ACT.Copy).then_inc(drained["a"], 1)
                for i in range(2):
                    key = (l, "ckv", i)
                    if i == 1:
                        splits.upto(START[l, "low"] + 4)
                    wait_product(act, key)
                    square((l, "ckv"), i, bank_of(key)[:, :])
                    act.activation(ckv[:, i, :], bank_of(key)[:, :], ACT.Copy).then_inc(drained["a"], 1)
                key = (l, "krope")
                wait_product(act, key)
                act.activation(kr[tail, 0, :], bank_of(key)[0:ROPE, :], ACT.Copy)
                act.activation(kr[ROPE:ROPE + 16, 0, :], bank_of(key)[ROPE:ROPE + 16, :],
                               ACT.Copy).then_inc(drained["a"], 1)
                root((l, "cq"), LQ, w)
                root((l, "ckv"), LKV)
                act.wait_ge(drained["a"], count_after(number[key], "a"))
                act.wait_ge(summed, units[(l, "ckv")][1] + 2)
                for i in range(4):
                    act.activation(sq[tail, i, :], kr[tail, 0, :], ACT.Square)
                for hd in range(MH):
                    key = (l, "nope", hd // 2)
                    rows = slice(NOPE * (hd % 2), NOPE * (hd % 2) + NOPE)
                    if hd % 2 == 0:
                        wait_product(act, key)
                    square((l, "k"), hd, bank_of(key)[rows, :], slice(0, NOPE))
                    last = act.activation(kk[0:NOPE, hd, :], bank_of(key)[rows, :], ACT.Copy)
                    if hd % 2:
                        last.then_inc(drained["a"], 1)
                for t in range(4):
                    wait_product(act, (l, "mv", t))
                    act.activation(vm[:, t, :], bank_of((l, "mv", t))[:, :], ACT.Copy).then_inc(drained["a"], 1)
                root((l, "k"), QK, rows=slice(0, MH))
                for hd in range(MH):
                    key = (l, "uq", hd)
                    wait_product(act, key)
                    square((l, "q"), hd, bank_of(key)[0:QK, 0:w], slice(0, QK), w)
                    act.activation(qq[0:QK, hd, 0:w], bank_of(key)[0:QK, 0:w], ACT.Copy).then_inc(drained["a"], 1)
                root((l, "q"), QK, w, slice(0, MH))
                splits.upto(START[l, "qkv"] + 1)
                a0 = ATT[l]
                for i in range(nt * MH + 2):
                    if i < nt * MH:
                        a = a0 + i
                        s = a % 4
                        act.wait_ge(att_max, a + 1)
                        keys = slice(0, T) if i // MH < 2 else slice(0, CTX)
                        if a >= 4:
                            act.wait_ge(att_t, a - 3)
                        act.activation(pr[:, s, keys], bank[S_BANKS[s]][:, keys], ACT.Exp,
                                       scale=QK ** -0.5, bias=nb[:, s:s + 1],
                                       accum_out=rs[:, s:s + 1]).then_inc(att_exp, 1)
                    if i > 1:
                        b = a0 + i - 2
                        nk = 4 if (i - 2) // MH < 2 else 2
                        act.wait_ge(att_t, b + 1)
                        if b >= 2:
                            act.wait_ge(att_o, b - 1)
                        act.activation(prT[:, b % 2, 0:nk * P], bank[2 + b % 2][:, 0:nk * P],
                                       ACT.Copy).then_inc(att_pt, 1)

                act.wait_ge(dt_ready, l + 1)
                act.wait_ge(par_in, 16 * (l + 1))
                act.activation(t1, t1, ACT.Exp, scale=-1.0)
                act.activation(beta, gab[:, :, 8:16], ACT.Exp, scale=-1.0)
                step(act.activation(expa, par_of("a_log"), ACT.Exp))
                step.wait()
                act.activation(t1, t1, ACT.Ln, bias=ones[:, 0:1]).then_inc(dt_ln, 1)

                def conv_in(c):
                    key = (l, "qkv", c)
                    if c % 2 == 0:
                        splits.upto(START[l, "qkv"] + c // 2 + 2)
                    wait_product(act, key)
                    if 12 * l + c >= 3:
                        act.wait_ge(conv_done, 12 * l + c - 2)
                    act.activation(convin[:, c % 3, :, 2:258],
                                   bank_of(key)[:, :].rearrange("p (s w) -> p s w", s=2),
                                   ACT.Copy).then_inc(drained["a"], 1)

                def conv_out(c):
                    act.wait_ge(conv_done, 12 * l + c + 1)
                    dst = qT[:, c, :] if c < 4 else kT[:, c - 4, :] if c < 8 else vT[:, c % 2, :]
                    if c >= 10:
                        act.wait_ge(tok_t, 8 * l + c - 9)
                    act.activation(dst, acc[:, c % 2, :], ACT.Silu).then_inc(conv_silu, 1)

                def tok_copy(i):
                    act.wait_ge(tok_t, 8 * l + i + 1)
                    dst = (vtok if i < 4 else ktok)[:, :, (i % 4) * P:(i % 4 + 1) * P]
                    act.activation(dst, bank[6][:, :].rearrange("p (t c) -> p t c", t=4),
                                   ACT.Copy).then_inc(tok_c, 1)

                conv_in(0)
                conv_in(1)
                for c in range(12):
                    if c + 2 < 12:
                        conv_in(c + 2)
                    conv_out(c)
                    if c >= 9:
                        tok_copy(c - 9)
                tok_copy(3)
                act.wait_ge(conv_silu, 12 * l + 12)
                for i in range(9):
                    if i < 8:
                        square((l, "qk", i), 0, (kT if i < 4 else qT)[:, i % 4, :])
                    if i > 0:
                        root((l, "qk", i - 1), 1.0)
                    if 2 <= i <= 5:
                        tok_copy(2 + i)

                for j in range(4):
                    it = l * 4 + j
                    for d in range(2):
                        A = bank[3 * d]
                        act.wait_ge(ddve[d], it * D_DVE + 2)
                        act.activation(E[:, d, :], E[:, d, :], ACT.Exp).then_inc(dact[d], 1)
                        act.activation(EG[:, d, :], A[:, :], ACT.Exp).then_inc(dact[d], 1)
                        act.wait_ge(ddve[d], it * D_DVE + 3)
                        act.activation(egam[:, d, :], gamc[:, d, :], ACT.Exp)
                        act.activation(kds[:, d, :], kds[:, d, :], ACT.Exp).then_inc(dact[d], 1)
                    for n in range(LEVELS):
                        for d in range(2):
                            act.wait_ge(dpe[d], it * D_PE + (3 if n == 0 else 2 + 2 * n))
                            act.activation((X if n == 0 else Y)[:, d, :], bank[3 * d][:, :],
                                           ACT.Copy).then_inc(dact[d], 1)
                    for d in range(2):
                        act.wait_ge(dpe[d], it * D_PE + 16)
                        act.activation(nwT[:, d, :], bank[3 * d][:, :], ACT.Copy, scale=-1.0).then_inc(dact[d], 1)

                for d in range(2):
                    act.wait_ge(ddve[d], (l * 4 + 4) * D_DVE)
                for i in range(5):
                    if i < 4:
                        square((l, "o", i), 0, yb[:, i, 0:w], w=w)
                    if i > 0:
                        root((l, "o", i - 1), P, w)
                for c in range(4):
                    key = (l, "z", c)
                    if c % 2 == 0:
                        splits.upto(START[l, "z"] + c // 2 + 2)
                    wait_product(act, key)
                    act.activation(zs[:, c, 0:w], bank_of(key)[:, 0:w], ACT.Silu).then_inc(drained["a"], 1)

                for pair in range(DC // 2):
                    n = START[l, "merge", pair]
                    for b in range(3):
                        splits.upto(n + 2)
                        n += 1
                        if b and l + 1 < DEPTH:
                            ada_copy(l + 1, 3 * pair + b - 1)
                        for c in range(2):
                            key = (l, "gate", 2 * pair + c, b)
                            wait_product(act, key)
                            if pair:
                                wait_drained(act, (l, "branch", 2 * pair + c - 2, b))
                            act.activation(sig[:, 2 * b + c, 0:w], bank_of(key)[:, 0:w],
                                           ACT.Sigmoid).then_inc(drained["a"], 1)
                        if l + 1 < DEPTH:
                            splits.upto(n + 2)
                            n += 1
                    if l + 1 < DEPTH:
                        ada_copy(l + 1, 3 * pair + 2)
                    n += 2
                    splits.upto(n + 1)
                    if pair == 3 and l + 1 < DEPTH:
                        n += 1
                        splits.upto(n + 1)
                        ada_copy(l + 1, 12)
                    for c in range(2):
                        act.wait_ge(m_added, DC * l + 2 * pair + c + 1)
                        act.activation(m_hi[:, 2 * pair + c, 0:w], macc[:, c, 0:w], ACT.Copy).then_inc(m_rounded, 1)
                for p in range(4):
                    splits.upto(START[l, "out"] + p + 2)
                norm(l, 2, w, (l, "out"))
                ffn(l, 1, w, l + 1 if l + 1 < DEPTH else None)

        @block.tensor
        def _(pe):
            class Weights:

                def __init__(self):
                    self.n, self.r, self.per = 0, 0, 0
                    self.release, self.left, self.following = None, None, None
                    self.unreported, self.owed, self.count = 0, 0, 0

                def raw(self):
                    n = self.n
                    assert KINDS[n] == "raw"
                    pe.wait_ge(panel_in[n % RING], 16 * (n // RING + 1))
                    self.n += 1
                    self.left, self.release = self.release, None
                    self.following = n % RING
                    self.owed = 0
                    return ring[:, n % RING * PANEL:(n % RING + 1) * PANEL]

                def half(self, part):
                    n, kind = self.n, KINDS[self.n]
                    sb = split_before[n]
                    if part == 0:
                        pe.wait_ge(lo_first, sb + 1 + self.r * self.per)
                        self.left = self.release
                        self.release = None
                    else:
                        pe.wait_ge(panel_left[n % RING], n // RING + 1 + self.r * (self.per // RING))
                        self.n += 1
                        self.left = None
                    self.following = None
                    b = 2 * sb + part
                    self.owed, self.unreported, self.count = self.unreported, 1, 0
                    width = UNIT if kind == "k" else P
                    return [x[:, b % HALVES, :].rearrange("p (k n) -> p k n", n=width) for x in (w_hi, w_lo)]

                def both(self):
                    first = self.half(0)
                    left, owed = self.left, self.owed
                    second = self.half(1)
                    self.left, self.owed, self.unreported = left, owed, 2
                    return first, second

                def used(self, ins):
                    self.count += 1
                    if self.left is not None:
                        ins.then_inc(panel_left[self.left], 1)
                        self.left = None
                    elif self.owed and self.count > 1:
                        ins.then_inc(half_used, 1)
                        self.owed -= 1
                    if self.following is not None:
                        self.release, self.following = self.following, None
                    return ins

            weights = Weights()

            def free_bank(key):
                q = number[key]
                if q >= 4:
                    wait_drained(pe, q - 4)

            def product(out, parts, signal):
                for n, (lhsT, rhs) in enumerate(parts):
                    last = weights.used(pe.matmul(out, lhsT, rhs, start=n == 0, stop=n == len(parts) - 1))
                if signal is not None:
                    last.then_inc(signal, 1)

            def split_matmul(out, lhs, rhs, start, stop):
                for n, (a, b) in enumerate(((0, 0), (1, 0), (0, 1))):
                    last = weights.used(pe.matmul(out, lhs[a], rhs[b], start=start and n == 0, stop=stop and n == 2))
                return last

            def ada_turn(l, p, r=0, per=0):
                pe.wait_ge(ada_copied, ADA_PANELS * l + p + 1 + r * per)
                for c in range(2):
                    at = 2 * (2 * p + c)
                    out = bank[7][:, at:at + 2] if isinstance(r, int) else bank[7][:, bass.ds(r * (4 * per) + at, 2)]
                    last = pe.matmul(out, ada_rows[:, p % 2, c * P:(c + 1) * P], C("fold", slice(0, 4)), start=True,
                                     stop=True)
                last.then_inc(ada_done, 1)

            def ada(l, p, r=0, per=0, first=False):
                g = ADA_PANELS * l + p
                if g >= 2:
                    pe.wait_ge(ada_copied, g - 1 + r * per)
                out = bank[5 + p % 2][0:4, 0:UNIT]
                for part in range(2):
                    w2 = weights.half(part)
                    for k in range(4):
                        for a in range(2):
                            last = weights.used(pe.matmul(out, c4[:, 4 * part + k, :], w2[a][:, k, :],
                                                          start=part == k == a == 0, stop=part == a == 1 and k == 3))
                last.then_inc(ada_product, 1)
                if not first:
                    ada_turn(l, p - 1, r, per)

            def sums(key, w=T, rows=slice(0, P)):
                n, m, count = units[key]
                if n >= 2:
                    pe.wait_ge(roots, n - 1)
                for k in range(count):
                    pe.wait_ge(squares, m + k + 1)
                    pe.matmul(bank[4 + n % 2][:, 0:w], ones[rows, :], sq[rows, (m + k) % 4, 0:w],
                              start=k == 0, stop=k == count - 1).then_inc(summed, 1)

            def std(keys, w, src, ready, base):
                for c, key in enumerate(keys):
                    w2 = weights.half(c)
                    free_bank(key)
                    for k in range(DC):
                        if ready is not None:
                            pe.wait_ge(ready, base + k + 1)
                        last = split_matmul(bank_of(key)[:, 0:w], [x[:, k, :] for x in w2],
                                            [x[:, k, 0:w] for x in src], k == 0, k == DC - 1)
                    ready = None
                    last.then_inc(prod, 1)

            def head_sum(key, hd, w=T):
                n, m, count = units[key]
                if hd == 0:
                    pe.wait_ge(roots, n - 1)
                pe.wait_ge(squares, m + hd + 1)
                pe.matmul(bank[4 + n % 2][0:32, 0:w], C("pick", slice(0, QK))[:, 31 - hd:63 - hd],
                          sq[0:QK, (m + hd) % 4, 0:w], start=hd == 0, stop=hd == count - 1).then_inc(summed, 1)

            def streamed(outs, w, src, ready, base):
                for c, w2 in enumerate(weights.both()):
                    outs[c] = (outs[c], w2)
                for k in range(DC):
                    pe.wait_ge(ready, base + k + 1)
                    for out, w2 in outs:
                        last = split_matmul(out, [x[:, k, :] for x in w2], [x[:, k, 0:w] for x in src], k == 0,
                                            k == DC - 1)
                        if k == DC - 1:
                            last.then_inc(prod, 1)

            u = (u_hi, u_lo)

            def ffn(l, f, w, carry, ready_base):
                q0 = number[(l, "g", f, 0)]
                v0 = counts["v"][q0]
                a0 = counts["a"][q0]
                h0 = FC * (2 * l + f)
                d0 = number[(l, "down", f, 0)]
                peel, body = (1, 2) if carry is not None else (2, 3)

                def pair(i, loop=None):
                    r = 0 if loop is None else loop
                    more = r * body
                    for part in range(2):
                        if i == 0 and part == 0:
                            for c in range(2):
                                free_bank((l, "g", f, c))
                            streamed([bank[(q0 + c) % 4][:, 0:w] for c in range(2)], w, u, mod_done, ready_base)
                            continue
                        for c in range(2):
                            w2 = weights.half(c)
                            b = 2 * part + c
                            if i == 0:
                                free_bank((l, "gu"[part], f, c))
                            elif part == 0:
                                pe.wait_ge(drained["a"], a0 + 2 * (i - 1) + c + 1 + 2 * more)
                            else:
                                pe.wait_ge(drained["v"], v0 + 2 * (i - 1) + c + 1 + 2 * more)
                            for k in range(DC):
                                last = split_matmul(bank[(q0 + b) % 4][:, 0:w], [x[:, k, :] for x in w2],
                                                    [x[:, k, 0:w] for x in u], k == 0, k == DC - 1)
                            last.then_inc(prod, 1)
                    if carry is not None:
                        ada(carry, ADA_FIRST + i, r, body, i == 0)

                if carry is not None:
                    pe.wait_ge(mods_ready, 2 * carry + 1)
                for i in range(peel):
                    pair(i)
                rounds = (FC // 2 - peel) // body
                n0 = weights.n
                weights.per = body * (3 if carry is not None else 2)
                with pe.Fori(0, rounds) as r:
                    weights.r = r
                    for i in range(body):
                        pair(peel + i, r)
                weights.r, weights.n = 0, n0 + rounds * weights.per

                pe.wait_ge(drained["a"], a0 + FC)
                vd = counts["v"][d0]
                n0 = weights.n
                weights.per = 12 if carry is not None else 6
                hid = (h_hi, h_lo)
                with pe.Fori(0, 2) as r:
                    weights.r = r
                    for g in range(2):
                        for s in range(3):
                            for c in range(2):
                                w2 = weights.half(c)
                                if g == 0 and c == 0:
                                    pe.wait_ge(hidden_ready, h0 + min(8 * s + 8, FC))
                                m = 2 * g + c
                                if s == 0:
                                    pe.wait_ge(drained["v"], r * 4 + (vd + m - 3))
                                for k in range(8 * s, min(8 * s + 8, FC)):
                                    last = split_matmul(bank[(d0 + m) % 4][:, 0:w], [x[:, k - 8 * s, :] for x in w2],
                                                        [x[:, k, 0:w] for x in hid], k == 0, k == FC - 1)
                                if s == 2:
                                    last.then_inc(prod, 1)
                            if carry is not None:
                                ada(carry, ADA_FIRST + FC // 2 + 3 * g + s, r, 6)
                weights.n, weights.r = n0 + 2 * weights.per, 0
                weights.per = 0
                if carry is not None:
                    ada_turn(carry, ADA_PANELS - 1)

            pe.wait_ge(inputs_in, 16 * (DC + 3))
            pe.wait_ge(c_ready, 1)
            for p in range(ADA_FIRST):
                ada(0, p, first=p == 0)
            ada_turn(0, ADA_FIRST - 1)
            for l in range(DEPTH):
                w = width(l)
                nt = w // P
                sums((l, "norm", 0))
                ffn(l, 0, T, 0 if l == 0 else None, (3 * l) * DC)
                sums((l, "norm", 1))

                for c in range(2):
                    free_bank((l, "gmu", c))
                streamed([bank_of((l, "gmu", c))[:, 0:w] for c in range(2)], w, u, mod_done, (3 * l + 1) * DC)
                std([(l, "gmu", 2), (l, "gmu", 3)], w, u, None, 0)
                for p in range(2):
                    for part in range(2):
                        w2 = weights.half(part)
                        for t in range(nt):
                            key = (l, "gmv", p, t)
                            if part == 0:
                                free_bank(key)
                            for k in range(4):
                                kc = 4 * part + k
                                last = split_matmul(bank_of(key)[:, 0:UNIT], [x[:, kc, t * P:(t + 1) * P] for x in u],
                                                    [x[:, k, :] for x in w2], kc == 0, kc == DC - 1)
                            if part == 1:
                                last.then_inc(prod, 1)

                std([(l, "cq", 0), (l, "cq", 1)], w, u, None, 0)
                std([(l, "cq", 2)], w, u, None, 0)
                for c, key in ((1, (l, "ckv", 0)), (0, (l, "ckv", 1)), (1, (l, "krope"))):
                    w2 = weights.half(c)
                    free_bank(key)
                    for k in range(DC):
                        last = split_matmul(bank_of(key)[:, :], [x[:, k, :] for x in w2], [x[:, k, :] for x in u],
                                            k == 0, k == DC - 1)
                    last.then_inc(prod, 1)
                sums((l, "cq"), w)
                pe.wait_ge(gmv_norm, l + 1)
                pe.wait_ge(par_in, 16 * (l + 1))
                for c in range(GMC):
                    key = (l, "spatial", c)
                    free_bank(key)
                    for t in range(nt):
                        last = pe.matmul(bank_of(key)[:, t * P:(t + 1) * P], gv[:, t, c * P:(c + 1) * P],
                                         par_of("gm_ws", c * P, (c + 1) * P), start=True, stop=True)
                    last.then_inc(prod, 1)
                sums((l, "ckv"))
                wait_drained(pe, (l, "krope"))
                for t in range(4):
                    last = pe.transpose(bank[6][:, 16 * t:16 * t + 16], kr[ROPE:ROPE + 16, 0, t * P:(t + 1) * P],
                                        ident[ROPE:ROPE + 16, ROPE:ROPE + 16])
                last.then_inc(ab_turned, 1)
                pe.wait_ge(kr_ready, l + 1)
                pe.wait_ge(ab_read, l + 1)
                pe.matmul(bank[6][tail, 0:SEQ], C("rot", tail), krw[tail, 0, 0:SEQ], start=True,
                          stop=True).then_inc(kr_rot, 1)
                ukv = weights.raw().rearrange("p (k n) -> p k n", n=1024)
                pe.wait_ge(scaled, units[(l, "ckv")][0] + 1)
                for hp in range(4):
                    key = (l, "nope", hp)
                    free_bank(key)
                    product(bank_of(key)[:, :], [(ukv[:, k, hp * P:(hp + 1) * P], ckv[:, k, :]) for k in range(2)], prod)
                    for hd in (2 * hp, 2 * hp + 1):
                        head_sum((l, "k"), hd)
                for t in range(4):
                    key = (l, "mv", t)
                    free_bank(key)
                    product(bank_of(key)[:, :], [(ckv[:, k, t * P:(t + 1) * P], ukv[:, k, 512:1024]) for k in range(2)],
                            prod)

                def rotate_q(hd):
                    wait_drained(pe, (l, "q_spread", hd))
                    if hd or l:
                        pe.wait_ge(q_ready, MH * l + hd)
                    pe.matmul(bank[6][tail, 0:SEQ], C("rot", tail), qq[tail, hd, 0:SEQ], start=True,
                              stop=True).then_inc(q_rot, 1)

                pe.wait_ge(krw_ready, l + 1)

                def spread(kind, w):
                    n = units[(l, kind)][0]
                    pe.wait_ge(inverted, 2 * l + 1 + (kind == "q"))
                    for hd in range(MH):
                        key = (l, kind + "_spread", hd)
                        free_bank(key)
                        pe.matmul(bank_of(key)[:, 0:w], ident[0:MH, hd:hd + 1].to_broadcast([MH, P]),
                                  rt[0:MH, n % 2, 0:w], start=True, stop=True).then_inc(prod, 1)
                        if kind == "q" and hd:
                            rotate_q(hd - 1)

                for hd in range(MH):
                    if hd % 4 == 0:
                        uq = weights.raw()[:, 0:3 * 4 * QK].rearrange("p (k n) -> p k n", n=4 * QK)
                    key = (l, "uq", hd)
                    free_bank(key)
                    at = (hd % 4) * QK
                    product(bank_of(key)[0:QK, 0:w], [(uq[:, k, at:at + QK], cq[:, k, 0:w]) for k in range(3)], prod)
                    head_sum((l, "q"), hd, w)
                spread("k", T)
                spread("q", w)
                rotate_q(MH - 1)

                a0 = ATT[l]
                pe.wait_ge(q_ready, MH * (l + 1))
                na = nt * MH
                for i in range(na + 3):
                    if i < na:
                        a = a0 + i
                        t, hd = divmod(i, MH)
                        keys = slice(0, T) if t < 2 else slice(CTX, T)
                        if a >= 4:
                            pe.wait_ge(att_exp, a - 3)
                        pe.matmul(bank[S_BANKS[a % 4]][:, 0:keys.stop - keys.start], qq[0:QK, hd, t * P:(t + 1) * P],
                                  kk[0:QK, hd, keys], start=True, stop=True).then_inc(att_s, 1)
                    if 1 < i <= na + 1:
                        a = a0 + i - 2
                        nk = 4 if (i - 2) // MH < 2 else 2
                        pe.wait_ge(att_p, a + 1)
                        if a >= 2:
                            pe.wait_ge(att_pt, a - 1)
                        for n in range(nk):
                            last = pe.transpose(bank[2 + a % 2][:, n * P:(n + 1) * P], pr[:, a % 4, n * P:(n + 1) * P],
                                                ident)
                        last.then_inc(att_t, 1)
                    if i > 2:
                        a = a0 + i - 3
                        t, hd = divmod(i - 3, MH)
                        nk, k0 = (4, 0) if t < 2 else (2, 2)
                        pe.wait_ge(att_pt, a + 1)
                        if a >= 2:
                            pe.wait_ge(att_y, a - 1)
                        rows = slice(NOPE * (hd % 2), NOPE * (hd % 2) + NOPE)
                        for n in range(nk):
                            last = pe.matmul(bank[6][rows, 0:P], vm[:, k0 + n, hd * 64:hd * 64 + 64],
                                             prT[:, a % 2, n * P:(n + 1) * P], start=n == 0, stop=n == nk - 1)
                        last.then_inc(att_o, 1)

                pe.wait_ge(att_pt, a0 + na)
                pe.wait_ge(att_y, a0 + na)

                def turn(i, src):
                    if 8 * l + i:
                        pe.wait_ge(tok_c, 8 * l + i)
                    for t in range(4):
                        last = pe.transpose(bank[6][:, t * P:(t + 1) * P], src[:, t * P:(t + 1) * P], ident)
                    last.then_inc(tok_t, 1)

                for p in range(6):
                    std([(l, "qkv", 2 * p), (l, "qkv", 2 * p + 1)], T, u, None, 0)
                for i in range(4):
                    pe.wait_ge(conv_silu, 12 * l + 9 + i)
                    turn(i, vT[:, i % 2, :])
                for i in range(8):
                    sums((l, "qk", i))
                    if 1 <= i <= 4:
                        pe.wait_ge(scaled, units[(l, "qk", i - 1)][0] + 1)
                        turn(3 + i, kT[:, i - 1, :])

                pe.wait_ge(scaled, units[(l, "qk", 7)][0] + 1)
                pe.wait_ge(tok_c, 8 * (l + 1))
                pe.wait_ge(g_ready, l + 1)
                for j in range(4):
                    it = l * 4 + j
                    tiles = [ORDER[d][j] for d in range(2)]

                    def each(what, d):
                        for hd in range(HEADS):
                            last = what(hd, slice(hd * P, (hd + 1) * P), slice(tiles[d] * P, (tiles[d] + 1) * P))
                        last.then_inc(dpe[d], 1)

                    def mm(out, lhsT, rhs, start=True, stop=True):
                        return pe.matmul(out, lhsT, rhs, start=start, stop=stop)

                    for d in range(2):
                        pe.wait_ge(ddve[d], it * D_DVE + 1)
                        mm(bank[6][:, 4 * d:4 * d + 4], C("upto" if d == 0 else "from"),
                           g[:, tiles[d], 4 * d:4 * d + 4])
                    for d in range(2):
                        A, upto = bank[3 * d], C("upto" if d == 0 else "from")
                        each(lambda hd, c, t: mm(A[:, c], gB[:, d, c], upto), d)
                    for d in range(2):
                        B, K = bank[3 * d + 1], bank[3 * d + 2]

                        def pairs(hd, c, t):
                            mm(B[:, c], kT[:, hd, t], kT[:, hd, t])
                            return mm(K[:, c], kT[:, hd, t], qT[:, hd, t])
                        each(pairs, d)
                    for d in range(2):
                        pe.wait_ge(ddve[d], it * D_DVE + 6)
                        pe.wait_ge(dact[d], it * D_ACT + 2)
                        each(lambda hd, c, t: pe.transpose(bank[3 * d][:, c], XT[:, d, c], ident), d)
                    for n in range(1, LEVELS):
                        level = E if n % 2 else ml
                        for d in range(2):
                            pe.wait_ge(dpool[d], it * D_POOL + 2 + n)
                            if n == 1:
                                pe.wait_ge(dact[d], it * D_ACT + 4)
                            else:
                                pe.wait_ge(ddve[d], it * D_DVE + 7 + n)
                            each(lambda hd, c, t: mm(bank[3 * d][:, c], level[:, d, c], X[:, d, c]), d)
                        for d in range(2):
                            pe.wait_ge(dact[d], it * D_ACT + 4 + n)

                            def step_z(hd, c, t):
                                if n < LEVELS - 1:
                                    mm(bank[3 * d + 1][:, c], XT[:, d, c], Y[:, d, c])
                                return mm(bank[3 * d + 2][:, c], Y[:, d, c], XT[:, d, c])
                            each(step_z, d)
                    for d in range(2):
                        pe.wait_ge(ddve[d], it * D_DVE + 14)
                        each(lambda hd, c, t: mm(bank[3 * d][:, c], kg[:, d, c], XT[:, d, c]), d)
                    for d in range(2):
                        pe.wait_ge(dact[d], it * D_ACT + 11)

                        def fresh(hd, c, t):
                            last = mm(bank[3 * d + 1][:, c], XT[:, d, c], vtok[:, tiles[d], c], stop=j == 0)
                            if j:
                                last = mm(bank[3 * d + 1][:, c], nwT[:, d, c], S[:, d, c], start=False)
                            return last
                        each(fresh, d)
                    for d in range(2):
                        pe.wait_ge(ddve[d], it * D_DVE + 15)

                        def outs(hd, c, t):
                            last = None
                            if tiles[d] < nt:
                                if j:
                                    mm(bank[3 * d][:, c], S[:, d, c], EG[:, d, c], stop=False)
                                last = mm(bank[3 * d][:, c], vnew[:, d, c], att[:, d, c], start=j == 0)
                            if j < 3:
                                last = mm(bank[3 * d + 2][:, c], kd[:, d, c], vnew[:, d, c])
                            return last
                        each(outs, d)

                for d in range(2):
                    pe.wait_ge(ddve[d], (l * 4 + 4) * D_DVE)
                for c in range(4):
                    sums((l, "o", c), w)
                for p in range(2):
                    std([(l, "z", 2 * p), (l, "z", 2 * p + 1)], w, u, None, 0)

                if l + 1 < DEPTH:
                    pe.wait_ge(mods_ready, 2 * l + 2)
                pe.wait_ge(ya_ready, l + 1)
                pe.wait_ge(yb_ready, l + 1)
                for gq in range(4):
                    for b in range(3):
                        std([(l, "gate", 2 * gq + c, b) for c in range(2)], w, u, None, 0)
                        if l + 1 < DEPTH:
                            ada(l + 1, 3 * gq + b, first=3 * gq + b == 0)
                    for b, src in enumerate((ya, yb, yc)):
                        if b != 1:
                            panel = weights.raw().rearrange("p (k n) -> p k n", n=UNIT)
                        for c in range(2):
                            key = (l, "branch", 2 * gq + c, b)
                            free_bank(key)
                            product(bank_of(key)[:, 0:w],
                                    [(panel[:, k + 4 * (b == 1), c * P:(c + 1) * P], src[:, k, 0:w]) for k in range(4)],
                                    prod)
                if l + 1 < DEPTH:
                    ada(l + 1, 12)
                    ada_turn(l + 1, ADA_FIRST - 1)
                for c in range(2):
                    free_bank((l, "out", c))
                streamed([bank_of((l, "out", c))[:, 0:w] for c in range(2)], w, (m_hi, m_lo), m_ready, DC * l)
                for p in range(1, 4):
                    std([(l, "out", 2 * p), (l, "out", 2 * p + 1)], w, (m_hi, m_lo), None, 0)
                sums((l, "norm", 2), w)
                ffn(l, 1, w, l + 1 if l + 1 < DEPTH else None, (3 * l + 2) * DC)

        @block.vector
        def _(dve):
            step = Steps(dve, dve_step)
            tt, ts, stt = dve.tensor_tensor, dve.tensor_scalar, dve.scalar_tensor_tensor

            def rest_of_panel(n, sb, kind, r, per):
                for part in range(2):
                    b = 2 * sb + part
                    dve.wait_ge(hi_ready, b + 1 + r * (2 * per))
                    tt(half_dest(w_lo, b, kind), half_source(n % RING, kind, part),
                       half_dest(w_hi, b, kind).bitcast(F32), ALU.subtract).then_inc(
                           panel_left[n % RING] if part else lo_first, 1)

            splits = Splits(rest_of_panel)

            def reciprocal_root(key, w=T, rows=slice(0, P)):
                n = units[key][0]
                r = rt[rows, n % 2, 0:w]
                dve.wait_ge(roots, n + 1)
                step(dve.reciprocal(r, r))
                step.wait()
                return r

            def norm(l, i, w):
                n = units[(l, "norm", i)][0]
                r = reciprocal_root((l, "norm", i), w)

                def rest(k):
                    dve.wait_ge(u_rounded, (3 * l + i) * DC + k + 1)
                    tt(u_lo[:, k, 0:w], sq[:, k % 4, 0:w], u_hi[:, k, 0:w].bitcast(F32),
                       ALU.subtract).then_inc(mod_done, 1)

                for k in range(DC + 2):
                    if 4 <= k < DC:
                        dve.wait_ge(mod_done, (3 * l + i) * DC + k - 3)
                    if k < DC:
                        tt(sq[:, k % 4, 0:w], h[:, k, 0:w], r, ALU.mult).then_inc(normed if k < DC - 1 else scaled, 1)
                    if k >= 2:
                        rest(k - 2)

            def modulations(l, part):
                a, b = (0, 24) if part == 0 else (24, 72)
                dve.wait_ge(ada_done, ADA_PANELS * l + (ADA_FIRST if part == 0 else ADA_PANELS))
                step(tt(mods[:, l, a:b, :], bank[7][:, 2 * a:2 * b].rearrange("p (c s) -> p c s", s=2),
                        mod_par[:, l, a:b].unsqueeze(2).to_broadcast([P, b - a, 2]), ALU.add))
                step.wait()
                for i in ((0,) if part == 0 else (1, 2)):
                    c = (3 * i + 1) * DC
                    step(stt(scales[:, l, i, :, :], mods[:, l, c:c + DC, :], 1.0,
                             mod_par[:, l, 72 + i * DC:72 + (i + 1) * DC].unsqueeze(2).to_broadcast([P, DC, 2]),
                             ALU.add, ALU.mult))
                c = (2 if part == 0 else 8) * DC
                step(ts(mods[:, l, c:c + DC, :], mods[:, l, c:c + DC, :], 0.5, None, ALU.mult))
                step.wait()
                dve.sem_inc(mods_ready, 1)

            def residual(key, l, i, j, w):
                wait_product(dve, key)
                for s, cols in halves(w):
                    last = stt(h[:, j, cols], bank_of(key)[:, cols], mods[:, l, (3 * i + 2) * DC + j, s:s + 1],
                               h[:, j, cols], ALU.mult, ALU.add)
                last.then_inc(drained["v"], 1)

            def ffn(l, f, w, carry):
                q0 = number[(l, "g", f, 0)]
                a0 = counts["a"][q0]
                h0 = FC * (2 * l + f)
                flat_hi = h_hi[:, :, :].rearrange("p n w -> p (n w)")
                flat_lo = h_lo[:, :, :].rearrange("p n w -> p (n w)")
                peel, body = (1, 2) if carry is not None else (2, 3)

                def pair(i, loop=None):
                    r = 0 if loop is None else loop
                    more = r * body
                    splits.next(3 if carry is not None else 2)
                    for c in range(2):
                        dve.wait_ge(prod, q0 + 4 * i + 3 + c + 4 * more)
                        dve.wait_ge(drained["a"], a0 + 2 * i + c + 1 + 2 * more)
                        tt(sg[:, c, 0:w], sg[:, c, 0:w], bank[(q0 + 2 + c) % 4][:, 0:w],
                           ALU.mult).then_inc(drained["v"], 1)
                    for c in range(2):
                        if loop is not None:
                            at = more * (2 * T) + (2 * i + c) * T
                            hi, lo = flat_hi[:, bass.ds(at, w)], flat_lo[:, bass.ds(at, w)]
                        else:
                            hi, lo = h_hi[:, 2 * i + c, 0:w], h_lo[:, 2 * i + c, 0:w]
                        dve.wait_ge(hidden_rounded, h0 + 2 * i + c + 1 + 2 * more)
                        tt(lo, sg[:, c, 0:w], hi.bitcast(F32), ALU.subtract).then_inc(hidden_ready, 1)

                splits.upto(START[l, "gu", f] + 1)
                for i in range(peel):
                    pair(i)
                n0, rounds = splits.n, (FC // 2 - peel) // body
                splits.per = body * (3 if carry is not None else 2)
                with dve.Fori(0, rounds) as r:
                    splits.r = r
                    for i in range(body):
                        pair(peel + i, r)
                splits.r, splits.n = 0, n0 + rounds * splits.per
                splits.per = 0
                n = START[l, "down", f]
                for g in range(4):
                    for s in range(3):
                        for part in range(2 if carry is not None else 1):
                            splits.upto(n + 2)
                            n += 1
                    for c in range(2):
                        residual((l, "down", f, 2 * g + c), l, 0 if f == 0 else 2, 2 * g + c, w)

            def rope(dst, source, at, out_sem):
                tmp = rsin[tail, at, 0:SEQ]
                step(tt(tmp, source, C("sin", tail), ALU.mult))
                step(tt(dst, dst, C("cos", tail), ALU.mult))
                step.wait()
                return tt(dst, dst, tmp, ALU.add).then_inc(out_sem, 1)

            dve.wait_ge(inputs_in, 16 * (DC + 3))
            dve.wait_ge(cond_ready, 1)
            tt(c4[:, :, 2:4], cond[:, :, :], c4[:, :, 0:2].bitcast(F32), ALU.subtract).then_inc(c_ready, 1)
            for p in range(ADA_FIRST):
                splits.upto(p + 2)
            modulations(0, 0)
            for l in range(DEPTH):
                w = width(l)
                nt = w // P
                norm(l, 0, T)
                ffn(l, 0, T, 0 if l == 0 else None)
                modulations(l, 1)
                norm(l, 1, T)

                for n in range(START[l, "gmu"], START[l, "low"]):
                    splits.upto(n + 2)
                dve.wait_ge(par_in, 16 * (l + 1))
                for t in range(nt):
                    wait_drained(dve, (l, "gmv", 1, t))
                    step(dve.bn_stats(stats, gv[:, t, :]))
                    step.wait()
                    step(dve.bn_aggr(mv[:, t, :], stats))
                    step.wait()
                dve.sem_inc(gmv_var, 1)
                dve.wait_ge(gmv_root, l + 1)
                step(dve.reciprocal(lnr[:, 0:nt], lnr[:, 0:nt]))
                step.wait()
                for t in range(nt):
                    last = ts(gv[:, t, :], gv[:, t, :], mv[:, t, 0:1], lnr[:, t:t + 1], ALU.subtract, ALU.mult)
                last.then_inc(gmv_norm, 1)

                for n in range(START[l, "low"], START[l, "ukv"]):
                    splits.upto(n + 2)
                wait_drained(dve, (l, "krope"))
                stt_w = par_of("qk_k", rows=tail)
                ts(krw[tail, 0, :], kr[tail, 0, :], stt_w, None, ALU.mult).then_inc(kr_ready, 1)
                dve.wait_ge(ab_turned, l + 1)
                dve.tensor_copy(gab, bank[6][:, 0:64].rearrange("p (t c) -> p t c", c=16)).then_inc(ab_read, 1)
                dve.wait_ge(ab_read, l + 1)
                step(tt(gab[:, :, 0:8], gab[:, :, 0:8], par_of("dt_bias").unsqueeze(1).to_broadcast([P, 4, 8]), ALU.add))
                step.wait()
                step(ts(t1, gab[:, :, 0:8], -1.0, None, ALU.mult))
                step.wait()
                tt(t1, t1, gab[:, :, 0:8], ALU.max).then_inc(dt_ready, 1)

                r = reciprocal_root((l, "cq"), w)
                for i in range(3):
                    last = stt(cq[:, i, 0:w], cq[:, i, 0:w], par_of("q_norm", i, i + 1), r, ALU.mult, ALU.mult)
                last.then_inc(scaled, 1)
                for c in range(GMC):
                    key = (l, "spatial", c)
                    wait_product(dve, key)
                    bias = par_of("gm_bs", c * P, (c + 1) * P).unsqueeze(1).to_broadcast([P, nt, P])
                    stt(gtmp[:, c % 2, 0:w].rearrange("p (t c) -> p t c", c=P),
                        bank_of(key)[:, 0:w].rearrange("p (t c) -> p t c", c=P),
                        par_of("gm_ln", c, c + 1), bias, ALU.mult, ALU.add).then_inc(drained["v"], 1)
                    wait_drained(dve, key)
                    step(tt(ya[:, c, 0:w], gtmp[:, c % 2, 0:w], ya[:, c, 0:w], ALU.mult))
                    step.wait()
                dve.sem_inc(ya_ready, 1)
                r = reciprocal_root((l, "ckv"))
                for i in range(2):
                    last = stt(ckv[:, i, :], ckv[:, i, :], par_of("kv_norm", i, i + 1), r, ALU.mult, ALU.mult)
                last.then_inc(scaled, 1)
                dve.wait_ge(kr_rot, l + 1)
                dve.wait_ge(kr_ready, l + 1)
                rope(krw[tail, 0, 0:SEQ], bank[6][tail, 0:SEQ], 0, krw_ready)
                dve.wait_ge(krw_ready, l + 1)
                for kind, ww in (("k", T), ("q", w)):
                    n = units[(l, kind)][0]
                    dve.wait_ge(roots, n + 1)
                    r = rt[0:MH, n % 2, 0:ww]
                    dve.reciprocal(r, r).then_inc(inverted, 1)
                for hd in range(MH):
                    key = (l, "k_spread", hd)
                    wait_product(dve, key)
                    r = bank_of(key)
                    stt(kk[0:NOPE, hd, :], kk[0:NOPE, hd, :], par_of("qk_k", rows=slice(0, NOPE)), r[0:NOPE, :],
                        ALU.mult, ALU.mult)
                    tt(kk[tail, hd, :], krw[tail, 0, :], r[tail, :], ALU.mult).then_inc(drained["v"], 1)
                wait_drained(dve, (l, "k_spread", MH - 1))
                dve.sem_inc(scaled, 1)
                for hd in range(MH):
                    key = (l, "q_spread", hd)
                    wait_product(dve, key)
                    stt(qq[0:QK, hd, 0:w], qq[0:QK, hd, 0:w], par_of("qk_q", rows=slice(0, QK)),
                        bank_of(key)[0:QK, 0:w], ALU.mult, ALU.mult).then_inc(drained["v"], 1)
                    wait_drained(dve, key)
                    dve.wait_ge(q_rot, MH * l + hd + 1)
                    rope(qq[tail, hd, 0:SEQ], bank[6][tail, 0:SEQ], hd % 2, q_ready)
                dve.sem_inc(scaled, 1)

                splits.upto(START[l, "qkv"] + 1)
                a0 = ATT[l]
                for i in range(nt * MH + 3):
                    if i < nt * MH:
                        a = a0 + i
                        s = a % 4
                        keys = slice(0, T) if i // MH < 2 else slice(0, CTX)
                        dve.wait_ge(att_s, a + 1)
                        if a >= 4:
                            dve.wait_ge(att_exp, a - 3)
                        step(dve.reduce_max(mx[:, s:s + 1], bank[S_BANKS[s]][:, keys], AX.X))
                        step.wait()
                        ts(nb[:, s:s + 1], mx[:, s:s + 1], -QK ** -0.5, None, ALU.mult).then_inc(att_max, 1)
                    if 0 < i <= nt * MH:
                        a = a0 + i - 1
                        s = a % 4
                        keys = slice(0, T) if (i - 1) // MH < 2 else slice(0, CTX)
                        dve.wait_ge(att_exp, a + 1)
                        step(dve.reciprocal(ri[:, s:s + 1], rs[:, s:s + 1]))
                        step.wait()
                        ts(pr[:, s, keys], pr[:, s, keys], ri[:, s:s + 1], None, ALU.mult).then_inc(att_p, 1)
                    if i > 2:
                        a = a0 + i - 3
                        t, hd = divmod(i - 3, MH)
                        rows = slice(NOPE * (hd % 2), NOPE * (hd % 2) + NOPE)
                        dve.wait_ge(att_o, a + 1)
                        dve.tensor_copy(yc[rows, hd // 2, t * P:(t + 1) * P], bank[6][rows, 0:P]).then_inc(att_y, 1)

                dve.wait_ge(dt_ln, l + 1)
                step(stt(g, gab[:, :, 0:8], 0.0, t1, ALU.max, ALU.add))
                step(ts(beta, beta, 1.0, None, ALU.add))
                step.wait()
                step(stt(g, g, -1.0, expa.unsqueeze(1).to_broadcast([P, 4, 8]), ALU.mult, ALU.mult))
                step(dve.reciprocal(beta, beta))
                step.wait()
                dve.sem_inc(g_ready, 1)

                dve.wait_ge(pads, l + 1)
                for c in range(12):
                    if c % 2 == 0:
                        splits.upto(START[l, "qkv"] + c // 2 + 2)
                    wait_drained(dve, (l, "qkv", c))
                    if 12 * l + c >= 2:
                        dve.wait_ge(conv_silu, 12 * l + c - 1)
                    a = acc[:, c % 2, :].rearrange("p (s w) -> p s w", s=2)
                    for tap in range(5):
                        src = convin[:, c % 3, :, tap:tap + SEQ]
                        wt = par_of("conv", 5 * c + tap, 5 * c + tap + 1)
                        if tap == 0:
                            step(ts(a, src, wt, None, ALU.mult))
                        elif tap < 4:
                            step(stt(a, src, wt, a, ALU.mult, ALU.add))
                        else:
                            stt(a, src, wt, a, ALU.mult, ALU.add).then_inc(conv_done, 1)
                        if tap < 4:
                            step.wait()
                for i in range(8):
                    r = reciprocal_root((l, "qk", i))
                    if i < 4:
                        tt(kT[:, i, :], kT[:, i, :], r, ALU.mult).then_inc(scaled, 1)
                    else:
                        stt(qT[:, i - 4, :], qT[:, i - 4, :], float(P) ** -0.5, r, ALU.mult, ALU.mult).then_inc(scaled, 1)
                dve.wait_ge(scaled, units[(l, "qk", 7)][0] + 1)
                dve.wait_ge(tok_c, 8 * (l + 1))

                def per_head(x):
                    return x.unsqueeze(2).to_broadcast([P, HEADS, P])

                for j in range(4):
                    it = l * 4 + j
                    tiles = [ORDER[d][j] for d in range(2)]
                    for d in range(2):
                        dve.wait_ge(ddve[d], it * D_DVE) if it else None
                        dve.tensor_copy(heads(gB[:, d, :]), per_head(g[:, tiles[d], 4 * d:4 * d + 4])).then_inc(ddve[d], 1)
                    for d in range(2):
                        A = heads(bank[3 * d][:, :])
                        end = P - 1 if d == 0 else 0
                        dve.wait_ge(dpe[d], it * D_PE + 1)
                        step(dve.tensor_copy(gamc[:, d, :], bank[6][:, 4 * d:4 * d + 4]))
                        step.wait()
                        step(tt(heads(E[:, d, :]), A, per_head(gamc[:, d, :]), ALU.subtract))
                        step(tt(kds[:, d, :], A[:, :, end], gamc[:, d, :], ALU.subtract))
                        step.wait()
                        ts(E[:, d, :], E[:, d, :], 0.0, None, ALU.min).then_inc(ddve[d], 1)
                        dve.wait_ge(ddve[d], it * D_DVE + 2)
                        dve.sem_inc(ddve[d], 1)
                    for d in range(2):
                        dve.wait_ge(dpe[d], it * D_PE + 2)
                        dve.wait_ge(dpool[d], it * D_POOL + 1)
                        tt(att[:, d, :], bank[3 * d + 2][:, :], E[:, d, :], ALU.mult).then_inc(ddve[d], 1)
                        step(tt(mt[:, d, :], bank[3 * d + 1][:, :], E[:, d, :], ALU.mult))
                        step.wait()
                        tt(heads(mt[:, d, :]), heads(mt[:, d, :]), per_head(beta[:, tiles[d], 4 * d:4 * d + 4]),
                           ALU.mult).then_inc(ddve[d], 1)
                    for d in range(2):
                        dve.wait_ge(dpool[d], it * D_POOL + 2)
                        tt(heads(XT[:, d, :]), ident.unsqueeze(1).to_broadcast([P, HEADS, P]), heads(ml[:, d, :]),
                           ALU.subtract).then_inc(ddve[d], 1)
                    for d in range(2):
                        end = P - 1 if d == 0 else 0
                        qs = qT[:, :, tiles[d] * P:(tiles[d] + 1) * P]
                        dve.wait_ge(dact[d], it * D_ACT + 3)
                        step(dve.tensor_copy(eL[:, d, :], heads(EG[:, d, :])[:, :, end]))
                        step.wait()
                        tt(heads(EG[:, d, :]), heads(EG[:, d, :]), qs, ALU.mult).then_inc(ddve[d], 1)
                        tt(heads(kg[:, d, :]), heads(ktok[:, tiles[d], :]), per_head(egam[:, d, :]),
                           ALU.mult).then_inc(ddve[d], 1)
                    for n in range(1, LEVELS):
                        for d in range(2):
                            dve.wait_ge(dpe[d], it * D_PE + 3 + 2 * n)
                            if n < LEVELS - 1:
                                step(tt(X[:, d, :], X[:, d, :], bank[3 * d + 1][:, :], ALU.subtract))
                            tt(XT[:, d, :], XT[:, d, :], bank[3 * d + 2][:, :], ALU.subtract).then_inc(ddve[d], 1)
                    for d in range(2):
                        step(tt(heads(kd[:, d, :]), heads(ktok[:, tiles[d], :]), per_head(kds[:, d, :]), ALU.mult))
                        dve.wait_ge(dpe[d], it * D_PE + 17)
                        tt(heads(vnew[:, d, :]), heads(bank[3 * d + 1][:, :]),
                           per_head(beta[:, tiles[d], 4 * d:4 * d + 4]), ALU.mult).then_inc(ddve[d], 1)
                    for d in range(2):
                        dve.wait_ge(dpe[d], it * D_PE + 18)
                        t = tiles[d]
                        last = None
                        if t < nt:
                            out = yb[:, :, t * P:(t + 1) * P]
                            o = heads(bank[3 * d][:, :])
                            if j % 2 == 0:
                                last = dve.tensor_copy(out, o)
                            else:
                                last = tt(out, out, o, ALU.add)
                        if j < 3:
                            if last is not None:
                                step(last)
                            if j:
                                step(tt(heads(S[:, d, :]), heads(S[:, d, :]), per_head(eL[:, d, :]), ALU.mult))
                                step.wait()
                                last = tt(S[:, d, :], S[:, d, :], bank[3 * d + 2][:, :], ALU.add)
                            else:
                                last = dve.tensor_copy(S[:, d, :], bank[3 * d + 2][:, :])
                        last.then_inc(ddve[d], 1)
                    for d in range(2):
                        dve.wait_ge(ddve[d], (it + 1) * D_DVE)

                for i in range(4):
                    r = reciprocal_root((l, "o", i), w)
                    stt(yb[:, i, 0:w], yb[:, i, 0:w], par_of("dn_out"), r, ALU.mult, ALU.mult).then_inc(scaled, 1)
                for p in range(2):
                    splits.upto(START[l, "z"] + p + 2)
                dve.wait_ge(scaled, units[(l, "o", 3)][0] + 1)
                wait_drained(dve, (l, "z", 3))
                tt(yb[:, :, 0:w], yb[:, :, 0:w], zs[:, :, 0:w], ALU.mult).then_inc(yb_ready, 1)

                for pair in range(DC // 2):
                    n = START[l, "merge", pair]
                    for b in range(6 if l + 1 < DEPTH else 3):
                        splits.upto(n + 2)
                        n += 1
                    for b in range(3):
                        for c in range(2):
                            key = (l, "branch", 2 * pair + c, b)
                            wait_product(dve, key)
                            wait_drained(dve, (l, "gate", 2 * pair + c, b))
                            m = macc[:, c, 0:w]
                            dst = m if b == 0 else mtmp[:, c, 0:w]
                            tt(dst, sig[:, 2 * b + c, 0:w], bank_of(key)[:, 0:w], ALU.mult).then_inc(drained["v"], 1)
                            if b:
                                wait_drained(dve, key)
                                last = tt(m, m, mtmp[:, c, 0:w], ALU.add)
                                if b == 1:
                                    step(last)
                                    step.wait()
                                else:
                                    last.then_inc(m_added, 1)
                    n += 2
                    splits.upto(n + 1 + (pair == 3 and l + 1 < DEPTH))
                    for c in range(2):
                        j = 2 * pair + c
                        dve.wait_ge(m_rounded, DC * l + j + 1)
                        tt(m_lo[:, j, 0:w], macc[:, c, 0:w], m_hi[:, j, 0:w].bitcast(F32),
                           ALU.subtract).then_inc(m_ready, 1)
                if l + 1 < DEPTH:
                    modulations(l + 1, 0)
                for j in range(DC):
                    if j % 2 == 0:
                        splits.upto(START[l, "out"] + j // 2 + 2)
                    residual((l, "out", j), l, 1, j, w)
                norm(l, 2, w)
                ffn(l, 1, w, l + 1 if l + 1 < DEPTH else None)


_NAMES = ("wts", "par", "cst", "mod", "x", "c")


def kernel(**inputs):
    import concourse.bacc as bacc
    from concourse.bass_utils import run_bass_kernel_spmd

    inp = {k: np.asarray(v) for k, v in inputs.items()}
    arrays = {
        "wts": stream(inp),
        "par": params(inp),
        "cst": constants(),
        "mod": np.ascontiguousarray(modulation_params(inp)),
        "x": np.ascontiguousarray(np.concatenate([inp["x"][0].T, inp["ctx"][0].T], axis=1)),
        "c": np.ascontiguousarray(np.stack([inp["c"][0], inp["c_ctx"]], axis=-1).reshape(DC, P, 2).transpose(1, 0, 2)),
    }
    nc = bacc.Bacc("TRN2", target_bir_lowering=False, num_devices=1, dynamic_dma_scratch_size=1024)
    args = [nc.dram_tensor("in_" + n, arrays[n].shape, F32, kind="ExternalInput").ap() for n in _NAMES]
    args.append(nc.dram_tensor("out", (D, SEQ), F32, kind="ExternalOutput").ap())
    backbone(nc, *args)
    r = run_bass_kernel_spmd(nc, [{"in_" + n: arrays[n] for n in _NAMES}], core_ids=[0])
    return np.asarray(r.results[0]["out"]).T.reshape(1, SEQ, D)
```

```python
from contextlib import ExitStack

import numpy as np

import concourse.bass as bass
from concourse import mybir

F32 = mybir.dt.float32
F32R = mybir.dt.float32r
ACT = mybir.ActivationFunctionType
ALU = mybir.AluOpType
AX = mybir.AxisListType

P = 128
D = 1024
DC = D // P
SEQ = 256
CTX = 256
T = SEQ + CTX
DEPTH = 2
FFN = 2816
FC = FFN // P
EPS = 1e-6
GMW = 512
GMC = GMW // P
HEADS = 4
MH = 8
NOPE = 64
ROPE = 32
QK = NOPE + ROPE
LQ = 384
LKV = 256
GRID_W = 64
LEVELS = 7
UNIT = 256
PANEL = 8 * UNIT
RING = 3
HALF = PANEL // 2
HALVES = 3
ADA_PANELS = 36
ADA_FIRST = 8
ADA_PAIR = 2

PAR = {}
_at = 0
for _name, _n in (("gm_ln", 4), ("conv", 60),
                  ("dn_out", 1), ("q_norm", 3), ("kv_norm", 2), ("qk_q", 1), ("qk_k", 1),
                  ("dt_bias", 8), ("a_log", 8), ("gm_bs", 512), ("gm_ws", 512)):
    PAR[_name] = (_at, _n)
    _at += _n
NPAR = _at
CST = {}
_at = 0
for _name, _n in (("ident", 128), ("upto", 128), ("from", 128), ("not_upto", 128), ("not_from", 128),
                  ("ones", 128), ("level", LEVELS * 128),
                  ("cos", 256), ("sin", 256), ("rot", 32), ("fold", 2), ("pick", 63)):
    CST[_name] = (_at, _n)
    _at += _n
NCST = _at


def constants():
    c = np.zeros((P, NCST), np.float32)

    def put(name, a, rows=slice(0, P)):
        at, n = CST[name]
        c[rows, at:at + n] = a.reshape(a.shape[0], n)

    i = np.arange(P)
    put("ident", np.eye(P, dtype=np.float32))
    put("upto", (i[:, None] <= i[None, :]).astype(np.float32))
    put("from", (i[:, None] >= i[None, :]).astype(np.float32))
    put("not_upto", np.where(i[:, None] <= i[None, :], 0.0, -30000.0).astype(np.float32))
    put("not_from", np.where(i[:, None] >= i[None, :], 0.0, -30000.0).astype(np.float32))
    put("ones", np.ones((P, P), np.float32))
    lev = np.zeros((P, LEVELS, P), np.float32)
    for n in range(LEVELS):
        b = 1 << n
        lev[:, n, :] = (i[:, None] // (2 * b) == i[None, :] // (2 * b)) & (i[:, None] // b != i[None, :] // b)
    put("level", lev)
    pos = np.arange(SEQ)
    half = ROPE // 2
    freq = (1.0 / (np.float32(10000.0) ** (np.arange(0, half, 2, dtype=np.float32) / np.float32(half)))).astype(np.float32)
    row = (pos // GRID_W).astype(np.float32)[:, None] * freq
    col = (pos % GRID_W).astype(np.float32)[:, None] * freq
    ang = np.concatenate([row, row, col, col], axis=-1)
    tail = slice(NOPE, QK)
    put("cos", np.cos(ang).astype(np.float32).T, tail)
    put("sin", np.sin(ang).astype(np.float32).T, tail)
    rot = np.zeros((ROPE, ROPE), np.float32)
    q = half // 2
    for base in (0, half):
        for m in range(q):
            rot[base + q + m, base + m] = -1.0
            rot[base + m, base + q + m] = 1.0
    put("rot", rot, tail)
    pick = np.zeros((P, 63), np.float32)
    pick[:, 31] = 1.0
    put("pick", pick)
    put("fold", np.concatenate([np.eye(2), np.eye(2)]).astype(np.float32), slice(0, 4))
    return c


def stream(inp):
    out, pending = [], []

    def rows(w, cols):
        w = w[:, cols]
        return w.reshape(w.shape[0] // P, P, w.shape[1]).transpose(1, 0, 2)

    def half(a):
        if pending:
            out.append(np.concatenate([pending.pop(), a.reshape(P, -1)], axis=1))
        else:
            pending.append(a.reshape(P, -1))

    def put(*parts):
        assert not pending
        panel = np.zeros((P, PANEL), np.float32)
        at = 0
        for part in parts:
            flat = part.reshape(P, -1)
            panel[:, at:at + flat.shape[1]] = flat
            at += flat.shape[1]
        out.append(panel)

    def chunk(w, c0):
        a = rows(w, slice(c0, c0 + P))
        full = np.zeros((P, 8, P), np.float32)
        full[:, :a.shape[1], :a.shape[2]] = a
        half(full)

    def std(w, c0):
        chunk(w, c0)
        chunk(w, c0 + P)

    def ada_half(l, n):
        p, part = divmod(n, 2)
        half(rows(inp["ada_w"][l][part * 512:(part + 1) * 512], slice(p * UNIT, (p + 1) * UNIT)))

    def ada(l, p):
        ada_half(l, 2 * p)
        ada_half(l, 2 * p + 1)

    def ffn(l, f, carry):
        gu, down = inp[f"ffn{f + 1}_w_gu"][l], inp[f"ffn{f + 1}_w_down"][l]
        a = 2 * ADA_FIRST
        for i in range(FC // 2):
            mains = [2 * i * P, (2 * i + 1) * P, FFN + 2 * i * P, FFN + (2 * i + 1) * P]
            if carry is None:
                order = mains
            elif i == 0:
                order = mains[:2] + [None, mains[2], None, mains[3], None, None]
            else:
                order = [o for m in mains for o in (m, None)]
            for o in order:
                if o is None:
                    ada_half(carry, a)
                    a += 1
                else:
                    chunk(gu, o)
        for g in range(4):
            for s in range(3):
                for c in range(2):
                    chunk(down[s * D:(s + 1) * D], (2 * g + c) * P)
                    if c == 0 and carry is not None:
                        ada_half(carry, a)
                        a += 1
        assert carry is None or a == 2 * ADA_PANELS

    for p in range(ADA_FIRST):
        ada(0, p)
    for l in range(DEPTH):
        ffn(l, 0, 0 if l == 0 else None)
        w = inp["w_in"][l]
        for i in range(2):
            std(w, i * UNIT)
        for i in range(2, 4):
            for part in range(2):
                half(rows(w[part * 512:(part + 1) * 512], slice(i * UNIT, (i + 1) * UNIT)))
        o = 2 * GMW + 4 * 512 + 16
        ab, cq, ckv = 2 * GMW + 4 * 512, o, o + LQ
        gates = ckv + LKV + ROPE
        last = np.zeros((D, UNIT), np.float32)
        last[:, 0:128] = w[:, ckv + 128:ckv + 256]
        last[:, 128:128 + ROPE] = w[:, ckv + 256:ckv + 256 + ROPE]
        last[:, 128 + ROPE:128 + ROPE + 16] = w[:, ab:ab + 16]
        chunk(w, ckv)
        std(last, 0)
        for c0 in (cq, cq + 128, cq + 256):
            chunk(w, c0)
        uq, ukv = inp["mla_w_uq"][l], inp["mla_w_ukv"][l]
        h = np.arange(MH)[:, None] * 128
        put(rows(ukv, np.concatenate([(h + np.arange(64)).ravel(), (h + 64 + np.arange(64)).ravel()])))
        put(rows(uq, slice(0, 4 * QK)))
        put(rows(uq, slice(4 * QK, 8 * QK)))
        for i in range(6):
            std(w, 2 * GMW + i * UNIT)
        for i in range(2):
            std(w, 2 * GMW + 1536 + i * UNIT)
        for g in range(4):
            cols = slice(g * UNIT, (g + 1) * UNIT)
            for b in range(3):
                for c in range(2):
                    chunk(w, gates + b * D + g * UNIT + c * P)
                    if b < 2 and l + 1 < DEPTH:
                        ada_half(l + 1, 4 * g + 2 * b + c)
            for b in ("gm", "dn", "mla"):
                half(rows(inp["w_branch_" + b][l], cols))
        for g in range(4):
            std(inp["w_out"][l], g * UNIT)
        ffn(l, 1, l + 1 if l + 1 < DEPTH else None)
    return np.stack(out)


def params(inp):
    out = np.zeros((P, DEPTH, NPAR), np.float32)

    def feat(v):
        return v.reshape(-1, P).T

    for l in range(DEPTH):
        def put(name, a, rows=slice(0, P)):
            at, n = PAR[name]
            out[rows, l, at:at + n] = a.reshape(a.shape[0], n)

        put("gm_ln", feat(inp["gm_ln"][l]))
        put("conv", inp["dn_conv"][l].reshape(5, 12, P).transpose(2, 1, 0))
        put("dn_out", feat(inp["dn_out_norm"][l]))
        put("q_norm", feat(inp["mla_q_norm"][l]))
        put("kv_norm", feat(inp["mla_kv_norm"][l]))
        put("qk_q", inp["mla_qk_norm_q"][l][:, None], slice(0, QK))
        put("qk_k", inp["mla_qk_norm_k"][l][:, None], slice(0, QK))
        put("dt_bias", np.broadcast_to(inp["dn_dt_bias"][l].reshape(1, 8), (P, 8)))
        put("a_log", np.broadcast_to(inp["dn_a_log"][l].reshape(1, 8), (P, 8)))
        put("gm_bs", np.broadcast_to(inp["gm_bs"][l].reshape(1, 512), (P, 512)))
        put("gm_ws", inp["gm_ws"][l].transpose(2, 0, 1))
    return out.reshape(P, DEPTH * NPAR)


def modulation_params(inp):
    both = [np.concatenate([inp["ada_b"][l], inp["ffn1_norm"][l], inp["mix_norm"][l], inp["ffn2_norm"][l]])
            for l in range(DEPTH)]
    return np.stack(both).reshape(DEPTH, 96, P).transpose(2, 0, 1)


def panel_kinds():
    out, start = ["split"] * ADA_FIRST, {}

    def ffn(l, f, carry):
        start[l, "gu", f] = len(out)
        out.extend(["split"] * (FC // 2 * (2 + ADA_PAIR * carry)))
        start[l, "down", f] = len(out)
        out.extend(["split"] * (12 + 6 * carry))

    for l in range(DEPTH):
        more = l + 1 < DEPTH
        ffn(l, 0, l == 0)
        for stage, kind, n in (("gmu", "split", 2), ("gmv", "split", 2), ("low", "split", 3), ("ukv", "raw", 1),
                               ("uq", "raw", 2), ("qkv", "split", 6), ("z", "split", 2)):
            start[l, stage] = len(out)
            out.extend([kind] * n)
        start[l, "merge"] = len(out)
        out.extend(["split"] * (4 * (9 + 4 * more) // 2))
        start[l, "out"] = len(out)
        out.extend(["split"] * 4)
        ffn(l, 1, more)
    return out, start


KINDS, START = panel_kinds()
N_PANELS = len(KINDS)


def product_owners():
    number, owner = {}, []

    def add(key, who):
        number[key] = len(owner)
        owner.append(who)

    for l in range(DEPTH):
        nt = 4 if l + 1 < DEPTH else 2
        for f in range(2):
            if f == 1:
                for c in range(GMC):
                    add((l, "gmu", c), "a")
                for p in range(2):
                    for t in range(nt):
                        add((l, "gmv", p, t), "a")
                for c in range(2):
                    add((l, "ckv", c), "a")
                add((l, "krope"), "a")
                for c in range(3):
                    add((l, "cq", c), "a")
                for c in range(4):
                    add((l, "nope", c), "a")
                for t in range(4):
                    add((l, "mv", t), "a")
                for c in range(GMC):
                    add((l, "spatial", c), "v")
                for h in range(MH):
                    add((l, "uq", h), "a")
                for kind in ("k_spread", "q_spread"):
                    for h in range(MH):
                        add((l, kind, h), "v")
                for c in range(12):
                    add((l, "qkv", c), "a")
                for c in range(4):
                    add((l, "z", c), "a")
                for pair in range(DC // 2):
                    for kind, who in (("gate", "a"), ("branch", "v")):
                        for b in range(3):
                            for j in (2 * pair, 2 * pair + 1):
                                add((l, kind, j, b), who)
                for j in range(DC):
                    add((l, "out", j), "v")
            for i in range(FC // 2):
                for c in (2 * i, 2 * i + 1):
                    add((l, "g", f, c), "a")
                for c in (2 * i, 2 * i + 1):
                    add((l, "u", f, c), "v")
            for j in range(DC):
                add((l, "down", f, j), "v")
    counts = {"a": [0], "v": [0]}
    for who in owner:
        for k in "av":
            counts[k].append(counts[k][-1] + (who == k))
    return number, owner, counts


def backbone(nc, wts, par_d, cst_d, mod_d, x_d, c_d, out_d):
    number, owner, counts = product_owners()
    split_before = np.cumsum([0] + [k != "raw" for k in KINDS]).tolist()
    with ExitStack() as ctx:
        def sb(name, shape, dt=F32):
            return ctx.enter_context(nc.sbuf_tensor(name, shape, dt))

        def sem(name):
            return ctx.enter_context(nc.semaphore(name))

        ring = sb("ring", [P, RING * PANEL])
        w_hi = sb("w_hi", [P, HALVES, HALF], F32R)
        w_lo = sb("w_lo", [P, HALVES, HALF], F32R)
        h = sb("h", [P, DC, T])
        u_hi = sb("u_hi", [P, DC, T], F32R)
        u_lo = sb("u_lo", [P, DC, T], F32R)
        sq = sb("sq", [P, 4, T])
        rt = sb("rt", [P, 2, T])
        par = sb("par", [P, NPAR])
        cst = sb("cst", [P, NCST])
        cond = sb("cond", [P, DC, 2])
        c4 = sb("c4", [P, DC, 4], F32R)
        ada_rows = sb("ada_rows", [4, UNIT])
        mod_par = sb("mod_par", [P, DEPTH, 96])
        mods = sb("mods", [P, DEPTH, 72, 2])
        scales = sb("scales", [P, DEPTH, 3, DC, 2])
        small = sb("small", [P, 256])

        SLOT = T * 4
        base = -(-nc.sbuf_base // 32) * 32
        sb("arena", [P, 48 * T])

        def at(name, slot, n, dt=F32):
            return nc.alloc_sbuf_tensor_at(name, [P, n, T], dt, offset=base + slot * SLOT)

        h_hi = at("hidden_hi", 0, FC, F32R)
        h_lo = at("hidden_lo", FC, FC, F32R)
        sg = at("sg", 2 * FC, 2)
        work = nc.alloc_sbuf_tensor_at("work", [P, 36 * T], F32, offset=base)
        ya, yb, yc = at("ya", 36, 4), at("yb", 40, 4), at("yc", 44, 4)
        m_hi = at("m_hi", 0, DC, F32R)
        m_lo = at("m_lo", DC, DC, F32R)

        def view(at, n, w=T):
            return work[:, at * T:at * T + n * w].rearrange("p (n w) -> p n w", w=w)

        gv = view(29, 4)
        gtmp = view(33, 2)
        cq = view(0, 3)
        ckv = view(3, 2)
        kr = view(5, 1)
        krw = view(6, 1)
        rsin = view(7, 2)
        kk = view(9, MH)
        qq = view(9 + MH, MH)
        vm = view(25, 4)
        pr = view(29, 4)
        prT = view(33, 2)
        qT = view(0, 4)
        kT = view(4, 4)
        ktok = view(8, 4)
        vtok = view(12, 4)
        S = view(16, 2)
        E = view(18, 2)
        EG = view(20, 2)
        att = view(22, 2)
        mt = view(24, 2)
        ml = view(26, 2)
        X = view(28, 2)
        XT = view(30, 2)
        Y = view(32, 2)
        gB = view(34, 2)
        vnew, nwT, kd, kg = mt, X, Y, gB
        vT = view(32, 2)
        acc = view(26, 4)
        CONV = 16 * T
        convin = work[:, CONV:CONV + 3 * 520].rearrange("p (n s w) -> p n s w", n=3, s=2)
        sig = view(16, 6)
        macc = view(22, 2)
        mtmp = sq[:, 0:2, :]
        y_hi = [at(f"y{b}_hi", 24 + 4 * b, 4, F32R) for b in range(3)]
        y_lo = [at(f"y{b}_lo", 36 + 4 * b, 4, F32R) for b in range(3)]
        qk_sq = view(22, 4)
        o_sq = view(0, 4)

        gab = small[:, 0:64].rearrange("p (t c) -> p t c", c=16)
        g = small[:, 64:96].rearrange("p (t c) -> p t c", c=8)
        beta = small[:, 96:128].rearrange("p (t c) -> p t c", c=8)
        t1 = small[:, 128:160].rearrange("p (t c) -> p t c", c=8)
        expa = small[:, 160:168]
        gamc = small[:, 168:176].rearrange("p (d c) -> p d c", c=4)
        egam = small[:, 176:184].rearrange("p (d c) -> p d c", c=4)
        kds = small[:, 184:192].rearrange("p (d c) -> p d c", c=4)
        mx = small[:, 192:196]
        nb = small[:, 196:200]
        eL = small[:, 220:228].rearrange("p (d c) -> p d c", c=4)
        rs = small[:, 232:236]
        ri = small[:, 236:240]
        stats = small[:, 200:206]
        mv = small[:, 208:216].rearrange("p (t c) -> p t c", c=2)
        lnr = small[:, 216:220]
        eps = small[:, 228:229]

        bank = [ctx.enter_context(nc.psum_tensor(f"bank{i}", [P, 512], F32)) for i in range(8)]

        def C(name, rows=slice(0, P)):
            at, n = CST[name]
            return cst[rows, at:at + n]

        def par_of(name, a=0, b=None, rows=slice(0, P)):
            at, n = PAR[name]
            return par[rows, at + a:at + (n if b is None else b)]

        ident, ones = C("ident"), C("ones")
        tail = slice(NOPE, QK)

        def heads(ap):
            return ap.rearrange("p (h c) -> p h c", h=HEADS)

        cond_in = sem("cond_in")
        inputs_in = sem("inputs_in")
        par_in = sem("par_in")
        panel_in = [sem(f"panel_in{i}") for i in range(RING)]
        panel_left = [sem(f"panel_left{i}") for i in range(RING)]
        half_used = sem("half_used")
        weights_rounded = sem("weights_rounded")
        first_rest_ready = sem("first_rest_ready")
        c_split = sem("c_split")
        ada_product = sem("ada_product")
        ada_copied = sem("ada_copied")
        u_rounded = sem("u_rounded")
        hidden_rounded = sem("hidden_rounded")
        hidden_ready = sem("hidden_ready")
        ab_turned = sem("ab_turned")
        ab_read = sem("ab_read")
        m_added = sem("m_added")
        y_rounded = sem("y_rounded")
        y_rest_ready = sem("y_rest_ready")
        m_rounded = sem("m_rounded")
        cond_ready = sem("cond_ready")
        ada_done = sem("ada_done")
        mods_ready = sem("mods_ready")
        product_made = sem("product_made")
        drained = {"a": sem("drained_by_act"), "v": sem("drained_by_dve")}
        squares = sem("squares")
        summed = sem("summed")
        roots = sem("roots")
        root_used = sem("root_used")
        chunk_scaled = sem("chunk_scaled")
        u_rest_ready = sem("u_rest_ready")
        gmv_normed = sem("gmv_normed")
        gmv_stats_ready = sem("gmv_stats_ready")
        gmv_root_ready = sem("gmv_root_ready")
        ya_ready = sem("ya_ready")
        borders_zeroed = sem("borders_zeroed")
        key_rope_weighted = sem("key_rope_weighted")
        key_rope_rotated = sem("key_rope_rotated")
        key_rope_ready = sem("key_rope_ready")
        query_rotated = sem("query_rotated")
        query_ready = sem("query_ready")
        head_roots_inverted = sem("head_roots_inverted")
        att_scored = sem("att_scored")
        att_max = sem("att_max")
        att_exp = sem("att_exp")
        att_normed = sem("att_normed")
        att_turned = sem("att_turned")
        att_turned_kept = sem("att_turned_kept")
        att_valued = sem("att_valued")
        att_kept = sem("att_kept")
        conv_done = sem("conv_done")
        conv_silu = sem("conv_silu")
        tokens_turned = sem("tokens_turned")
        tokens_kept = sem("tokens_kept")
        softplus_ready = sem("softplus_ready")
        softplus_log = sem("softplus_log")
        decays_ready = sem("decays_ready")
        dpe = [sem(f"delta_product{d}") for d in range(2)]
        dact = [sem(f"delta_act{d}") for d in range(2)]
        ddve = [sem(f"delta_dve{d}") for d in range(2)]
        dpool = [sem(f"delta_pool{d}") for d in range(2)]
        decays_spread = [sem(f"decays_spread{d}") for d in range(2)]
        x_updated = [sem(f"x_updated{d}") for d in range(2)]
        m_rest_ready = sem("m_rest_ready")
        yb_ready = sem("yb_ready")
        eps_ready = sem("eps_ready")
        act_step = sem("act_step")
        dve_step = sem("dve_step")
        out_done = sem("out_done")
        ATT = [0, 4 * MH]
        S_BANKS = (0, 1, 4, 5)

        class Steps:

            def __init__(self, eng, s):
                self.eng, self.s, self.n = eng, s, 0

            def __call__(self, ins):
                ins.then_inc(self.s, 1)
                self.n += 1
                return self.n

            def wait(self, n=None):
                self.eng.wait_ge(self.s, self.n if n is None else n)

        def unit_plan():
            plan, n, m = {}, 0, 0

            def add(key, k):
                nonlocal n, m
                plan[key] = (n, m, k)
                n += 1
                m += k

            for l in range(DEPTH):
                add((l, "norm", 0), 2)
                add((l, "norm", 1), 2)
                add((l, "ckv"), 2)
                add((l, "cq"), 3)
                add((l, "k"), MH)
                add((l, "q"), MH)
                for c in range(8):
                    add((l, "qk", c), 1)
                for c in range(4):
                    add((l, "o", c), 1)
                add((l, "norm", 2), 2)
            return plan

        units = unit_plan()
        units_width = {(l, "norm", i): T if i < 2 or l + 1 < DEPTH else SEQ for l in range(DEPTH) for i in range(3)}

        def width(l):
            return T if l + 1 < DEPTH else SEQ

        def halves(nt):
            return [(0, slice(0, SEQ)), (1, slice(SEQ, T))][:nt // SEQ]

        def count_after(q, who):
            return counts[who][q + 1]

        def wait_drained(eng, key):
            q = number[key] if isinstance(key, tuple) else key
            eng.wait_ge(drained[owner[q]], count_after(q, owner[q]))

        def wait_product(eng, key):
            eng.wait_ge(product_made, number[key] + 1)

        def bank_of(key):
            return bank[number[key] % 4]

        ORDER = [[2, 3, 0, 1], [3, 2, 1, 0]]
        D_PE, D_ACT, D_DVE, D_POOL = 18, 11, 16, 6
        block = ctx.enter_context(nc.Block())

        def half_source(slot, part):
            at = slot * PANEL + part * HALF
            return ring[:, at:at + HALF]

        class Splits:

            def __init__(self, one):
                self.one, self.n, self.r, self.per = one, 0, 0, 0

            def next(self, count=1):
                for _ in range(count):
                    while self.n < N_PANELS and KINDS[self.n] == "raw":
                        self.n += 1
                    if self.n >= N_PANELS:
                        return
                    self.one(self.n, split_before[self.n], self.r, self.per)
                    self.n += 1

            def past(self, start, half):
                self.upto(START[start] + half // 2 + 2)

            def upto(self, n):
                while self.n < min(n, N_PANELS):
                    if KINDS[self.n] == "raw":
                        self.n += 1
                    else:
                        self.next()

        @block.sync
        def _(sp):
            sp.dma_start(cond[:, :, :], c_d).then_inc(cond_in, 16)
            rounds = N_PANELS // RING
            for i in range(RING):
                sp.dma_start(ring[:, i * PANEL:(i + 1) * PANEL], wts[i]).then_inc(panel_in[i], 16)
            sp.dma_start(cst[:, :], cst_d).then_inc(inputs_in, 16)
            for k in range(DC):
                sp.dma_start(h[:, k, :], x_d[k * P:(k + 1) * P, :]).then_inc(inputs_in, 16)
            sp.dma_start(mod_par[:, :, :], mod_d).then_inc(inputs_in, 16)
            with sp.Fori(1, rounds) as r:
                for i in range(RING):
                    sp.wait_ge(panel_left[i], r)
                    sp.dma_start(ring[:, i * PANEL:(i + 1) * PANEL],
                                 wts[bass.ds(r * RING + i, 1)].rearrange("o p n -> p (o n)")).then_inc(panel_in[i], 16)
            for n in range(rounds * RING, N_PANELS):
                i = n % RING
                sp.wait_ge(panel_left[i], n // RING)
                sp.dma_start(ring[:, i * PANEL:(i + 1) * PANEL], wts[n]).then_inc(panel_in[i], 16)
            last = DEPTH - 1
            for j in range(DC):
                wait_drained(sp, (last, "down", 1, j))
                sp.dma_start(out_d[j * P:(j + 1) * P, :], h[:, j, 0:SEQ]).then_inc(out_done, 16)
            sp.wait_ge(out_done, 16 * DC)

        @block.gpsimd
        def _(pool):
            pool.memset(eps, EPS).then_inc(eps_ready, 1)
            pool.wait_ge(inputs_in, 16 * (DC + 2))
            for l in range(DEPTH):
                pool.wait_ge(att_kept, ATT[l] + width(l) // P * MH)
                for a in (0, 258):
                    last = pool.memset(convin[:, :, :, a:a + 2], 0.0)
                last.then_inc(borders_zeroed, 1)
                for j in range(4):
                    it = l * 4 + j
                    for n in range(1, LEVELS):
                        for d in range(2):
                            if n == 1:
                                pool.wait_ge(ddve[d], it * D_DVE + 3)
                            elif n == 2:
                                pool.wait_ge(ddve[d], it * D_DVE + 5)
                            else:
                                pool.wait_ge(dpe[d], it * D_PE + 2 + 2 * (n - 2))
                            dst = (ml if n % 2 else E)[:, d, :]
                            mask = C("level")[:, n * P:(n + 1) * P].unsqueeze(1).to_broadcast([P, HEADS, P])
                            pool.tensor_tensor(heads(dst), heads(mt[:, d, :]), mask, ALU.mult).then_inc(dpool[d], 1)

        @block.scalar
        def _(act):
            step = Steps(act, act_step)

            def round_panel(n, sb, r, per):
                for part in range(2):
                    b = 2 * sb + part
                    if part == 0:
                        act.wait_ge(panel_in[n % RING], 16 * (n // RING + 1) + r * (16 * per // RING))
                    if b >= HALVES:
                        act.wait_ge(half_used, b - HALVES + 1 + r * (2 * per))
                    act.activation(w_hi[:, b % HALVES, :], half_source(n % RING, part), ACT.Copy).then_inc(weights_rounded, 1)

            splits = Splits(round_panel)

            def ada_copy(l, p, r=0, per=0):
                g = ADA_PANELS * l + p
                act.wait_ge(ada_product, g + 1 + r * per)
                if g:
                    act.wait_ge(ada_done, g + r * per)
                act.activation(ada_rows[:, :], bank[6][0:4, 0:UNIT], ACT.Copy).then_inc(ada_copied, 1)

            def square(key, k, src, rows=slice(0, P), w=T, buf=sq):
                n, m, _ = units[key]
                m += k
                if m >= 4:
                    act.wait_ge(summed, m - 3)
                act.activation(buf[rows, m % 4, 0:w], src, ACT.Square).then_inc(squares, 1)

            def root(key, size, w=T, rows=slice(0, P)):
                n, m, k = units[key]
                act.wait_ge(summed, m + k)
                if n >= 2:
                    act.wait_ge(root_used, n - 1)
                act.activation(rt[rows, n % 2, 0:w], bank[4 + n % 2][rows, 0:w], ACT.Sqrt, bias=eps[rows, :],
                               scale=1.0 / size).then_inc(roots, 1)

            def norm(l, i, w, h_key):
                n, m, _ = units[(l, "norm", i)]
                if h_key is not None:
                    wait_drained(act, h_key + (DC - 1,))
                act.wait_ge(squares, m + 1)
                square((l, "norm", i), 1, h[:, DC - 1, 0:w], w=w)
                root((l, "norm", i), D, w)
                act.wait_ge(mods_ready, 3 * l + (1 if i == 0 else 3))
                for k in range(DC):
                    if k < DC - 1:
                        act.wait_ge(chunk_scaled, (3 * l + i) * (DC - 1) + k + 1)
                    else:
                        act.wait_ge(root_used, n + 1)
                    for s, cols in halves(w):
                        last = act.activation(u_hi[:, k, cols], sq[:, k % 4, cols], ACT.Identity,
                                              bias=mods[:, l, 3 * i * DC + k, s:s + 1])
                    last.then_inc(u_rounded, 1)

            def ffn(l, f, w, carry):
                q0 = number[(l, "g", f, 0)]
                v0 = counts["v"][q0]
                h0 = FC * (2 * l + f)
                flat = h_hi[:, :, :].rearrange("p n w -> p (n w)")
                peel, body = 2, 3

                def pair(i, loop=None):
                    r = 0 if loop is None else loop
                    more = r * body

                    def rounded(c):
                        act.wait_ge(drained["v"], v0 + 2 * i + c + 1 + 2 * more)
                        at = (2 * i + c) * T
                        dst = flat[:, at:at + w] if loop is None else flat[:, bass.ds(more * (2 * T) + at, w)]
                        act.activation(dst, sg[:, c, 0:w], ACT.Copy).then_inc(hidden_rounded, 1)

                    def gate(c):
                        act.wait_ge(product_made, q0 + 1 + 4 * i + c + 4 * more)
                        if i:
                            act.wait_ge(hidden_ready, h0 + 2 * i + c - 1 + 2 * more)
                        act.activation(sg[:, c, 0:w], bank[(q0 + c) % 4][:, 0:w], ACT.Silu).then_inc(drained["a"], 1)

                    p = ADA_FIRST + ADA_PAIR * i
                    splits.next()
                    gate(0)
                    if carry is None:
                        gate(1)
                        splits.next()
                        rounded(0)
                    elif i == 0:
                        gate(1)
                        splits.next()
                        rounded(0)
                        ada_copy(carry, p)
                        splits.next(2)
                    else:
                        splits.next()
                        gate(1)
                        ada_copy(carry, p, r, ADA_PAIR * body)
                        splits.next()
                        rounded(0)
                        splits.next()
                    rounded(1)
                    if carry is not None:
                        ada_copy(carry, p + 1, r, ADA_PAIR * body)

                splits.upto(START[l, "gu", f] + 1)
                for i in range(peel):
                    pair(i)
                n0, rounds = splits.n, (FC // 2 - peel) // body
                splits.per = body * (2 + (ADA_PAIR if carry is not None else 0))
                with act.Fori(0, rounds) as r:
                    splits.r = r
                    for i in range(body):
                        pair(peel + i, r)
                splits.r, splits.n = 0, n0 + rounds * splits.per
                splits.per = 0
                if carry is None:
                    for s in range(12):
                        splits.upto(START[l, "down", f] + s + 2)
                else:
                    for s in range(6):
                        splits.past((l, "down", f), 6 * s + 4)
                        ada_copy(carry, ADA_PANELS - 6 + s)
                    splits.past((l, "down", f), 35)

            act.wait_ge(cond_in, 16)
            step(act.activation(cond[:, :, :], cond[:, :, :], ACT.Silu))
            step.wait()
            act.activation(c4[:, :, 0:2], cond[:, :, :], ACT.Copy).then_inc(cond_ready, 1)
            act.wait_ge(eps_ready, 1)
            for p in range(ADA_FIRST):
                splits.upto(p + 2)
                ada_copy(0, p)
            act.wait_ge(inputs_in, 16 * (DC + 2))
            act.dma_start(par[:, :], par_d[:, 0:NPAR]).then_inc(par_in, 16)
            for l in range(DEPTH):
                w = width(l)
                nt = w // P
                if l:
                    wait_drained(act, (l - 1, "out", DC - 1))
                    act.dma_start(par[:, :], par_d[:, l * NPAR:(l + 1) * NPAR]).then_inc(par_in, 16)
                norm(l, 0, T, (l - 1, "down", 1) if l else None)
                ffn(l, 0, T, 0 if l == 0 else None)
                norm(l, 1, T, (l, "down", 0))

                for c in range(GMC):
                    if c % 2 == 0:
                        splits.upto(START[l, "gmu"] + c // 2 + 2)
                    wait_product(act, (l, "gmu", c))
                    act.activation(ya[:, c, 0:w], bank_of((l, "gmu", c))[:, 0:w],
                                   ACT.Gelu_apprx_tanh).then_inc(drained["a"], 1)
                for p in range(2):
                    splits.upto(START[l, "gmv"] + p + 2)
                    for t in range(nt):
                        wait_product(act, (l, "gmv", p, t))
                        act.activation(gv[:, t, p * UNIT:(p + 1) * UNIT], bank_of((l, "gmv", p, t))[:, 0:UNIT],
                                       ACT.Gelu_apprx_tanh).then_inc(drained["a"], 1)
                act.wait_ge(gmv_stats_ready, l + 1)
                act.activation(lnr[:, 0:nt], mv[:, 0:nt, 1], ACT.Sqrt, bias=eps[:, :]).then_inc(gmv_root_ready, 1)

                for i in range(2):
                    key = (l, "ckv", i)
                    splits.past((l, "low"), i)
                    wait_product(act, key)
                    square((l, "ckv"), i, bank_of(key)[:, :])
                    act.activation(ckv[:, i, :], bank_of(key)[:, :], ACT.Copy).then_inc(drained["a"], 1)
                key = (l, "krope")
                splits.past((l, "low"), 2)
                wait_product(act, key)
                act.activation(kr[tail, 0, :], bank_of(key)[0:ROPE, :], ACT.Copy)
                act.activation(kr[ROPE:ROPE + 16, 0, :], bank_of(key)[ROPE:ROPE + 16, :],
                               ACT.Copy).then_inc(drained["a"], 1)
                root((l, "ckv"), LKV)
                for i in range(3):
                    key = (l, "cq", i)
                    splits.past((l, "low"), 3 + i)
                    wait_product(act, key)
                    square((l, "cq"), i, bank_of(key)[:, 0:w], w=w)
                    act.activation(cq[:, i, 0:w], bank_of(key)[:, 0:w], ACT.Copy).then_inc(drained["a"], 1)
                root((l, "cq"), LQ, w)
                act.wait_ge(drained["a"], count_after(number[l, "krope"], "a"))
                act.wait_ge(summed, units[(l, "cq")][1] + 3)
                for i in range(4):
                    act.activation(sq[tail, i, :], kr[tail, 0, :], ACT.Square)
                for hd in range(MH):
                    key = (l, "nope", hd // 2)
                    rows = slice(NOPE * (hd % 2), NOPE * (hd % 2) + NOPE)
                    if hd % 2 == 0:
                        wait_product(act, key)
                    square((l, "k"), hd, bank_of(key)[rows, :], slice(0, NOPE))
                    last = act.activation(kk[0:NOPE, hd, :], bank_of(key)[rows, :], ACT.Copy)
                    if hd % 2:
                        last.then_inc(drained["a"], 1)
                for t in range(4):
                    wait_product(act, (l, "mv", t))
                    act.activation(vm[:, t, :], bank_of((l, "mv", t))[:, :], ACT.Copy).then_inc(drained["a"], 1)
                root((l, "k"), QK, rows=slice(0, MH))
                for hd in range(MH):
                    key = (l, "uq", hd)
                    wait_product(act, key)
                    square((l, "q"), hd, bank_of(key)[0:QK, 0:w], slice(0, QK), w)
                    act.activation(qq[0:QK, hd, 0:w], bank_of(key)[0:QK, 0:w], ACT.Copy).then_inc(drained["a"], 1)
                root((l, "q"), QK, w, slice(0, MH))
                splits.upto(START[l, "qkv"] + 1)
                a0 = ATT[l]
                for i in range(nt * MH + 2):
                    if i < nt * MH:
                        a = a0 + i
                        s = a % 4
                        act.wait_ge(att_max, a + 1)
                        keys = slice(0, T) if i // MH < 2 else slice(0, CTX)
                        if a >= 4:
                            act.wait_ge(att_turned, a - 3)
                        act.activation(pr[:, s, keys], bank[S_BANKS[s]][:, keys], ACT.Exp,
                                       scale=QK ** -0.5, bias=nb[:, s:s + 1],
                                       accum_out=rs[:, s:s + 1]).then_inc(att_exp, 1)
                    if i > 1:
                        b = a0 + i - 2
                        nk = 4 if (i - 2) // MH < 2 else 2
                        act.wait_ge(att_turned, b + 1)
                        if b >= 2:
                            act.wait_ge(att_valued, b - 1)
                        act.activation(prT[:, b % 2, 0:nk * P], bank[2 + b % 2][:, 0:nk * P],
                                       ACT.Copy).then_inc(att_turned_kept, 1)

                act.wait_ge(softplus_ready, l + 1)
                act.wait_ge(par_in, 16 * (l + 1))
                act.activation(t1, t1, ACT.Exp, scale=-1.0)
                act.activation(beta, gab[:, :, 8:16], ACT.Exp, scale=-1.0)
                step(act.activation(expa, par_of("a_log"), ACT.Exp))
                step.wait()
                act.activation(t1, t1, ACT.Ln, bias=ones[:, 0:1]).then_inc(softplus_log, 1)

                def conv_in(c):
                    key = (l, "qkv", c)
                    if c % 2 == 0:
                        splits.upto(START[l, "qkv"] + c // 2 + 2)
                    wait_product(act, key)
                    if 12 * l + c >= 3:
                        act.wait_ge(conv_done, 12 * l + c - 2)
                    if c >= 4:
                        act.wait_ge(conv_silu, 12 * l + c - 3)
                    act.activation(acc[:, c % 4, :], bank_of(key)[:, :], ACT.Copy,
                                   scale=par_of("conv", 5 * c + 2, 5 * c + 3))
                    act.activation(convin[:, c % 3, :, 2:258],
                                   bank_of(key)[:, :].rearrange("p (s w) -> p s w", s=2),
                                   ACT.Copy).then_inc(drained["a"], 1)

                def conv_out(c):
                    act.wait_ge(conv_done, 12 * l + c + 1)
                    dst = qT[:, c, :] if c < 4 else kT[:, c - 4, :] if c < 8 else vT[:, c % 2, :]
                    if c >= 10:
                        act.wait_ge(tokens_turned, 8 * l + c - 9)
                    act.activation(dst, acc[:, c % 4, :], ACT.Silu).then_inc(conv_silu, 1)

                def tok_copy(i):
                    act.wait_ge(tokens_turned, 8 * l + i + 1)
                    dst = (vtok if i < 4 else ktok)[:, :, (i % 4) * P:(i % 4 + 1) * P]
                    act.activation(dst, bank[6][:, :].rearrange("p (t c) -> p t c", t=4),
                                   ACT.Copy).then_inc(tokens_kept, 1)

                def z_silu(c):
                    if c == 1:
                        splits.upto(START[l, "z"] + 2)
                    elif c == 3:
                        splits.upto(START[l, "z"] + 3)
                    wait_product(act, (l, "z", c))
                    act.activation(sq[:, c, 0:w], bank_of((l, "z", c))[:, 0:w], ACT.Silu).then_inc(drained["a"], 1)

                def qk_square(i):
                    act.wait_ge(conv_silu, 12 * l + i + 1)
                    square((l, "qk", i), 0, (qT if i < 4 else kT)[:, i % 4, :], buf=qk_sq)

                conv_in(0)
                conv_in(1)
                for c in range(12):
                    if c + 2 < 12:
                        conv_in(c + 2)
                    conv_out(c)
                    if c >= 4:
                        qk_square(c - 4)
                    if c >= 5:
                        root((l, "qk", c - 5), 1.0)
                    if c >= 9:
                        z_silu(c - 9)
                        tok_copy(c - 9)
                root((l, "qk", 7), 1.0)
                z_silu(3)
                for i in range(3, 8):
                    tok_copy(i)

                for j in range(4):
                    it = l * 4 + j
                    for d in range(2):
                        act.wait_ge(ddve[d], it * D_DVE + 2)
                        act.activation(E[:, d, :], E[:, d, :], ACT.Exp).then_inc(dact[d], 1)
                        act.activation(EG[:, d, :], bank[3 * d][:, :], ACT.Exp).then_inc(dact[d], 1)
                    for d in range(2):
                        act.activation(egam[:, d, :], gamc[:, d, :], ACT.Exp)
                        act.activation(kds[:, d, :], kds[:, d, :], ACT.Exp).then_inc(dact[d], 1)
                    for n in range(LEVELS):
                        for d in range(2):
                            act.wait_ge(dpe[d], it * D_PE + (3 if n == 0 else 2 + 2 * n))
                            act.activation((X if n == 0 else Y)[:, d, :], bank[3 * d][:, :],
                                           ACT.Copy).then_inc(dact[d], 1)
                    for d in range(2):
                        act.wait_ge(dpe[d], it * D_PE + 16)
                        act.activation(nwT[:, d, :], bank[3 * d][:, :], ACT.Copy, scale=-1.0).then_inc(dact[d], 1)

                for d in range(2):
                    act.wait_ge(ddve[d], (l * 4 + 4) * D_DVE)
                for i in range(4):
                    square((l, "o", i), 0, yb[:, i, 0:w], w=w, buf=o_sq)
                for i in range(4):
                    if i == 2:
                        splits.past((l, "merge"), 0)
                    root((l, "o", i), P, w)
                act.wait_ge(ya_ready, l + 1)
                for b, y in ((0, ya), (2, yc)):
                    act.activation(y_hi[b][:, :, 0:w], y[:, :, 0:w], ACT.Copy).then_inc(y_rounded, 1)

                for pair in range(DC // 2):
                    more = l + 1 < DEPTH
                    n_gates = 10 if more else 6
                    h0 = pair * (n_gates + 3)
                    for b in range(3):
                        for c in range(2):
                            key = (l, "gate", 2 * pair + c, b)
                            splits.past((l, "merge"), h0 + ((4 * b + 2 * c if b < 2 else 8 + c) if more else 2 * b + c))
                            wait_product(act, key)
                            if pair:
                                wait_drained(act, (l, "branch", 2 * pair + c - 2, b))
                            act.activation(sig[:, 2 * b + c, 0:w], bank_of(key)[:, 0:w],
                                           ACT.Sigmoid).then_inc(drained["a"], 1)
                        if more and b < 2:
                            splits.past((l, "merge"), h0 + 4 * b + 3)
                            ada_copy(l + 1, 2 * pair + b)
                        if pair == 0 and b == 1:
                            act.wait_ge(yb_ready, l + 1)
                            act.activation(y_hi[1][:, :, 0:w], yb[:, :, 0:w], ACT.Copy).then_inc(y_rounded, 1)
                    for b in range(3):
                        splits.past((l, "merge"), h0 + n_gates + b)
                    for c in range(2):
                        act.wait_ge(m_added, DC * l + 2 * pair + c + 1)
                        act.activation(m_hi[:, 2 * pair + c, 0:w], macc[:, c, 0:w], ACT.Copy).then_inc(m_rounded, 1)
                for p in range(4):
                    splits.upto(START[l, "out"] + p + 2)
                norm(l, 2, w, (l, "out"))
                ffn(l, 1, w, l + 1 if l + 1 < DEPTH else None)

        @block.tensor
        def _(pe):
            class Weights:

                def __init__(self):
                    self.n, self.part, self.r, self.per = 0, 0, 0, 0
                    self.release, self.left, self.following = None, None, None
                    self.unreported, self.owed, self.count = 0, 0, 0

                def raw(self):
                    n = self.n
                    assert KINDS[n] == "raw"
                    pe.wait_ge(panel_in[n % RING], 16 * (n // RING + 1))
                    self.n += 1
                    self.left, self.release = self.release, None
                    self.following = n % RING
                    self.owed = 0
                    return ring[:, n % RING * PANEL:(n % RING + 1) * PANEL]

                def half(self, width=P):
                    n, part = self.n, self.part
                    assert KINDS[n] == "split"
                    sb = split_before[n]
                    self.part = 1 - part
                    if part == 0:
                        pe.wait_ge(first_rest_ready, sb + 1 + self.r * self.per)
                        self.left = self.release
                        self.release = None
                    else:
                        pe.wait_ge(panel_left[n % RING], n // RING + 1 + self.r * (self.per // RING))
                        self.n += 1
                        self.left = None
                    self.following = None
                    b = 2 * sb + part
                    self.owed, self.unreported, self.count = self.unreported, 1, 0
                    return [x[:, b % HALVES, :].rearrange("p (k n) -> p k n", n=width) for x in (w_hi, w_lo)]

                def both(self):
                    assert self.part == 0
                    first = self.half()
                    left, owed = self.left, self.owed
                    second = self.half()
                    self.left, self.owed, self.unreported = left, owed, 2
                    return first, second

                def used(self, ins):
                    self.count += 1
                    if self.left is not None:
                        ins.then_inc(panel_left[self.left], 1)
                        self.left = None
                    elif self.owed and self.count > 1:
                        ins.then_inc(half_used, 1)
                        self.owed -= 1
                    if self.following is not None:
                        self.release, self.following = self.following, None
                    return ins

            weights = Weights()

            def free_bank(key):
                q = number[key]
                if q >= 4:
                    wait_drained(pe, q - 4)

            def product(out, parts, signal):
                for n, (lhsT, rhs) in enumerate(parts):
                    last = weights.used(pe.matmul(out, lhsT, rhs, start=n == 0, stop=n == len(parts) - 1))
                if signal is not None:
                    last.then_inc(signal, 1)

            def split_matmul(out, lhs, rhs, start, stop):
                for n, (a, b) in enumerate(((0, 0), (1, 0), (0, 1))):
                    last = weights.used(pe.matmul(out, lhs[a], rhs[b], start=start and n == 0, stop=stop and n == 2))
                return last

            def ada_turn(l, p, r=0, per=0):
                pe.wait_ge(ada_copied, ADA_PANELS * l + p + 1 + r * per)
                for c in range(2):
                    at = 2 * (2 * p + c)
                    out = bank[7][:, at:at + 2] if isinstance(r, int) else bank[7][:, bass.ds(r * (4 * per) + at, 2)]
                    last = pe.matmul(out, ada_rows[:, c * P:(c + 1) * P], C("fold", slice(0, 4)), start=True,
                                     stop=True)
                last.then_inc(ada_done, 1)

            def ada_half(l, n, r=0, per=0):
                p, part = divmod(n, 2)
                g = ADA_PANELS * l + p
                if part == 0 and g:
                    pe.wait_ge(ada_copied, g + r * per)
                w2 = weights.half(UNIT)
                for k in range(4):
                    for a in range(2):
                        last = weights.used(pe.matmul(bank[6][0:4, 0:UNIT], c4[:, 4 * part + k, :], w2[a][:, k, :],
                                                      start=part == k == a == 0, stop=part == a == 1 and k == 3))
                if part:
                    last.then_inc(ada_product, 1)
                elif p not in (0, ADA_FIRST):
                    ada_turn(l, p - 1, r, per)

            def sums(key, w=T, buf=sq):
                n, m, count = units[key]
                if n >= 2:
                    pe.wait_ge(roots, n - 1)
                for k in range(count):
                    pe.wait_ge(squares, m + k + 1)
                    pe.matmul(bank[4 + n % 2][:, 0:w], ones, buf[:, (m + k) % 4, 0:w],
                              start=k == 0, stop=k == count - 1).then_inc(summed, 1)

            def std(keys, w, src, ready, base):
                for c, key in enumerate(keys):
                    w2 = weights.half()
                    free_bank(key)
                    for k in range(DC):
                        if ready is not None:
                            pe.wait_ge(ready, base + k + 1)
                        last = split_matmul(bank_of(key)[:, 0:w], [x[:, k, :] for x in w2],
                                            [x[:, k, 0:w] for x in src], k == 0, k == DC - 1)
                    ready = None
                    last.then_inc(product_made, 1)

            def head_sum(key, hd, w=T):
                n, m, count = units[key]
                if hd == 0:
                    pe.wait_ge(roots, n - 1)
                pe.wait_ge(squares, m + hd + 1)
                pe.matmul(bank[4 + n % 2][0:32, 0:w], C("pick", slice(0, QK))[:, 31 - hd:63 - hd],
                          sq[0:QK, (m + hd) % 4, 0:w], start=hd == 0, stop=hd == count - 1).then_inc(summed, 1)

            def streamed(outs, w, src, ready, base):
                for c, w2 in enumerate(weights.both()):
                    outs[c] = (outs[c], w2)
                for k in range(DC):
                    pe.wait_ge(ready, base + k + 1)
                    for out, w2 in outs:
                        last = split_matmul(out, [x[:, k, :] for x in w2], [x[:, k, 0:w] for x in src], k == 0,
                                            k == DC - 1)
                        if k == DC - 1:
                            last.then_inc(product_made, 1)

            u = (u_hi, u_lo)

            def ffn(l, f, w, carry, ready_base):
                q0 = number[(l, "g", f, 0)]
                v0 = counts["v"][q0]
                a0 = counts["a"][q0]
                h0 = FC * (2 * l + f)
                d0 = number[(l, "down", f, 0)]
                peel, body = 2, 3

                def pair(i, loop=None):
                    r = 0 if loop is None else loop
                    more = r * body
                    n = 2 * (ADA_FIRST + ADA_PAIR * i)
                    for part in range(2):
                        if i == 0 and part == 0:
                            for c in range(2):
                                free_bank((l, "g", f, c))
                            streamed([bank[(q0 + c) % 4][:, 0:w] for c in range(2)], w, u, u_rest_ready, ready_base)
                            continue
                        for c in range(2):
                            if i == 0 and carry is not None:
                                ada_half(carry, n + c)
                            w2 = weights.half()
                            b = 2 * part + c
                            if i == 0:
                                free_bank((l, "gu"[part], f, c))
                            elif part == 0:
                                pe.wait_ge(drained["a"], a0 + 2 * (i - 1) + c + 1 + 2 * more)
                            else:
                                pe.wait_ge(drained["v"], v0 + 2 * (i - 1) + c + 1 + 2 * more)
                            for k in range(DC):
                                last = split_matmul(bank[(q0 + b) % 4][:, 0:w], [x[:, k, :] for x in w2],
                                                    [x[:, k, 0:w] for x in u], k == 0, k == DC - 1)
                            last.then_inc(product_made, 1)
                            if i and carry is not None:
                                ada_half(carry, n + b, r, ADA_PAIR * body)
                    if i == 0 and carry is not None:
                        ada_half(carry, n + 2)
                        ada_half(carry, n + 3)

                if carry is not None:
                    pe.wait_ge(mods_ready, 3 * carry + 1)
                for i in range(peel):
                    pair(i)
                rounds = (FC // 2 - peel) // body
                n0 = weights.n
                weights.per = body * (2 + (ADA_PAIR if carry is not None else 0))
                with pe.Fori(0, rounds) as r:
                    weights.r = r
                    for i in range(body):
                        pair(peel + i, r)
                weights.r, weights.n = 0, n0 + rounds * weights.per

                pe.wait_ge(drained["a"], a0 + FC)
                vd = counts["v"][d0]
                n0 = weights.n
                weights.per = 9 if carry is not None else 6
                hid = (h_hi, h_lo)
                with pe.Fori(0, 2) as r:
                    weights.r = r
                    for g in range(2):
                        for s in range(3):
                            for c in range(2):
                                w2 = weights.half()
                                if g == 0 and c == 0:
                                    pe.wait_ge(hidden_ready, h0 + min(8 * s + 8, FC))
                                m = 2 * g + c
                                if s == 0:
                                    pe.wait_ge(drained["v"], r * 4 + (vd + m - 3))
                                for k in range(8 * s, min(8 * s + 8, FC)):
                                    last = split_matmul(bank[(d0 + m) % 4][:, 0:w], [x[:, k - 8 * s, :] for x in w2],
                                                        [x[:, k, 0:w] for x in hid], k == 0, k == FC - 1)
                                if s == 2:
                                    last.then_inc(product_made, 1)
                                if c == 0 and carry is not None:
                                    pe.wait_ge(mods_ready, 3 * carry + 2)
                                    ada_half(carry, 2 * (ADA_PANELS - 6) + 3 * g + s, r, 3)
                weights.n, weights.r = n0 + 2 * weights.per, 0
                weights.per = 0
                if carry is not None:
                    ada_turn(carry, ADA_PANELS - 1)

            pe.wait_ge(c_split, 1)
            for n in range(2 * ADA_FIRST):
                if n == 2:
                    pe.wait_ge(inputs_in, 16 * (DC + 2))
                ada_half(0, n)
            ada_turn(0, ADA_FIRST - 1)
            for l in range(DEPTH):
                w = width(l)
                nt = w // P
                sums((l, "norm", 0))
                ffn(l, 0, T, 0 if l == 0 else None, (3 * l) * DC)
                sums((l, "norm", 1))

                for c in range(2):
                    free_bank((l, "gmu", c))
                streamed([bank_of((l, "gmu", c))[:, 0:w] for c in range(2)], w, u, u_rest_ready, (3 * l + 1) * DC)
                std([(l, "gmu", 2), (l, "gmu", 3)], w, u, None, 0)
                for p in range(2):
                    for part in range(2):
                        w2 = weights.half(UNIT)
                        for t in range(nt):
                            key = (l, "gmv", p, t)
                            if part == 0:
                                free_bank(key)
                            for k in range(4):
                                kc = 4 * part + k
                                last = split_matmul(bank_of(key)[:, 0:UNIT], [x[:, kc, t * P:(t + 1) * P] for x in u],
                                                    [x[:, k, :] for x in w2], kc == 0, kc == DC - 1)
                            if part == 1:
                                last.then_inc(product_made, 1)

                for key in ((l, "ckv", 0), (l, "ckv", 1), (l, "krope")):
                    std([key], T, u, None, 0)
                sums((l, "ckv"))
                std([(l, "cq", 0)], w, u, None, 0)
                wait_drained(pe, (l, "krope"))
                for t in range(4):
                    last = pe.transpose(bank[6][:, 16 * t:16 * t + 16], kr[ROPE:ROPE + 16, 0, t * P:(t + 1) * P],
                                        ident[ROPE:ROPE + 16, ROPE:ROPE + 16])
                last.then_inc(ab_turned, 1)
                std([(l, "cq", 1)], w, u, None, 0)
                pe.wait_ge(key_rope_weighted, l + 1)
                pe.wait_ge(ab_read, l + 1)
                pe.matmul(bank[6][tail, 0:SEQ], C("rot", tail), krw[tail, 0, 0:SEQ], start=True,
                          stop=True).then_inc(key_rope_rotated, 1)
                std([(l, "cq", 2)], w, u, None, 0)
                sums((l, "cq"), w)
                ukv = weights.raw().rearrange("p (k n) -> p k n", n=1024)
                pe.wait_ge(root_used, units[(l, "ckv")][0] + 1)
                for hp in range(4):
                    key = (l, "nope", hp)
                    free_bank(key)
                    product(bank_of(key)[:, :], [(ukv[:, k, hp * P:(hp + 1) * P], ckv[:, k, :]) for k in range(2)], product_made)
                    for hd in (2 * hp, 2 * hp + 1):
                        head_sum((l, "k"), hd)
                for t in range(4):
                    key = (l, "mv", t)
                    free_bank(key)
                    product(bank_of(key)[:, :], [(ckv[:, k, t * P:(t + 1) * P], ukv[:, k, 512:1024]) for k in range(2)],
                            product_made)
                pe.wait_ge(gmv_normed, l + 1)
                pe.wait_ge(par_in, 16 * (l + 1))
                for c in range(GMC):
                    key = (l, "spatial", c)
                    free_bank(key)
                    for t in range(nt):
                        last = pe.matmul(bank_of(key)[:, t * P:(t + 1) * P], gv[:, t, c * P:(c + 1) * P],
                                         par_of("gm_ws", c * P, (c + 1) * P), start=True, stop=True)
                    last.then_inc(product_made, 1)

                def rotate_q(hd):
                    wait_drained(pe, (l, "q_spread", hd))
                    if hd or l:
                        pe.wait_ge(query_ready, MH * l + hd)
                    pe.matmul(bank[6][tail, 0:SEQ], C("rot", tail), qq[tail, hd, 0:SEQ], start=True,
                              stop=True).then_inc(query_rotated, 1)

                pe.wait_ge(key_rope_ready, l + 1)
                pe.wait_ge(root_used, units[(l, "cq")][0] + 1)

                def spread(kind, w):
                    n = units[(l, kind)][0]
                    pe.wait_ge(head_roots_inverted, 2 * l + 1 + (kind == "q"))
                    for hd in range(MH):
                        key = (l, kind + "_spread", hd)
                        free_bank(key)
                        pe.matmul(bank_of(key)[:, 0:w], ident[0:MH, hd:hd + 1].to_broadcast([MH, P]),
                                  rt[0:MH, n % 2, 0:w], start=True, stop=True).then_inc(product_made, 1)
                        if kind == "q" and hd:
                            rotate_q(hd - 1)

                for hd in range(MH):
                    if hd % 4 == 0:
                        uq = weights.raw()[:, 0:3 * 4 * QK].rearrange("p (k n) -> p k n", n=4 * QK)
                    key = (l, "uq", hd)
                    free_bank(key)
                    at = (hd % 4) * QK
                    product(bank_of(key)[0:QK, 0:w], [(uq[:, k, at:at + QK], cq[:, k, 0:w]) for k in range(3)], product_made)
                    head_sum((l, "q"), hd, w)
                spread("k", T)
                spread("q", w)
                rotate_q(MH - 1)

                a0 = ATT[l]
                pe.wait_ge(query_ready, MH * (l + 1))
                na = nt * MH
                for i in range(na + 3):
                    if i < na:
                        a = a0 + i
                        t, hd = divmod(i, MH)
                        keys = slice(0, T) if t < 2 else slice(CTX, T)
                        if a >= 4:
                            pe.wait_ge(att_exp, a - 3)
                        pe.matmul(bank[S_BANKS[a % 4]][:, 0:keys.stop - keys.start], qq[0:QK, hd, t * P:(t + 1) * P],
                                  kk[0:QK, hd, keys], start=True, stop=True).then_inc(att_scored, 1)
                    if 1 < i <= na + 1:
                        a = a0 + i - 2
                        nk = 4 if (i - 2) // MH < 2 else 2
                        pe.wait_ge(att_normed, a + 1)
                        if a >= 2:
                            pe.wait_ge(att_turned_kept, a - 1)
                        for n in range(nk):
                            last = pe.transpose(bank[2 + a % 2][:, n * P:(n + 1) * P], pr[:, a % 4, n * P:(n + 1) * P],
                                                ident)
                        last.then_inc(att_turned, 1)
                    if i > 2:
                        a = a0 + i - 3
                        t, hd = divmod(i - 3, MH)
                        nk, k0 = (4, 0) if t < 2 else (2, 2)
                        pe.wait_ge(att_turned_kept, a + 1)
                        if a >= 2:
                            pe.wait_ge(att_kept, a - 1)
                        rows = slice(NOPE * (hd % 2), NOPE * (hd % 2) + NOPE)
                        for n in range(nk):
                            last = pe.matmul(bank[6][rows, 0:P], vm[:, k0 + n, hd * 64:hd * 64 + 64],
                                             prT[:, a % 2, n * P:(n + 1) * P], start=n == 0, stop=n == nk - 1)
                        last.then_inc(att_valued, 1)

                pe.wait_ge(att_turned_kept, a0 + na)
                pe.wait_ge(att_kept, a0 + na)

                def turn(i, src):
                    if 8 * l + i:
                        pe.wait_ge(tokens_kept, 8 * l + i)
                    for t in range(4):
                        last = pe.transpose(bank[6][:, t * P:(t + 1) * P], src[:, t * P:(t + 1) * P], ident)
                    last.then_inc(tokens_turned, 1)

                for c in range(12):
                    std([(l, "qkv", c)], T, u, None, 0)
                    if c >= 7:
                        sums((l, "qk", c - 7), buf=qk_sq)
                for i in range(4):
                    std([(l, "z", i)], w, u, None, 0)
                    pe.wait_ge(conv_silu, 12 * l + 9 + i)
                    turn(i, vT[:, i % 2, :])
                    if i < 3:
                        sums((l, "qk", 5 + i), buf=qk_sq)
                for i in range(4):
                    pe.wait_ge(root_used, units[(l, "qk", 4 + i)][0] + 1)
                    turn(4 + i, kT[:, i, :])

                wait_drained(pe, (l, "z", 3))
                pe.wait_ge(root_used, units[(l, "qk", 7)][0] + 1)
                pe.wait_ge(tokens_kept, 8 * (l + 1))
                pe.wait_ge(decays_ready, l + 1)
                for j in range(4):
                    it = l * 4 + j
                    tiles = [ORDER[d][j] for d in range(2)]

                    def each(what, d):
                        for hd in range(HEADS):
                            last = what(hd, slice(hd * P, (hd + 1) * P), slice(tiles[d] * P, (tiles[d] + 1) * P))
                        last.then_inc(dpe[d], 1)

                    def mm(out, lhsT, rhs, start=True, stop=True):
                        return pe.matmul(out, lhsT, rhs, start=start, stop=stop)

                    for d in range(2):
                        pe.wait_ge(decays_spread[d], it + 1)
                        if it:
                            pe.wait_ge(ddve[d], it * D_DVE - 1)
                        mm(bank[6][:, 4 * d:4 * d + 4], C("upto" if d == 0 else "from"),
                           g[:, tiles[d], 4 * d:4 * d + 4])
                    for d in range(2):
                        A, upto = bank[3 * d], C("upto" if d == 0 else "from")
                        each(lambda hd, c, t: mm(A[:, c], gB[:, d, c], upto), d)
                    for d in range(2):
                        B, K = bank[3 * d + 1], bank[3 * d + 2]

                        if it:
                            pe.wait_ge(ddve[d], it * D_DVE)

                        def pairs(hd, c, t):
                            mm(B[:, c], kT[:, hd, t], kT[:, hd, t])
                            return mm(K[:, c], kT[:, hd, t], qT[:, hd, t])
                        each(pairs, d)
                    for d in range(2):
                        pe.wait_ge(ddve[d], it * D_DVE + 4)
                        pe.wait_ge(dact[d], it * D_ACT + 2)
                        each(lambda hd, c, t: pe.transpose(bank[3 * d][:, c], XT[:, d, c], ident), d)
                    for n in range(1, LEVELS):
                        level = ml if n % 2 else E
                        for d in range(2):
                            pe.wait_ge(dpool[d], it * D_POOL + n)
                            if n == 1:
                                pe.wait_ge(dact[d], it * D_ACT + 4)
                            else:
                                pe.wait_ge(x_updated[d], it * (LEVELS - 2) + n - 1)
                            each(lambda hd, c, t: mm(bank[3 * d][:, c], level[:, d, c], X[:, d, c]), d)
                        for d in range(2):
                            pe.wait_ge(dact[d], it * D_ACT + 4 + n)
                            pe.wait_ge(ddve[d], it * D_DVE + (5 if n == 1 else 6 + n))

                            def step_z(hd, c, t):
                                if n < LEVELS - 1:
                                    mm(bank[3 * d + 1][:, c], XT[:, d, c], Y[:, d, c])
                                return mm(bank[3 * d + 2][:, c], Y[:, d, c], XT[:, d, c])
                            each(step_z, d)
                    for d in range(2):
                        pe.wait_ge(ddve[d], it * D_DVE + 13)
                        each(lambda hd, c, t: mm(bank[3 * d][:, c], kg[:, d, c], XT[:, d, c]), d)
                    for d in range(2):
                        pe.wait_ge(dact[d], it * D_ACT + 11)

                        def fresh(hd, c, t):
                            last = mm(bank[3 * d + 1][:, c], XT[:, d, c], vtok[:, tiles[d], c], stop=j == 0)
                            if j:
                                last = mm(bank[3 * d + 1][:, c], nwT[:, d, c], S[:, d, c], start=False)
                            return last
                        each(fresh, d)
                    for d in range(2):
                        pe.wait_ge(ddve[d], it * D_DVE + 14)

                        def outs(hd, c, t):
                            last = None
                            if tiles[d] < nt:
                                if j:
                                    mm(bank[3 * d][:, c], S[:, d, c], EG[:, d, c], stop=False)
                                last = mm(bank[3 * d][:, c], vnew[:, d, c], att[:, d, c], start=j == 0)
                            if j < 3:
                                last = mm(bank[3 * d + 2][:, c], kd[:, d, c], vnew[:, d, c])
                            return last
                        each(outs, d)

                for d in range(2):
                    pe.wait_ge(ddve[d], (l * 4 + 4) * D_DVE)
                for c in range(2):
                    sums((l, "o", c), w, o_sq)

                if l + 1 < DEPTH:
                    pe.wait_ge(mods_ready, 3 * l + 3)
                for gq in range(4):
                    for b in range(3):
                        for c in range(2):
                            std([(l, "gate", 2 * gq + c, b)], w, u, None, 0)
                            if gq == b == c == 0:
                                for i in (2, 3):
                                    sums((l, "o", i), w, o_sq)
                            if b < 2 and l + 1 < DEPTH:
                                ada_half(l + 1, 4 * gq + 2 * b + c)
                    for b in range(3):
                        w2 = weights.half(UNIT)
                        if gq == 0:
                            pe.wait_ge(y_rest_ready, 3 * (l + 1))
                        for c in range(2):
                            key = (l, "branch", 2 * gq + c, b)
                            free_bank(key)
                            for k in range(4):
                                last = split_matmul(bank_of(key)[:, 0:w], [x[:, k, c * P:(c + 1) * P] for x in w2],
                                                    [x[b][:, k, 0:w] for x in (y_hi, y_lo)], k == 0, k == 3)
                            last.then_inc(product_made, 1)
                if l + 1 < DEPTH:
                    ada_turn(l + 1, ADA_FIRST - 1)
                for c in range(2):
                    free_bank((l, "out", c))
                streamed([bank_of((l, "out", c))[:, 0:w] for c in range(2)], w, (m_hi, m_lo), m_rest_ready, DC * l)
                for p in range(1, 4):
                    std([(l, "out", 2 * p), (l, "out", 2 * p + 1)], w, (m_hi, m_lo), None, 0)
                sums((l, "norm", 2), w)
                ffn(l, 1, w, l + 1 if l + 1 < DEPTH else None, (3 * l + 2) * DC)

        @block.vector
        def _(dve):
            step = Steps(dve, dve_step)
            tt, ts, stt = dve.tensor_tensor, dve.tensor_scalar, dve.scalar_tensor_tensor

            def rest_of_panel(n, sb, r, per):
                for part in range(2):
                    b = 2 * sb + part
                    dve.wait_ge(weights_rounded, b + 1 + r * (2 * per))
                    tt(w_lo[:, b % HALVES, :], half_source(n % RING, part),
                       w_hi[:, b % HALVES, :].bitcast(F32), ALU.subtract).then_inc(
                           panel_left[n % RING] if part else first_rest_ready, 1)

            splits = Splits(rest_of_panel)

            def reciprocal_root(key, w=T, rows=slice(0, P)):
                n = units[key][0]
                r = rt[rows, n % 2, 0:w]
                dve.wait_ge(roots, n + 1)
                step(dve.reciprocal(r, r))
                step.wait()
                return r

            def square_sum(key, k, w):
                n, m, _ = units[key]
                total, fresh = sq[:, m % 4, 0:w], sq[:, (m + 2) % 4, 0:w]
                if k == 0 and m:
                    dve.wait_ge(summed, m)
                step(tt(total if k == 0 else fresh, h[:, k, 0:w], h[:, k, 0:w], ALU.mult))
                step.wait()
                if k:
                    last = tt(total, total, fresh, ALU.add)
                    if k < DC - 2:
                        step(last)
                        step.wait()
                    else:
                        last.then_inc(squares, 1)

            def norm(l, i, w):
                n = units[(l, "norm", i)][0]
                r = reciprocal_root((l, "norm", i), w)

                def rest(k):
                    dve.wait_ge(u_rounded, (3 * l + i) * DC + k + 1)
                    for s, cols in halves(w):
                        last = stt(u_lo[:, k, cols], sq[:, k % 4, cols], mods[:, l, 3 * i * DC + k, s:s + 1],
                                   u_hi[:, k, cols].bitcast(F32), ALU.add, ALU.subtract)
                    last.then_inc(u_rest_ready, 1)

                for k in range(DC + 1):
                    if 4 <= k < DC:
                        dve.wait_ge(u_rest_ready, (3 * l + i) * DC + k - 3)
                    if k < DC:
                        for s, cols in halves(w):
                            last = stt(sq[:, k % 4, cols], h[:, k, cols], scales[:, l, i, k, s:s + 1], r[:, cols],
                                       ALU.mult, ALU.mult)
                        last.then_inc(chunk_scaled if k < DC - 1 else root_used, 1)
                    if k >= 1:
                        if k < DC:
                            dve.wait_ge(chunk_scaled, (3 * l + i) * (DC - 1) + k)
                        else:
                            dve.wait_ge(root_used, n + 1)
                        rest(k - 1)

            def modulations(l, part):
                a, b = ((0, 2 * DC), (2 * DC, 3 * DC), (3 * DC, 9 * DC))[part]
                dve.wait_ge(ada_done, ADA_PANELS * l + (ADA_FIRST, ADA_PANELS - 7, ADA_PANELS)[part])
                step(tt(mods[:, l, a:b, :], bank[7][:, 2 * a:2 * b].rearrange("p (c s) -> p c s", s=2),
                        mod_par[:, l, a:b].unsqueeze(2).to_broadcast([P, b - a, 2]), ALU.add))
                step.wait()
                for i in ((0,), (), (1, 2))[part]:
                    c = (3 * i + 1) * DC
                    step(stt(scales[:, l, i, :, :], mods[:, l, c:c + DC, :], 1.0,
                             mod_par[:, l, 72 + i * DC:72 + (i + 1) * DC].unsqueeze(2).to_broadcast([P, DC, 2]),
                             ALU.add, ALU.mult))
                if part:
                    c = (2 if part == 1 else 8) * DC
                    step(ts(mods[:, l, c:c + DC, :], mods[:, l, c:c + DC, :], 0.5, None, ALU.mult))
                step.wait()
                dve.sem_inc(mods_ready, 1)

            def residual(key, l, i, j, w, norm_key):
                wait_product(dve, key)
                for s, cols in halves(w):
                    last = stt(h[:, j, cols], bank_of(key)[:, cols], mods[:, l, (3 * i + 2) * DC + j, s:s + 1],
                               h[:, j, cols], ALU.mult, ALU.add)
                last.then_inc(drained["v"], 1)
                if norm_key is not None and j < DC - 1:
                    wait_drained(dve, key)
                    square_sum(norm_key, j, units_width[norm_key])

            def ffn(l, f, w, carry):
                q0 = number[(l, "g", f, 0)]
                a0 = counts["a"][q0]
                h0 = FC * (2 * l + f)
                flat_hi = h_hi[:, :, :].rearrange("p n w -> p (n w)")
                flat_lo = h_lo[:, :, :].rearrange("p n w -> p (n w)")
                peel, body = 2, 3

                def pair(i, loop=None):
                    r = 0 if loop is None else loop
                    more = r * body

                    def up(c):
                        dve.wait_ge(product_made, q0 + 4 * i + 3 + c + 4 * more)
                        dve.wait_ge(drained["a"], a0 + 2 * i + c + 1 + 2 * more)
                        tt(sg[:, c, 0:w], sg[:, c, 0:w], bank[(q0 + 2 + c) % 4][:, 0:w],
                           ALU.mult).then_inc(drained["v"], 1)

                    def rest(c):
                        if loop is not None:
                            at = more * (2 * T) + (2 * i + c) * T
                            hi, lo = flat_hi[:, bass.ds(at, w)], flat_lo[:, bass.ds(at, w)]
                        else:
                            hi, lo = h_hi[:, 2 * i + c, 0:w], h_lo[:, 2 * i + c, 0:w]
                        dve.wait_ge(hidden_rounded, h0 + 2 * i + c + 1 + 2 * more)
                        tt(lo, sg[:, c, 0:w], hi.bitcast(F32), ALU.subtract).then_inc(hidden_ready, 1)

                    splits.next(2)
                    if carry is not None and i:
                        splits.next()
                    up(0)
                    if carry is not None:
                        if i == 0:
                            splits.next()
                        rest(0)
                        if i:
                            splits.next()
                        up(1)
                        if i == 0:
                            splits.next()
                    else:
                        up(1)
                        rest(0)
                    rest(1)

                splits.upto(START[l, "gu", f] + 1)
                for i in range(peel):
                    pair(i)
                n0, rounds = splits.n, (FC // 2 - peel) // body
                splits.per = body * (2 + (ADA_PAIR if carry is not None else 0))
                with dve.Fori(0, rounds) as r:
                    splits.r = r
                    for i in range(body):
                        pair(peel + i, r)
                splits.r, splits.n = 0, n0 + rounds * splits.per
                splits.per = 0
                if carry is not None:
                    modulations(carry, 1)
                following = (l, "norm", 1) if f == 0 else (l + 1, "norm", 0) if l + 1 < DEPTH else None
                for j in range(DC):
                    g, c = divmod(j, 2)
                    last = 6 * g + 4 + c if carry is None else 9 * g + 6 + 2 * c
                    splits.past((l, "down", f), last)
                    residual((l, "down", f, j), l, 0 if f == 0 else 2, j, w, following)

            def rope(dst, source, at, out_sem):
                tmp = rsin[tail, at, 0:SEQ]
                step(tt(tmp, source, C("sin", tail), ALU.mult))
                step(tt(dst, dst, C("cos", tail), ALU.mult))
                step.wait()
                return tt(dst, dst, tmp, ALU.add).then_inc(out_sem, 1)

            dve.wait_ge(cond_ready, 1)
            tt(c4[:, :, 2:4], cond[:, :, :], c4[:, :, 0:2].bitcast(F32), ALU.subtract).then_inc(c_split, 1)
            for p in range(ADA_FIRST):
                splits.upto(p + 2)
                if p == 0:
                    dve.wait_ge(inputs_in, 16 * (DC + 2))
                if p < DC - 1:
                    square_sum((0, "norm", 0), p, T)
            modulations(0, 0)
            for l in range(DEPTH):
                w = width(l)
                nt = w // P
                norm(l, 0, T)
                ffn(l, 0, T, 0 if l == 0 else None)
                if l == 0:
                    modulations(0, 2)
                norm(l, 1, T)

                for n in range(START[l, "gmu"], START[l, "low"]):
                    splits.upto(n + 2)
                dve.wait_ge(par_in, 16 * (l + 1))
                for t in range(nt):
                    wait_drained(dve, (l, "gmv", 1, t))
                    step(dve.bn_stats(stats, gv[:, t, :]))
                    step.wait()
                    step(dve.bn_aggr(mv[:, t, :], stats))
                    step.wait()
                dve.sem_inc(gmv_stats_ready, 1)
                dve.wait_ge(gmv_root_ready, l + 1)
                step(dve.reciprocal(lnr[:, 0:nt], lnr[:, 0:nt]))
                step.wait()
                for t in range(nt):
                    last = ts(gv[:, t, :], gv[:, t, :], mv[:, t, 0:1], lnr[:, t:t + 1], ALU.subtract, ALU.mult)
                last.then_inc(gmv_normed, 1)

                splits.past((l, "low"), 2)
                wait_drained(dve, (l, "krope"))
                ts(krw[tail, 0, :], kr[tail, 0, :], par_of("qk_k", rows=tail), None, ALU.mult).then_inc(key_rope_weighted, 1)
                r = reciprocal_root((l, "ckv"))
                for i in range(2):
                    last = stt(ckv[:, i, :], ckv[:, i, :], par_of("kv_norm", i, i + 1), r, ALU.mult, ALU.mult)
                last.then_inc(root_used, 1)
                splits.past((l, "low"), 3)
                dve.wait_ge(ab_turned, l + 1)
                dve.tensor_copy(gab, bank[6][:, 0:64].rearrange("p (t c) -> p t c", c=16)).then_inc(ab_read, 1)
                dve.wait_ge(ab_read, l + 1)
                step(tt(gab[:, :, 0:8], gab[:, :, 0:8], par_of("dt_bias").unsqueeze(1).to_broadcast([P, 4, 8]), ALU.add))
                step.wait()
                step(ts(t1, gab[:, :, 0:8], -1.0, None, ALU.mult))
                step.wait()
                tt(t1, t1, gab[:, :, 0:8], ALU.max).then_inc(softplus_ready, 1)
                splits.past((l, "low"), 5)
                dve.wait_ge(key_rope_rotated, l + 1)
                dve.wait_ge(key_rope_weighted, l + 1)
                rope(krw[tail, 0, 0:SEQ], bank[6][tail, 0:SEQ], 0, key_rope_ready)
                dve.wait_ge(key_rope_ready, l + 1)
                r = reciprocal_root((l, "cq"), w)
                for i in range(3):
                    last = stt(cq[:, i, 0:w], cq[:, i, 0:w], par_of("q_norm", i, i + 1), r, ALU.mult, ALU.mult)
                last.then_inc(root_used, 1)
                for c in range(GMC):
                    key = (l, "spatial", c)
                    wait_product(dve, key)
                    bias = par_of("gm_bs", c * P, (c + 1) * P).unsqueeze(1).to_broadcast([P, nt, P])
                    stt(gtmp[:, c % 2, 0:w].rearrange("p (t c) -> p t c", c=P),
                        bank_of(key)[:, 0:w].rearrange("p (t c) -> p t c", c=P),
                        par_of("gm_ln", c, c + 1), bias, ALU.mult, ALU.add).then_inc(drained["v"], 1)
                    wait_drained(dve, key)
                    step(tt(ya[:, c, 0:w], gtmp[:, c % 2, 0:w], ya[:, c, 0:w], ALU.mult))
                    step.wait()
                dve.sem_inc(ya_ready, 1)
                for kind, ww in (("k", T), ("q", w)):
                    n = units[(l, kind)][0]
                    dve.wait_ge(roots, n + 1)
                    r = rt[0:MH, n % 2, 0:ww]
                    dve.reciprocal(r, r).then_inc(head_roots_inverted, 1)
                for hd in range(MH):
                    key = (l, "k_spread", hd)
                    wait_product(dve, key)
                    r = bank_of(key)
                    stt(kk[0:NOPE, hd, :], kk[0:NOPE, hd, :], par_of("qk_k", rows=slice(0, NOPE)), r[0:NOPE, :],
                        ALU.mult, ALU.mult)
                    tt(kk[tail, hd, :], krw[tail, 0, :], r[tail, :], ALU.mult).then_inc(drained["v"], 1)
                wait_drained(dve, (l, "k_spread", MH - 1))
                dve.sem_inc(root_used, 1)
                for hd in range(MH):
                    key = (l, "q_spread", hd)
                    wait_product(dve, key)
                    stt(qq[0:QK, hd, 0:w], qq[0:QK, hd, 0:w], par_of("qk_q", rows=slice(0, QK)),
                        bank_of(key)[0:QK, 0:w], ALU.mult, ALU.mult).then_inc(drained["v"], 1)
                    wait_drained(dve, key)
                    dve.wait_ge(query_rotated, MH * l + hd + 1)
                    rope(qq[tail, hd, 0:SEQ], bank[6][tail, 0:SEQ], hd % 2, query_ready)
                dve.sem_inc(root_used, 1)

                splits.upto(START[l, "qkv"] + 1)
                a0 = ATT[l]
                for i in range(nt * MH + 3):
                    if i < nt * MH:
                        a = a0 + i
                        s = a % 4
                        keys = slice(0, T) if i // MH < 2 else slice(0, CTX)
                        dve.wait_ge(att_scored, a + 1)
                        if a >= 4:
                            dve.wait_ge(att_exp, a - 3)
                        step(dve.reduce_max(mx[:, s:s + 1], bank[S_BANKS[s]][:, keys], AX.X))
                        step.wait()
                        ts(nb[:, s:s + 1], mx[:, s:s + 1], -QK ** -0.5, None, ALU.mult).then_inc(att_max, 1)
                    if 0 < i <= nt * MH:
                        a = a0 + i - 1
                        s = a % 4
                        keys = slice(0, T) if (i - 1) // MH < 2 else slice(0, CTX)
                        dve.wait_ge(att_exp, a + 1)
                        step(dve.reciprocal(ri[:, s:s + 1], rs[:, s:s + 1]))
                        step.wait()
                        ts(pr[:, s, keys], pr[:, s, keys], ri[:, s:s + 1], None, ALU.mult).then_inc(att_normed, 1)
                    if i > 2:
                        a = a0 + i - 3
                        t, hd = divmod(i - 3, MH)
                        rows = slice(NOPE * (hd % 2), NOPE * (hd % 2) + NOPE)
                        dve.wait_ge(att_valued, a + 1)
                        dve.tensor_copy(yc[rows, hd // 2, t * P:(t + 1) * P], bank[6][rows, 0:P]).then_inc(att_kept, 1)

                dve.wait_ge(softplus_log, l + 1)
                step(stt(g, gab[:, :, 0:8], 0.0, t1, ALU.max, ALU.add))
                step(ts(beta, beta, 1.0, None, ALU.add))
                step.wait()
                step(stt(g, g, -1.0, expa.unsqueeze(1).to_broadcast([P, 4, 8]), ALU.mult, ALU.mult))
                step(dve.reciprocal(beta, beta))
                step.wait()
                dve.sem_inc(decays_ready, 1)

                def qk_norm(i):
                    r = reciprocal_root((l, "qk", i))
                    if i < 4:
                        stt(qT[:, i, :], qT[:, i, :], float(P) ** -0.5, r, ALU.mult, ALU.mult).then_inc(root_used, 1)
                    else:
                        tt(kT[:, i - 4, :], kT[:, i - 4, :], r, ALU.mult).then_inc(root_used, 1)

                dve.wait_ge(borders_zeroed, l + 1)
                for c in range(12):
                    if c % 2 == 0:
                        splits.upto(START[l, "qkv"] + c // 2 + 2)
                    wait_drained(dve, (l, "qkv", c))
                    a = acc[:, c % 4, :].rearrange("p (s w) -> p s w", s=2)
                    for tap in (0, 1, 3, 4):
                        src = convin[:, c % 3, :, tap:tap + SEQ]
                        wt = par_of("conv", 5 * c + tap, 5 * c + tap + 1)
                        last = stt(a, src, wt, a, ALU.mult, ALU.add)
                        if tap < 4:
                            step(last)
                            step.wait()
                        else:
                            last.then_inc(conv_done, 1)
                    if c >= 6:
                        qk_norm(c - 6)
                    if c == 10:
                        splits.upto(START[l, "z"] + 2)
                qk_norm(6)
                qk_norm(7)
                splits.upto(START[l, "z"] + 3)
                dve.wait_ge(root_used, units[(l, "qk", 7)][0] + 1)
                dve.wait_ge(tokens_kept, 8 * (l + 1))

                def per_head(x):
                    return x.unsqueeze(2).to_broadcast([P, HEADS, P])

                for j in range(4):
                    it = l * 4 + j
                    tiles = [ORDER[d][j] for d in range(2)]

                    def spread_decays(j):
                        for d in range(2):
                            dve.tensor_copy(heads(gB[:, d, :]),
                                            per_head(g[:, ORDER[d][j], 4 * d:4 * d + 4])).then_inc(decays_spread[d], 1)

                    if j == 0:
                        spread_decays(0)
                    for d in range(2):
                        A = heads(bank[3 * d][:, :])
                        end = P - 1 if d == 0 else 0
                        dve.wait_ge(dpe[d], it * D_PE + 1)
                        step(dve.tensor_copy(gamc[:, d, :], bank[6][:, 4 * d:4 * d + 4]))
                        step.wait()
                        step(tt(heads(E[:, d, :]), A, per_head(gamc[:, d, :]), ALU.subtract))
                        step(tt(kds[:, d, :], A[:, :, end], gamc[:, d, :], ALU.subtract))
                        step.wait()
                        stt(heads(E[:, d, :]), heads(E[:, d, :]), 0.0,
                            C("not_upto" if d == 0 else "not_from").unsqueeze(1).to_broadcast([P, HEADS, P]),
                            ALU.min, ALU.add).then_inc(ddve[d], 1)
                        dve.wait_ge(ddve[d], it * D_DVE + 1)
                        dve.sem_inc(ddve[d], 1)
                    for d in range(2):
                        dve.wait_ge(dpe[d], it * D_PE + 2)
                        dve.wait_ge(dact[d], it * D_ACT + 1)
                        step(tt(mt[:, d, :], bank[3 * d + 1][:, :], E[:, d, :], ALU.mult))
                        step.wait()
                        tt(heads(mt[:, d, :]), heads(mt[:, d, :]), per_head(beta[:, tiles[d], 4 * d:4 * d + 4]),
                           ALU.mult).then_inc(ddve[d], 1)
                        dve.wait_ge(ddve[d], it * D_DVE + 3)
                        step(tt(heads(XT[:, d, :]), heads(mt[:, d, :]),
                                C("level")[:, 0:P].unsqueeze(1).to_broadcast([P, HEADS, P]), ALU.mult))
                        step.wait()
                        tt(heads(XT[:, d, :]), ident.unsqueeze(1).to_broadcast([P, HEADS, P]), heads(XT[:, d, :]),
                           ALU.subtract).then_inc(ddve[d], 1)
                    for d in range(2):
                        tt(att[:, d, :], bank[3 * d + 2][:, :], E[:, d, :], ALU.mult).then_inc(ddve[d], 1)
                    for d in range(2):
                        end = P - 1 if d == 0 else 0
                        qs = qT[:, :, tiles[d] * P:(tiles[d] + 1) * P]
                        dve.wait_ge(dact[d], it * D_ACT + 3)
                        step(dve.tensor_copy(eL[:, d, :], heads(EG[:, d, :])[:, :, end]))
                        step.wait()
                        tt(heads(EG[:, d, :]), heads(EG[:, d, :]), qs, ALU.mult).then_inc(ddve[d], 1)
                        tt(heads(kg[:, d, :]), heads(ktok[:, tiles[d], :]), per_head(egam[:, d, :]),
                           ALU.mult).then_inc(ddve[d], 1)
                    for n in range(1, LEVELS):
                        for d in range(2):
                            dve.wait_ge(dpe[d], it * D_PE + 3 + 2 * n)
                            if n < LEVELS - 1:
                                tt(X[:, d, :], X[:, d, :], bank[3 * d + 1][:, :], ALU.subtract).then_inc(x_updated[d], 1)
                            tt(XT[:, d, :], XT[:, d, :], bank[3 * d + 2][:, :], ALU.subtract).then_inc(ddve[d], 1)
                    for d in range(2):
                        step(tt(heads(kd[:, d, :]), heads(ktok[:, tiles[d], :]), per_head(kds[:, d, :]), ALU.mult))
                        dve.wait_ge(dpe[d], it * D_PE + 17)
                        tt(heads(vnew[:, d, :]), heads(bank[3 * d + 1][:, :]),
                           per_head(beta[:, tiles[d], 4 * d:4 * d + 4]), ALU.mult).then_inc(ddve[d], 1)
                    if j < 3:
                        spread_decays(j + 1)
                    for d in range(2):
                        dve.wait_ge(dpe[d], it * D_PE + 18)
                        t = tiles[d]
                        if t < nt:
                            out = yb[:, :, t * P:(t + 1) * P]
                            o = heads(bank[3 * d][:, :])
                            if j % 2 == 0:
                                dve.tensor_copy(out, o).then_inc(ddve[d], 1)
                            else:
                                tt(out, out, o, ALU.add).then_inc(ddve[d], 1)
                        else:
                            dve.sem_inc(ddve[d], 1)
                    for d in range(2):
                        if j == 3:
                            dve.wait_ge(ddve[d], (it + 1) * D_DVE - 1)
                            dve.sem_inc(ddve[d], 1)
                        elif j:
                            step(tt(heads(S[:, d, :]), heads(S[:, d, :]), per_head(eL[:, d, :]), ALU.mult))
                            step.wait()
                            tt(S[:, d, :], S[:, d, :], bank[3 * d + 2][:, :], ALU.add).then_inc(ddve[d], 1)
                        else:
                            dve.tensor_copy(S[:, d, :], bank[3 * d + 2][:, :]).then_inc(ddve[d], 1)
                    for d in range(2):
                        dve.wait_ge(ddve[d], (it + 1) * D_DVE)

                for i in range(4):
                    if i == 2:
                        splits.past((l, "merge"), 0)
                    r = reciprocal_root((l, "o", i), w)
                    stt(yb[:, i, 0:w], yb[:, i, 0:w], par_of("dn_out"), r, ALU.mult, ALU.mult).then_inc(root_used, 1)
                splits.past((l, "merge"), 2)
                dve.wait_ge(root_used, units[(l, "o", 3)][0] + 1)
                wait_drained(dve, (l, "z", 3))
                tt(yb[:, :, 0:w], yb[:, :, 0:w], sq[:, :, 0:w], ALU.mult).then_inc(yb_ready, 1)

                def y_rest(b, y, n):
                    dve.wait_ge(y_rounded, 3 * l + n)
                    tt(y_lo[b][:, :, 0:w], y[:, :, 0:w], y_hi[b][:, :, 0:w].bitcast(F32),
                       ALU.subtract).then_inc(y_rest_ready, 1)

                splits.past((l, "merge"), 4)
                y_rest(0, ya, 1)
                splits.past((l, "merge"), 5 if l + 1 == DEPTH else 6)
                y_rest(2, yc, 2)
                y_rest(1, yb, 3)
                dve.wait_ge(yb_ready, l + 1)

                for pair in range(DC // 2):
                    more = l + 1 < DEPTH
                    n_gates = 10 if more else 6
                    h0 = pair * (n_gates + 3)
                    splits.past((l, "merge"), h0 + n_gates - 1)
                    for b in range(3):
                        splits.past((l, "merge"), h0 + n_gates + b)
                        for c in range(2):
                            key = (l, "branch", 2 * pair + c, b)
                            wait_product(dve, key)
                            wait_drained(dve, (l, "gate", 2 * pair + c, b))
                            m = macc[:, c, 0:w]
                            dst = m if b == 0 else mtmp[:, c, 0:w]
                            tt(dst, sig[:, 2 * b + c, 0:w], bank_of(key)[:, 0:w], ALU.mult).then_inc(drained["v"], 1)
                            if b:
                                wait_drained(dve, key)
                                last = tt(m, m, mtmp[:, c, 0:w], ALU.add)
                                if b == 1:
                                    step(last)
                                    step.wait()
                                else:
                                    last.then_inc(m_added, 1)
                    for c in range(2):
                        j = 2 * pair + c
                        dve.wait_ge(m_rounded, DC * l + j + 1)
                        tt(m_lo[:, j, 0:w], macc[:, c, 0:w], m_hi[:, j, 0:w].bitcast(F32),
                           ALU.subtract).then_inc(m_rest_ready, 1)
                if l + 1 < DEPTH:
                    modulations(l + 1, 0)
                for j in range(DC):
                    if j % 2 == 0:
                        splits.upto(START[l, "out"] + j // 2 + 2)
                    residual((l, "out", j), l, 1, j, w, (l, "norm", 2))
                norm(l, 2, w)
                ffn(l, 1, w, l + 1 if l + 1 < DEPTH else None)
                if l + 1 < DEPTH:
                    modulations(l + 1, 2)


_NAMES = ("wts", "par", "cst", "mod", "x", "c")


def kernel(**inputs):
    import concourse.bacc as bacc
    from concourse.bass_utils import run_bass_kernel_spmd

    inp = {k: np.asarray(v) for k, v in inputs.items()}
    arrays = {
        "wts": stream(inp),
        "par": params(inp),
        "cst": constants(),
        "mod": np.ascontiguousarray(modulation_params(inp)),
        "x": np.ascontiguousarray(np.concatenate([inp["x"][0].T, inp["ctx"][0].T], axis=1)),
        "c": np.ascontiguousarray(np.stack([inp["c"][0], inp["c_ctx"]], axis=-1).reshape(DC, P, 2).transpose(1, 0, 2)),
    }
    nc = bacc.Bacc("TRN2", target_bir_lowering=False, num_devices=1, dynamic_dma_scratch_size=1024)
    args = [nc.dram_tensor("in_" + n, arrays[n].shape, F32, kind="ExternalInput").ap() for n in _NAMES]
    args.append(nc.dram_tensor("out", (D, SEQ), F32, kind="ExternalOutput").ap())
    backbone(nc, *args)
    r = run_bass_kernel_spmd(nc, [{"in_" + n: arrays[n] for n in _NAMES}], core_ids=[0])
    return np.asarray(r.results[0]["out"]).T.reshape(1, SEQ, D)
```
